# Optimizing a Trainium2 kernel written in Bass

```python
import jax, jax.numpy as jnp
from jax import lax
import numpy as np

D_MODEL = 1024
BATCH = 1
SEQ = 512
DEPTH = 2

N_MEM = 256
N_MIXERS = 2
N_GLA = (DEPTH + 1) // 2
N_CONV = DEPTH // 2
GLA_HEADS = 4
GLA_DK = 128
GLA_DV = 256
GLA_QK = GLA_HEADS * GLA_DK
GLA_V = GLA_HEADS * GLA_DV
GLA_GATE_RANK = 16
GLA_GATE_NORM = 16.0
GLA_CHUNK = 64
CONV_CH = D_MODEL
CONV_WIDTH = 31
MEM_HEADS = 4
MEM_DH = 128
MEM_W = MEM_HEADS * MEM_DH
D_FF = 2816
ALPHA = (2 * DEPTH) ** 0.25
BETA = (8 * DEPTH) ** -0.25
LN_EPS = 1e-5
RMS_EPS = 1e-6

GLA_IN = 2 * GLA_QK + 2 * GLA_V + GLA_GATE_RANK + MEM_W
GLA_OUT_IN = GLA_V + MEM_W
CONV_IN = 2 * CONV_CH + MEM_W
CONV_OUT_IN = CONV_CH + MEM_W

kernel_name = "hybrid_gla_conformer_deepnorm_memory"

def layer_norm(x, g, b):
    xf = x.astype(jnp.float32)
    mu = jnp.mean(xf, -1, keepdims=True)
    var = jnp.mean(jnp.square(xf - mu), -1, keepdims=True)
    return ((xf - mu) * lax.rsqrt(var + LN_EPS) * g + b).astype(x.dtype)

def swiglu(x, w_gu, w_down):
    a, b = jnp.split(x @ w_gu, 2, axis=-1)
    return (jax.nn.silu(a) * b) @ w_down

def mem_attention(qm, mem, w_kv):
    B, S, _ = qm.shape
    k, v = jnp.split(mem @ w_kv, 2, axis=-1)
    q = qm.reshape(B, S, MEM_HEADS, MEM_DH)
    k = k.reshape(B, -1, MEM_HEADS, MEM_DH)
    v = v.reshape(B, -1, MEM_HEADS, MEM_DH)
    s = jnp.einsum('bshd,bmhd->bhsm', q, k).astype(jnp.float32) * (MEM_DH ** -0.5)
    p = jax.nn.softmax(s, axis=-1).astype(v.dtype)
    o = jnp.einsum('bhsm,bmhd->bshd', p, v)
    return o.reshape(B, S, MEM_W)

def gla_mix(h, w_gate2, b_gate, g_onorm):
    B, S, _ = h.shape
    N, C = S // GLA_CHUNK, GLA_CHUNK
    splits = [GLA_QK, 2 * GLA_QK, 2 * GLA_QK + GLA_V, 2 * GLA_QK + 2 * GLA_V,
              2 * GLA_QK + 2 * GLA_V + GLA_GATE_RANK]
    q, k, v, r, a, qm = jnp.split(h, splits, axis=-1)
    f32 = jnp.float32
    lg = jax.nn.log_sigmoid((a @ w_gate2 + b_gate).astype(f32)) / GLA_GATE_NORM

    def chunks(t, d):
        return t.astype(f32).reshape(B, N, C, GLA_HEADS, d).transpose(1, 0, 3, 2, 4)

    qc = chunks(q, GLA_DK) * (GLA_DK ** -0.5)
    kc = chunks(k, GLA_DK)
    vc = chunks(v, GLA_DV)
    bcum = jnp.cumsum(chunks(lg, GLA_DK), axis=3)
    b_last = bcum[:, :, :, -1, :]
    qe = qc * jnp.exp(bcum)
    ke = kc * jnp.exp(-bcum)
    kd = kc * jnp.exp(b_last[:, :, :, None, :] - bcum)

    causal = jnp.tril(jnp.ones((C, C), dtype=bool))
    att = jnp.where(causal, jnp.einsum('nbhid,nbhjd->nbhij', qe, ke), 0.0)
    o_intra = jnp.einsum('nbhij,nbhje->nbhie', att, vc)

    def step(state, inp):
        qe_n, kd_n, v_n, bl_n = inp
        o = jnp.einsum('bhcd,bhde->bhce', qe_n, state)
        state = state * jnp.exp(bl_n)[..., None] + jnp.einsum('bhcd,bhce->bhde', kd_n, v_n)
        return state, o

    s0 = jnp.zeros((B, GLA_HEADS, GLA_DK, GLA_DV), f32)
    _, o_inter = lax.scan(step, s0, (qe, kd, vc, b_last))
    o = (o_intra + o_inter).transpose(1, 0, 3, 2, 4).reshape(B, S, GLA_HEADS, GLA_DV)
    o = o * lax.rsqrt(jnp.mean(jnp.square(o), -1, keepdims=True) + RMS_EPS) * g_onorm
    o = o.reshape(B, S, GLA_V) * jax.nn.silu(r.astype(f32))
    return o.astype(h.dtype), qm

def conv_mix(h, w_dw, b_dw, ln_g, ln_b):
    a, gt, qm = jnp.split(h, [CONV_CH, 2 * CONV_CH], axis=-1)
    u = a * jax.nn.sigmoid(gt)
    u = lax.conv_general_dilated(
        u, w_dw[:, None, :], window_strides=(1,), padding=[(CONV_WIDTH - 1, 0)],
        dimension_numbers=('NWC', 'WIO', 'NWC'), feature_group_count=CONV_CH) + b_dw
    u = jax.nn.silu(layer_norm(u, ln_g, ln_b))
    return u, qm

def setup_inputs(seed: int = 0) -> dict:
    key = jax.random.key(seed)
    ks = jax.random.split(key, 20)
    nrm = lambda k, shape, s: jax.random.normal(k, shape, jnp.float32) * s
    return {
        "x": nrm(ks[0], (BATCH, SEQ, D_MODEL), 1.0),
        "mem": nrm(ks[1], (BATCH, N_MEM, D_MODEL), 1.0),
        "ln_g": 1.0 + nrm(ks[2], (DEPTH, 3, D_MODEL), 0.01),
        "ln_b": nrm(ks[3], (DEPTH, 3, D_MODEL), 0.01),
        "ffn1_w_gu": nrm(ks[4], (DEPTH, D_MODEL, 2 * D_FF), D_MODEL ** -0.5),
        "ffn1_w_down": nrm(ks[5], (DEPTH, D_FF, D_MODEL), BETA * D_FF ** -0.5),
        "ffn2_w_gu": nrm(ks[6], (DEPTH, D_MODEL, 2 * D_FF), D_MODEL ** -0.5),
        "ffn2_w_down": nrm(ks[7], (DEPTH, D_FF, D_MODEL), BETA * D_FF ** -0.5),
        "mem_w_kv": nrm(ks[8], (DEPTH, D_MODEL, 2 * MEM_W), D_MODEL ** -0.5),
        "gla_w_in": nrm(ks[9], (N_GLA, D_MODEL, GLA_IN), D_MODEL ** -0.5),
        "gla_w_gate2": nrm(ks[10], (N_GLA, GLA_GATE_RANK, GLA_QK), GLA_GATE_RANK ** -0.5),
        "gla_b_gate": nrm(ks[11], (N_GLA, GLA_QK), 0.01),
        "gla_g_onorm": 1.0 + nrm(ks[12], (N_GLA, GLA_DV), 0.01),
        "gla_w_out": nrm(ks[13], (N_GLA, GLA_OUT_IN, D_MODEL), BETA * GLA_OUT_IN ** -0.5),
        "conv_w_in": nrm(ks[14], (N_CONV, D_MODEL, CONV_IN), D_MODEL ** -0.5),
        "conv_w_dw": nrm(ks[15], (N_CONV, CONV_WIDTH, CONV_CH), CONV_WIDTH ** -0.5),
        "conv_b_dw": nrm(ks[16], (N_CONV, CONV_CH), 0.01),
        "conv_ln_g": 1.0 + nrm(ks[17], (N_CONV, CONV_CH), 0.01),
        "conv_ln_b": nrm(ks[18], (N_CONV, CONV_CH), 0.01),
        "conv_w_out": nrm(ks[19], (N_CONV, CONV_OUT_IN, D_MODEL), BETA * CONV_OUT_IN ** -0.5),
    }

def reference(x, mem, ln_g, ln_b, ffn1_w_gu, ffn1_w_down, ffn2_w_gu, ffn2_w_down, mem_w_kv,
              gla_w_in, gla_w_gate2, gla_b_gate, gla_g_onorm, gla_w_out,
              conv_w_in, conv_w_dw, conv_b_dw, conv_ln_g, conv_ln_b, conv_w_out):
    for i in range(DEPTH):
        j = i // N_MIXERS
        x = layer_norm(ALPHA * x + 0.5 * swiglu(x, ffn1_w_gu[i], ffn1_w_down[i]), ln_g[i, 0], ln_b[i, 0])
        if i % N_MIXERS == 0:
            y, qm = gla_mix(x @ gla_w_in[j], gla_w_gate2[j], gla_b_gate[j], gla_g_onorm[j])
            w_out = gla_w_out[j]
        else:
            y, qm = conv_mix(x @ conv_w_in[j], conv_w_dw[j], conv_b_dw[j], conv_ln_g[j], conv_ln_b[j])
            w_out = conv_w_out[j]
        m = mem_attention(qm, mem, mem_w_kv[i])
        x = layer_norm(ALPHA * x + jnp.concatenate([y, m], axis=-1) @ w_out, ln_g[i, 1], ln_b[i, 1])
        x = layer_norm(ALPHA * x + 0.5 * swiglu(x, ffn2_w_gu[i], ffn2_w_down[i]), ln_g[i, 2], ln_b[i, 2])
    return x


_drawn_inputs = setup_inputs


def setup_inputs(seed=0):
    import zlib

    import numpy as np

    out = dict(_drawn_inputs(seed))
    spreads = {}
    factors = {'gla_w_gate2': 3.108,
     'gla_b_gate': 24.252,
     'gla_g_onorm': 55.629,
     'conv_b_dw': 8.0,
     'conv_ln_g': 53.668,
     'conv_ln_b': 54.165,
     'mem': 3.328,
     'mem_w_kv': 3.24}
    for name, (base, spread) in spreads.items():
        noise = np.random.default_rng([zlib.crc32(name.encode()), seed]).standard_normal(out[name].shape)
        drawn = base * np.exp(spread * noise) if base else spread * noise
        out[name] = __import__('jax').numpy.asarray(drawn.astype(out[name].dtype))
    for name, factor in factors.items():
        out[name] = (out[name] * factor).astype(out[name].dtype)
    return out
```

```python
from contextlib import ExitStack

import concourse.bass as bass
from concourse import mybir

ALU = mybir.AluOpType
ACT = mybir.ActivationFunctionType
F32 = mybir.dt.float32
F32R = mybir.dt.float32r
I32 = mybir.dt.int32
AX_X = mybir.AxisListType.X

P = 128
SEQ = 512
D = 1024
DK = D // P
TB = SEQ // P
NMEM = 256
MB = NMEM // P
FF = 2816
FK = FF // P
HEADS = 4
DKH = 128
CHUNK = 64
NCH = SEQ // CHUNK
RANK = 16
WIDTH = 31
PAD = WIDTH - 1
DEPTH = 2
ALPHA = (2 * DEPTH) ** 0.25
LN_EPS = 1e-5
RMS_EPS = 1e-6
GATE_NORM = 16.0
MEM_SCALE = P ** -0.5
GLA_SCALE = DKH ** -0.5
OUT_K = 12

ROW_G, ROW_B = 0, DEPTH * 3 * DK
ROW_BDW = 2 * ROW_B
ROW_CG, ROW_CB = ROW_BDW + DK, ROW_BDW + 2 * DK
ROW_GATE = ROW_BDW + 3 * DK
ROW_ONORM = ROW_GATE + HEADS
ROWS = ROW_ONORM + 2

KV_N = 0
N_FFN = FK + 16
FFN_N = [8, 70, 108, 164]
GLA_N, GLA_OUT_N = 46, 62
CONV_N, CONV_OUT_N = 146, 156
N_CHUNKS = 202
DOWN_K = [6, 6, 6, 4]
PROJ_K = [6, 6]

LN_FFN = [0, 2, 3, 6]
LN_GLA_OUT, LN_CONV, LN_CONV_OUT = 1, 4, 5
LN_ROW = {0: 0, 1: 1, 2: 2, 3: 3, 5: 4, 6: 5}
EVEN_BASE = [0, 4, 8, 12, 16, 16, 20]
RES_BASE = [0, 8, 24, 32, 40, 40, 56]
RES_PER = {0: 1, 1: 2, 2: 1, 3: 1, 5: 2, 6: 1}


def build(nc, a, out):
    kv_dram = nc.dram_tensor("kv_scratch", (DEPTH, P, 2048), F32, kind="Internal").ap()
    with ExitStack() as ctx:
        def sem(name):
            return ctx.enter_context(nc.semaphore(name))

        def views(*specs):
            got = []
            with ExitStack() as part:
                for n, (name, shape, dt) in enumerate(specs):
                    got.append(part.enter_context(nc.sbuf_tensor(name, shape, dt)))
            return got

        def sb(name, shape, dt=F32):
            return ctx.enter_context(nc.sbuf_tensor(name, shape, dt))

        xhi = sb("xhi", [P, DK, SEQ], F32R)
        xlo = sb("xlo", [P, DK, SEQ], F32R)
        u = sb("u", [P, DK, SEQ])
        raw = sb("raw", [P, 2, 8, 256])
        whi = sb("whi", [P, 2, 8, 256], F32R)
        wlo = sb("wlo", [P, 2, 8, 256], F32R)
        scratch = sb("scratch", [P, 9, SEQ])
        usum, qsum, shift, delta, rstd = (scratch[:, i, :] for i in range(5))
        sq = [scratch[:, 5, :], scratch[:, 6, :]]
        act_out = [scratch[:, 7, :], scratch[:, 8, :]]
        prm = sb("prm", [P, ROWS])
        w_dw = sb("w_dw", [P, DK * WIDTH])
        ident = sb("ident", [P, P])
        ones = sb("ones", [P, P])
        small = sb("small", [P, 16])
        row_max, neg_max, row_sum, inv_sum = (small[:, 4 * i:4 * i + 4] for i in range(4))
        exp_last = sb("exp_last", [P, HEADS, NCH])

        xin, mem_in, mem_hi, mem_lo, kv_t, kv_v, rows_in, dw_in = views(
            ("xin", [P, TB, D], F32), ("mem_in", [P, MB, D], F32),
            ("mem_hi", [P, DK, NMEM], F32R), ("mem_lo", [P, DK, NMEM], F32R),
            ("kv_t", [P, DEPTH, 8, NMEM], F32), ("kv_v", [P, DEPTH, MB, 512], F32),
            ("rows_in", [ROWS, P], F32), ("dw_in", [WIDTH, D], F32))
        h_hi, h_lo = views(("h_hi", [P, FK, SEQ], F32R), ("h_lo", [P, FK, SEQ], F32R))
        qkv, states, att0, qm_g, bk, ke, v_tok = views(
            ("qkv", [P, 16, SEQ], F32), ("states", [P, 2, 7, 256], F32), ("att0", [P, TB, P], F32),
            ("qm_g", [P, HEADS, SEQ], F32), ("bk", [P, HEADS, SEQ], F32), ("ke", [P, HEADS, SEQ], F32),
            ("v_tok", [P, TB, D], F32))
        _, mo_hi_g, mo_lo_g, r_act, _, y_lo, y_hi = views(
            ("pad_a", [P, 8, SEQ], F32), ("mo_hi_g", [P, HEADS, SEQ], F32R),
            ("mo_lo_g", [P, HEADS, SEQ], F32R), ("r_act", [P, 8, SEQ], F32),
            ("pad_b", [P, HEADS, SEQ], F32), ("y_lo", [P, 8, SEQ], F32R), ("y_hi", [P, 8, SEQ], F32R))
        conv_in, qm_c, mo_hi_c, mo_lo_c, kv_c, pp_c, c_lo = views(
            ("conv_in", [P, DK, PAD + SEQ], F32), ("qm_c", [P, HEADS, SEQ], F32),
            ("mo_hi_c", [P, HEADS, SEQ], F32R), ("mo_lo_c", [P, HEADS, SEQ], F32R),
            ("kv_c", [P, 2048], F32), ("pp_c", [P, 2048], F32), ("c_lo", [P, DK, SEQ], F32R))
        c_hi, = views(("c_hi", [P, DK, SEQ], F32R))
        out_tok, = views(("out_tok", [P, 4, TB, P], F32))

        att_mask, reset, exp_a, exp_b, gate_t = usum, qsum, shift, delta, rstd
        att = [att0[:, :, :], sq[0].rearrange("p (b i) -> p b i", b=TB)]
        a_t = sq[1][0:RANK, :]
        w_gate2 = act_out[0][0:RANK, :]
        uflat = u[:, :, :].rearrange("p k s -> p (k s)")
        kv_of = [uflat[:, 0:2048], kv_c[:, :]]
        pp_of = [uflat[:, 2048:4096], pp_c[:, :]]
        qm_of = [qm_g, qm_c]
        mo_hi_of, mo_lo_of = [mo_hi_g, mo_hi_c], [mo_lo_g, mo_lo_c]

        bank = [ctx.enter_context(nc.psum_tensor(f"bank{i}", [P, SEQ], F32)) for i in range(8)]

        rows_loaded, mem_loaded, x_loaded, consts, gate_w_loaded = (
            sem(n) for n in ("rows_loaded", "mem_loaded", "x_loaded", "consts", "gate_w_loaded"))
        raw_loaded = [sem("raw_loaded0"), sem("raw_loaded1")]
        hi_ready, lo_ready, w_used = sem("hi_ready"), sem("lo_ready"), sem("w_used")
        tr_done, tr_evac = sem("tr_done"), sem("tr_evac")
        mem_hi_ready, mem_ready = sem("mem_hi_ready"), sem("mem_ready")
        kv_evac, kvv_done, kvv_evac, kv_stored, kv_loaded = (
            sem(n) for n in ("kv_evac", "kvv_done", "kvv_evac", "kv_stored", "kv_loaded"))
        silu_done, mul_done, h_hi_done, h_done = (
            sem(n) for n in ("silu_done", "mul_done", "h_hi_done", "h_done"))
        y_even, y_evac, res_done, u0_ready, u_acc, q_acc, sq_done = (
            sem(n) for n in ("y_even", "y_evac", "res_done", "u0_ready", "u_acc", "q_acc", "sq_done"))
        shift_mm, shift_ready, stats_mm, stats_act, var_ready, var_tmp, sd_ready, rstd_ready = (
            sem(n) for n in ("shift_mm", "shift_ready", "stats_mm", "stats_act", "var_ready",
                             "var_tmp", "sd_ready", "rstd_ready"))
        centred, normed, affine_done, x_hi_ready, x_ready = (
            sem(n) for n in ("centred", "normed", "affine_done", "x_hi_ready", "x_ready"))
        gla_evac, z_mm, gate_act, gate_chain, vt_mm, v_evac, exps, prods = (
            sem(n) for n in ("gla_evac", "z_mm", "gate_act", "gate_chain", "vt_mm", "v_evac",
                             "exps", "prods"))
        scores_mm, max_done, neg_max_done, p_exp, inv_done, p_norm, pt_mm, pt_evac, mo_mm, mo_hi_done, mo_done = (
            sem(n) for n in ("scores_mm", "max_done", "neg_max_done", "p_exp", "inv_done", "p_norm",
                             "pt_mm", "pt_evac", "mo_mm", "mo_hi_done", "mo_done"))
        kdt_mm, kdt_evac, att_mm, att_evac, ds_mm, state_done, o_mm, o_read, ss_done = (
            sem(n) for n in ("kdt_mm", "kdt_evac", "att_mm", "att_evac", "ds_mm", "state_done",
                             "o_mm", "o_read", "ss_done"))
        reset_done, att_clear = sem("reset_done"), sem("att_clear")
        rms_mm, rms_var, rms_sd, rms_ready, y_scaled, y_ready, y_hi_done, y_done, gla_masks = (
            sem(n) for n in ("rms_mm", "rms_var", "rms_sd", "rms_ready", "y_scaled", "y_ready",
                             "y_hi_done", "y_done", "gla_masks"))
        conv_evac, glu_done, taps_done, conv_pad = (
            sem(n) for n in ("conv_evac", "glu_done", "taps_done", "conv_pad"))
        fin_mm, fin_evac, out_stored = sem("fin_mm"), sem("fin_evac"), [sem(f"out_stored{i}") for i in range(4)]

        block = ctx.enter_context(nc.Block())

        @block.sync
        def _(sp):
            def load(n, even, parts):
                s = even
                if not isinstance(n, int) or n >= 2:
                    sp.wait_ge(lo_ready, n - 1)
                for k0, src in parts:
                    kc, w = src.shape[1], src.shape[2]
                    sp.dma_start(raw[:, s, k0:k0 + kc, 0:w], src).then_inc(raw_loaded[s], 16)

            def cols(w, c0, width=256):
                return w[:, :, bass.ds(c0, width)]

            def ffn(f):
                layer, which = divmod(f, 2)
                w_gu = a["ffn1_w_gu" if which == 0 else "ffn2_w_gu"][layer].rearrange("(k p) n -> p k n", p=P)
                w_dn = a["ffn1_w_down" if which == 0 else "ffn2_w_down"][layer].rearrange("(k p) n -> p k n", p=P)
                n0 = FFN_N[f]
                with sp.Fori(0, FK // 2) as i:
                    load(n0 + 2 * i, 0, [(0, cols(w_gu, i * 256))])
                    load(n0 + 2 * i + 1, 1, [(0, cols(w_gu, i * 256 + FF))])
                n0 += FK
                with sp.Fori(0, 4) as p:
                    k = 0
                    for c, kc in enumerate(DOWN_K):
                        load(n0 + 4 * p + c, c % 2, [(0, cols(w_dn[:, k:k + kc, :], p * 256))])
                        k += kc

            def out_proj(w, n0):
                w = w.rearrange("(k p) n -> p k n", p=P)
                with sp.Fori(0, 4) as p:
                    load(n0 + 2 * p, 0, [(0, cols(w[:, 0:6, :], p * 256))])
                    load(n0 + 2 * p + 1, 1, [(0, cols(w[:, 6:12, :], p * 256))])

            sp.dma_start(mem_in[:, :, :], a["mem"][0].rearrange("(b p) d -> p b d", p=P)).then_inc(mem_loaded, 16)
            for layer in range(DEPTH):
                w = a["mem_w_kv"][layer].rearrange("(k p) n -> p k n", p=P)
                for c in range(4):
                    n = KV_N + 4 * layer + c
                    load(n, n % 2, [(0, cols(w, c * 256))])
                    if n == 1:
                        sp.dma_start(xin[:, :, :], a["x"][0].rearrange("(b p) d -> p b d", p=P)).then_inc(x_loaded, 16)
            ffn(0)
            w = a["gla_w_in"][0].rearrange("(k p) n -> p k n", p=P)
            n = GLA_N
            load(n, 0, [(0, cols(w, 3072, P))])
            load(n + 1, 1, [(0, cols(w, 3088, P))])
            with sp.Fori(0, 4) as i:
                load(n + 2 + 2 * i, 0, [(0, cols(w, i * 512))])
                load(n + 3 + 2 * i, 1, [(0, cols(w, i * 512 + 256))])
            sp.wait_ge(x_ready, 8 * (LN_FFN[0] + 2))
            sp.wait_ge(kv_stored, 64)
            sp.dma_start(kv_of[0], kv_dram[0]).then_inc(kv_loaded, 16)
            load(n + 10, 0, [(0, cols(w, 3216))])
            load(n + 11, 1, [(0, cols(w, 3472, P))])
            with sp.Fori(0, 2) as i:
                load(n + 12 + 2 * i, 0, [(0, cols(w, i * 512 + 2048))])
                load(n + 13 + 2 * i, 1, [(0, cols(w, i * 512 + 2304))])
            out_proj(a["gla_w_out"][0], GLA_OUT_N)
            ffn(1)
            ffn(2)
            w = a["conv_w_in"][0].rearrange("(k p) n -> p k n", p=P)
            n = CONV_N
            with sp.Fori(0, 4) as i:
                load(n + 2 * i, 0, [(0, cols(w, i * 256))])
                load(n + 2 * i + 1, 1, [(0, cols(w, i * 256 + D))])
            sp.wait_ge(x_ready, 8 * (LN_FFN[2] + 2))
            sp.dma_start(kv_of[1], kv_dram[1]).then_inc(kv_loaded, 16)
            load(n + 8, 0, [(0, cols(w, 2 * D))])
            load(n + 9, 1, [(0, cols(w, 2 * D + 256))])
            out_proj(a["conv_w_out"][0], CONV_OUT_N)
            ffn(3)
            for k in range(DK):
                sp.wait_ge(fin_evac, k + 1)
                sp.dma_start(out[0].rearrange("(b p) d -> p b d", p=P)[:, :, k * P:(k + 1) * P],
                             out_tok[:, k % 4, :, :]).then_inc(out_stored[k % 4], 16)
            for i in range(4):
                sp.wait_ge(out_stored[i], 32)

        @block.gpsimd
        def _(pool):
            def split_lo(n, s, kc=8, width=256):
                pool.wait_ge(hi_ready, n + 1)
                nc.gpsimd.tensor_tensor(wlo[:, s, 0:kc, 0:width], raw[:, s, 0:kc, 0:width],
                                        whi[:, s, 0:kc, 0:width].bitcast(F32), ALU.subtract).then_inc(lo_ready, 1)

            def lo_of_x(ln, lo, hi):
                for k in range(DK):
                    pool.wait_ge(x_hi_ready, 8 * (ln + 1) + k + 1)
                    nc.gpsimd.tensor_tensor(lo[:, k, :], u[:, k, :], hi[:, k, 0:SEQ].bitcast(F32),
                                            ALU.subtract).then_inc(x_ready, 1)

            def ffn(f):
                n0 = FFN_N[f]
                with pool.Fori(0, FK // 2 - 1) as i:
                    split_lo(n0 + 2 * i + 2, 0)
                    split_lo(n0 + 2 * i + 3, 1)
                down(n0 + FK)

            def down(n0):
                split_lo(n0, 0, 6)
                split_lo(n0 + 1, 1, 6)
                with pool.Fori(0, 3) as p:
                    for c in range(4):
                        split_lo(n0 + 4 * p + 2 + c, c % 2, DOWN_K[(c + 2) % 4])
                split_lo(n0 + 14, 0, 6)
                split_lo(n0 + 15, 1, 4)

            nc.gpsimd.memset(ones[:, :], 1.0).then_inc(consts, 1)
            nc.gpsimd.memset(ident[:, :], 0.0).then_inc(consts, 1)
            pool.wait_ge(consts, 2)
            nc.gpsimd.affine_select(out=ident[:, :], in_=ident[:, :], compare_op=ALU.not_equal, fill=1.0,
                                    base=0, pattern=[[-1, P]], channel_multiplier=1).then_inc(consts, 1)
            split_lo(0, 0)
            split_lo(1, 1)
            for k in range(DK):
                pool.wait_ge(mem_hi_ready, 2 * k + 2)
                nc.gpsimd.tensor_tensor(mem_lo[:, k, :], kv_t[:, 0, k, :],
                                        mem_hi[:, k, :].bitcast(F32), ALU.subtract).then_inc(mem_ready, 1)
            lo_of_x(-1, xlo, xhi)
            for n in range(2, 10):
                split_lo(n, n % 2)
            ffn(0)
            split_lo(GLA_N, 0, 8, P)
            split_lo(GLA_N + 1, 1, 8, P)
            lo_of_x(LN_FFN[0], xlo, xhi)
            nc.gpsimd.memset(att_mask, 1.0).then_inc(gla_masks, 1)
            pool.wait_ge(gla_masks, 1)
            m = att_mask.rearrange("p (b i) -> p b i", b=TB)
            nc.gpsimd.affine_select(out=m, in_=m, compare_op=ALU.is_ge, fill=0.0, base=0,
                                    pattern=[[0, TB], [1, P]], channel_multiplier=-1).then_inc(gla_masks, 1)
            pool.wait_ge(gla_masks, 2)
            nc.gpsimd.memset(m[0:CHUNK, :, CHUNK:P], 0.0).then_inc(gla_masks, 1)
            with pool.Fori(0, 4) as i:
                split_lo(GLA_N + 2 + 2 * i, 0)
                split_lo(GLA_N + 3 + 2 * i, 1)
            split_lo(GLA_N + 10, 0)
            split_lo(GLA_N + 11, 1, 8, P)
            with pool.Fori(0, 2) as i:
                split_lo(GLA_N + 12 + 2 * i, 0)
                split_lo(GLA_N + 13 + 2 * i, 1)
            with pool.Fori(0, 4) as i:
                split_lo(GLA_OUT_N + 2 * i, 0, 6)
                split_lo(GLA_OUT_N + 2 * i + 1, 1, 6)
            split_lo(FFN_N[1], 0)
            split_lo(FFN_N[1] + 1, 1)
            lo_of_x(LN_GLA_OUT, xlo, xhi)
            ffn(1)
            split_lo(FFN_N[2], 0)
            split_lo(FFN_N[2] + 1, 1)
            lo_of_x(LN_FFN[1], xlo, xhi)
            ffn(2)
            split_lo(CONV_N, 0)
            split_lo(CONV_N + 1, 1)
            lo_of_x(LN_FFN[2], xlo, xhi)
            nc.gpsimd.memset(conv_in[:, :, 0:PAD], 0.0).then_inc(conv_pad, 1)
            for i in range(4):
                split_lo(CONV_N + 2 * i + 2, 0)
                split_lo(CONV_N + 2 * i + 3, 1)
                pool.wait_ge(conv_evac, 4 * i + 4)
                for t in range(2):
                    nc.gpsimd.tensor_tensor(conv_in[:, 2 * i + t, PAD:PAD + SEQ], conv_in[:, 2 * i + t, PAD:PAD + SEQ],
                                            act_out[t], ALU.mult).then_inc(glu_done, 1)
            split_lo(CONV_OUT_N, 0, 6)
            split_lo(CONV_OUT_N + 1, 1, 6)
            lo_of_x(LN_CONV, c_lo, c_hi)
            with pool.Fori(1, 4) as i:
                split_lo(CONV_OUT_N + 2 * i, 0, 6)
                split_lo(CONV_OUT_N + 2 * i + 1, 1, 6)
            split_lo(FFN_N[3], 0)
            split_lo(FFN_N[3] + 1, 1)
            lo_of_x(LN_CONV_OUT, xlo, xhi)
            ffn(3)

        @block.scalar
        def _(act):
            def split_hi(turn, s, kc=8, width=256):
                n = 2 * turn + s
                if isinstance(n, int) and n >= N_CHUNKS:
                    return
                if not isinstance(n, int) or n >= 2:
                    act.wait_ge(w_used, n - 1)
                act.wait_ge(raw_loaded[s], 16 * (turn + 1))
                nc.scalar.copy(whi[:, s, 0:kc, 0:width], raw[:, s, 0:kc, 0:width]).then_inc(hi_ready, 1)

            def ffn_pair(f, i, nxt):
                t0 = FFN_N[f] // 2
                act.wait_ge(w_used, FFN_N[f] + 2 * i + 1)
                split_hi(t0 + i + 1, 0, 8 if nxt else DOWN_K[0])
                for t in range(2):
                    if not isinstance(i, int) or f + i > 0:
                        act.wait_ge(h_done, FK * f + 2 * i)
                    nc.scalar.activation(act_out[t], bank[t][:, :], ACT.Silu).then_inc(silu_done, 1)
                act.wait_ge(w_used, FFN_N[f] + 2 * i + 2)
                split_hi(t0 + i + 1, 1, 8 if nxt else DOWN_K[1])
                if isinstance(i, int) and f + i == 0:
                    act.wait_ge(kv_stored, 64)
                for t in range(2):
                    act.wait_ge(mul_done, FK * f + 2 * i + t + 1)
                    nc.scalar.copy(h_hi[:, bass.ds(2 * i + t, 1), :], act_out[t].rearrange("p (a s) -> p a s", a=1)).then_inc(h_hi_done, 1)

            def squares(ln, p):
                for t in range(2):
                    d = 2 * p + t
                    if isinstance(p, int) and d == 0:
                        act.wait_ge(u0_ready, ln + 1)
                    else:
                        act.wait_ge(y_evac, 8 * ln + d + 1)
                    if not isinstance(p, int) or d >= 2:
                        act.wait_ge(q_acc, 6 * ln + d - 1)
                    nc.scalar.activation(sq[t], u[:, bass.ds(d, 1), :].rearrange("p a s -> p (a s)"), ACT.Square).then_inc(sq_done, 1)

            def shift_copy(ln):
                act.wait_ge(shift_mm, ln + 1)
                nc.scalar.activation(shift, bank[4][:, :], ACT.Copy, scale=1.0 / P).then_inc(shift_ready, 1)

            def down_pair(f, p, last=False):
                t0 = (FFN_N[f] + FK) // 2 + 2 * p
                for c in range(3):
                    kc = 8 if last and c >= 2 else DOWN_K[(c + 2) % 4]
                    width = P if last and c == 2 and f in (0,) else 256
                    split_hi(t0 + 1 + c // 2, c % 2, kc, width)
                if isinstance(p, int) and p == 0:
                    shift_copy(LN_FFN[f])
                squares(LN_FFN[f], p)
                split_hi(t0 + 2, 1, 8 if last else DOWN_K[1], P if last and f == 0 else 256)

            def proj_pair(ln, n0, p, last=False):
                split_hi(n0 // 2 + p + 1, 0, 8 if last else 6)
                if isinstance(p, int) and p == 0:
                    shift_copy(ln)
                squares(ln, p)
                split_hi(n0 // 2 + p + 1, 1, 8 if last else 6)

            def stats(ln):
                act.wait_ge(stats_mm, 2 * ln + 1)
                nc.scalar.activation(delta, bank[5][:, :], ACT.Copy, scale=1.0 / D).then_inc(stats_act, 1)
                nc.scalar.activation(sq[0], bank[5][:, :], ACT.Square, scale=1.0 / D).then_inc(stats_act, 1)
                act.wait_ge(var_ready, ln + 1)
                nc.scalar.activation(qsum, sq[0], ACT.Sqrt).then_inc(sd_ready, 1)

            def affine(ln, hi, g_row, b_row, func=ACT.Identity):
                def one(k):
                    act.wait_ge(normed, 8 * ln + k + 1)
                    nc.scalar.activation(u[:, k, :], u[:, k, :], func, scale=prm[:, g_row + k:g_row + k + 1],
                                         bias=prm[:, b_row + k:b_row + k + 1]).then_inc(affine_done, 1)
                one(0)
                for k in range(DK):
                    if k + 1 < DK:
                        one(k + 1)
                    if hi is not None:
                        act.wait_ge(affine_done, 8 * ln + k + 1)
                        nc.scalar.copy(hi[:, k, 0:SEQ], u[:, k, :]).then_inc(x_hi_ready, 1)

            def norm(ln, hi=xhi):
                stats(ln)
                affine(ln, hi, ROW_G + LN_ROW[ln] * DK, ROW_B + LN_ROW[ln] * DK)

            def ffn(f):
                ffn_pair(f, 0, True)
                with act.Fori(1, FK // 2 - 1) as i:
                    ffn_pair(f, i, True)
                ffn_pair(f, FK // 2 - 1, False)
                down_pair(f, 0)
                with act.Fori(1, 3) as p:
                    down_pair(f, p)
                down_pair(f, 3, last=True)
                if f < 3:
                    norm(LN_FFN[f])

            def out_proj(ln, n0):
                proj_pair(ln, n0, 0)
                with act.Fori(1, 3) as p:
                    proj_pair(ln, n0, p)
                proj_pair(ln, n0, 3, last=True)
                norm(ln)

            def attention(m):
                pp = pp_of[m]
                probs = pp[:, 0:1024].rearrange("p (b m) -> p b m", b=TB)
                probs_t = pp[:, 1024:2048].rearrange("p (b s) -> p b s", b=MB)
                for h in range(HEADS):
                    g = HEADS * m + h
                    act.wait_ge(neg_max_done, g + 1)
                    if g:
                        act.wait_ge(pt_mm, 2 * g)
                    for b in range(TB):
                        nc.scalar.activation(probs[:, b, :], bank[4 + b // 2][:, (b % 2) * 256:(b % 2) * 256 + 256],
                                             ACT.Exp, scale=MEM_SCALE, bias=neg_max[:, b:b + 1],
                                             accum_out=row_sum[:, b:b + 1]).then_inc(p_exp, 1)
                    act.wait_ge(pt_mm, 2 * g + 1)
                    if g:
                        act.wait_ge(mo_mm, g)
                    nc.scalar.copy(probs_t[:, 0, :], bank[6][:, :]).then_inc(pt_evac, 1)
                    act.wait_ge(mo_mm, g + 1)
                    nc.scalar.copy(mo_hi_of[m][:, h, :], bank[h][:, :]).then_inc(mo_hi_done, 1)

            r0 = 0
            for name, rows in (("ln_g", DEPTH * 3 * DK), ("ln_b", DEPTH * 3 * DK), ("conv_b_dw", DK),
                               ("conv_ln_g", DK), ("conv_ln_b", DK), ("gla_b_gate", HEADS), ("gla_g_onorm", 2)):
                src = a[name]
                src = src.rearrange("l w (k p) -> (l w k) p", p=P) if len(src.shape) == 3 else src.rearrange("l (k p) -> (l k) p", p=P)
                act.dma_start(rows_in[r0:r0 + rows, :], src).then_inc(rows_loaded, 16)
                r0 += rows
            act.dma_start(dw_in[:, :], a["conv_w_dw"][0]).then_inc(rows_loaded, 16)
            split_hi(0, 0)
            split_hi(0, 1)
            act.wait_ge(tr_done, 1)
            nc.scalar.copy(prm[:, :], bank[7][:, 0:ROWS]).then_inc(tr_evac, 1)
            act.wait_ge(tr_done, 2)
            nc.scalar.copy(w_dw[:, :], bank[6][:, 0:DK * WIDTH]).then_inc(tr_evac, 1)
            for k in range(DK):
                act.wait_ge(tr_done, 3 + k)
                nc.scalar.copy(kv_t[:, 0, k, :], bank[4 + k % 4][:, 0:NMEM]).then_inc(mem_hi_ready, 1)
                act.wait_ge(mem_hi_ready, 2 * k + 1)
                nc.scalar.copy(mem_hi[:, k, :], kv_t[:, 0, k, :]).then_inc(mem_hi_ready, 1)
            for k in range(DK):
                act.wait_ge(tr_done, 3 + DK + k)
                nc.scalar.copy(u[:, k, :], bank[4 + k % 4][:, :]).then_inc(tr_evac, 1)
                act.wait_ge(tr_evac, 3 + k)
                nc.scalar.copy(xhi[:, k, :], u[:, k, :]).then_inc(x_hi_ready, 1)
            for n in range(8):
                act.wait_ge(w_used, n + 1)
                split_hi(n // 2 + 1, n % 2)
                for t in range(2):
                    if n == 0 and t == 0:
                        act.wait_ge(mem_ready, DK)
                    nc.scalar.copy(kv_t[:, n // 4, 2 * (n % 4) + t, :], bank[2 * (n % 2) + t][:, 0:NMEM]).then_inc(kv_evac, 1)
            for j in range(4):
                act.wait_ge(kvv_done, j + 1)
                nc.scalar.copy(kv_v[:, j // 2, j % 2, :], bank[4 + j][:, :]).then_inc(kvv_evac, 1)
            act.wait_ge(kvv_evac, 4)
            for layer in range(DEPTH):
                act.dma_start(kv_dram[layer, :, 0:1024],
                              kv_t[:, layer, 0:4, :].rearrange("p h m -> p (h m)")).then_inc(kv_stored, 16)
                act.dma_start(kv_dram[layer, :, 1024:2048],
                              kv_v[:, layer, :, :].rearrange("p b e -> p (b e)")).then_inc(kv_stored, 16)
            ffn(0)

            t0, n0 = GLA_N // 2, GLA_N
            act.dma_start(w_gate2, a["gla_w_gate2"][0]).then_inc(gate_w_loaded, 16)
            act.wait_ge(w_used, n0 + 1)
            split_hi(t0 + 1, 0)
            nc.scalar.copy(a_t, bank[0][0:RANK, :]).then_inc(gla_evac, 1)
            act.wait_ge(w_used, n0 + 2)
            split_hi(t0 + 1, 1)
            nc.scalar.copy(qm_g[:, 0, :], bank[2][:, :]).then_inc(gla_evac, 1)
            for i in range(4):
                act.wait_ge(z_mm, i + 1)
                act.wait_ge(gate_chain, 3 * i + 1)
                nc.scalar.activation(exp_a, bank[4 + i][:, :], ACT.Abs,
                                     bias=prm[:, ROW_GATE + i:ROW_GATE + i + 1]).then_inc(gate_act, 1)
                act.wait_ge(gate_act, 3 * i + 1)
                nc.scalar.activation(exp_a, exp_a, ACT.Exp, scale=-1.0).then_inc(gate_act, 1)
                act.wait_ge(gate_act, 3 * i + 2)
                nc.scalar.activation(exp_a, exp_a, ACT.Ln, bias=1.0).then_inc(gate_act, 1)
                for c in range(2):
                    act.wait_ge(w_used, n0 + 3 + 2 * i + c)
                    split_hi(t0 + 2 + i, c, 8, P if i == 3 and c == 1 else 256)
                    for t in range(2):
                        nc.scalar.copy(qkv[:, 4 * i + 2 * c + t, :], bank[2 * c + t][:, :]).then_inc(gla_evac, 1)
            for e in range(8):
                act.wait_ge(vt_mm, e + 1)
                nc.scalar.copy(v_tok[:, :, e * P:(e + 1) * P],
                               bank[4 + e % 4][:, :].rearrange("p (b e) -> p b e", b=TB)).then_inc(v_evac, 1)

            def decays(h):
                b_h = bk[:, h, :]
                if h:
                    act.wait_ge(prods, 4 * h)
                act.wait_ge(gate_chain, 3 * h + 4)
                nc.scalar.activation(exp_a, b_h, ACT.Exp, scale=1.0 / GATE_NORM).then_inc(exps, 1)
                nc.scalar.activation(exp_b, b_h, ACT.Exp, scale=-1.0 / GATE_NORM).then_inc(exps, 1)
                nc.scalar.activation(exp_last[:, h, :], bk[:, h, CHUNK - 1:SEQ:CHUNK], ACT.Exp,
                                     scale=1.0 / GATE_NORM).then_inc(exps, 1)
                act.wait_ge(prods, 4 * h + 2)
                nc.scalar.activation(exp_a, gate_t, ACT.Exp, scale=1.0 / GATE_NORM).then_inc(exps, 1)

            decays(0)
            decays(1)
            act.wait_ge(w_used, n0 + 11)
            split_hi(t0 + 6, 0)
            nc.scalar.copy(qm_g[:, 1, :], bank[0][:, :]).then_inc(gla_evac, 1)
            nc.scalar.copy(qm_g[:, 2, :], bank[1][:, :]).then_inc(gla_evac, 1)
            decays(2)
            act.wait_ge(w_used, n0 + 12)
            split_hi(t0 + 6, 1)
            nc.scalar.copy(qm_g[:, 3, :], bank[2][:, :]).then_inc(gla_evac, 1)
            decays(3)
            attention(0)

            def kd_evac(h):
                act.wait_ge(kdt_mm, h + 1)
                nc.scalar.copy(bk[:, h, :], bank[4][:, :]).then_inc(kdt_evac, 1)

            kd_evac(0)
            for h in range(HEADS):
                if h + 1 < HEADS:
                    kd_evac(h + 1)
                for e, tmp in ((0, exp_a), (1, exp_b)):
                    b = bank[2 * (h % 2) + e][:, :]
                    act.wait_ge(o_mm, 2 * h + e + 1)
                    nc.scalar.copy(u[:, 2 * h + e, :], b).then_inc(o_read, 1)
                    if h:
                        act.wait_ge(ss_done, h)
                    nc.scalar.activation(tmp, b, ACT.Square).then_inc(o_read, 1)
            for j in range(4):
                act.wait_ge(w_used, n0 + 13 + j)
                split_hi(t0 + 7 + j // 2, j % 2, 8 if j < 2 else 6)
                if j == 0:
                    for h in range(HEADS):
                        act.wait_ge(rms_var, h + 1)
                        nc.scalar.activation(ke[:, h, :], ke[:, h, :], ACT.Sqrt).then_inc(rms_sd, 1)
                for t in range(2):
                    nc.scalar.activation(r_act[:, 2 * j + t, :], bank[2 * (j % 2) + t][:, :], ACT.Silu).then_inc(gla_evac, 1)
                for k in (range(2 * j - 2, 2 * j) if 0 < j < 3 else range(4, 8) if j == 3 else ()):
                    act.wait_ge(y_ready, k + 1)
                    nc.scalar.copy(y_hi[:, k, :], u[:, k, :]).then_inc(y_hi_done, 1)
            out_proj(LN_GLA_OUT, GLA_OUT_N)
            ffn(1)
            ffn(2)

            t0, n0 = CONV_N // 2, CONV_N
            for i in range(4):
                act.wait_ge(w_used, n0 + 2 * i + 1)
                split_hi(t0 + i + 1, 0)
                for t in range(2):
                    nc.scalar.copy(conv_in[:, 2 * i + t, PAD:PAD + SEQ], bank[t][:, :]).then_inc(conv_evac, 1)
                act.wait_ge(w_used, n0 + 2 * i + 2)
                split_hi(t0 + i + 1, 1)
                if i:
                    act.wait_ge(glu_done, 2 * i)
                for t in range(2):
                    nc.scalar.activation(act_out[t], bank[2 + t][:, :], ACT.Sigmoid).then_inc(conv_evac, 1)
            shift_copy(LN_CONV)
            for c in range(2):
                act.wait_ge(w_used, n0 + 9 + c)
                split_hi(t0 + 5, c, 6)
                for t in range(2):
                    nc.scalar.copy(qm_c[:, 2 * c + t, :], bank[2 * c + t][:, :]).then_inc(conv_evac, 1)
            squares(LN_CONV, 0)
            squares(LN_CONV, 1)
            attention(1)
            squares(LN_CONV, 2)
            squares(LN_CONV, 3)
            stats(LN_CONV)
            affine(LN_CONV, c_hi, ROW_CG, ROW_CB, ACT.Silu)
            out_proj(LN_CONV_OUT, CONV_OUT_N)
            ffn(3)
            ln = LN_FFN[3]
            stats(ln)
            for k in range(DK + 1):
                if k < DK:
                    g, b = ROW_G + LN_ROW[ln] * DK + k, ROW_B + LN_ROW[ln] * DK + k
                    act.wait_ge(normed, 8 * ln + k + 1)
                    nc.scalar.activation(u[:, k, :], u[:, k, :], ACT.Identity, scale=prm[:, g:g + 1],
                                         bias=prm[:, b:b + 1]).then_inc(affine_done, 1)
                if k:
                    j = k - 1
                    act.wait_ge(fin_mm, j + 1)
                    if j >= 4:
                        act.wait_ge(out_stored[j % 4], 16)
                    nc.scalar.copy(out_tok[:, j % 4, :, :],
                                   bank[j % 4][:, :].rearrange("p (b e) -> p b e", b=TB)).then_inc(fin_evac, 1)

        @block.vector
        def _(dve):
            def ffn_pair(f, i):
                for t in range(2):
                    dve.wait_ge(w_used, FFN_N[f] + 2 * i + 2)
                    dve.wait_ge(silu_done, FK * f + 2 * i + t + 1)
                    nc.vector.tensor_tensor(act_out[t], act_out[t], bank[2 + t][:, :], ALU.mult).then_inc(mul_done, 1)
                for t in range(2):
                    dve.wait_ge(h_hi_done, FK * f + 2 * i + t + 1)
                    nc.vector.tensor_tensor(h_lo[:, bass.ds(2 * i + t, 1), :], act_out[t].rearrange("p (a s) -> p a s", a=1),
                                            h_hi[:, bass.ds(2 * i + t, 1), :].bitcast(F32),
                                            ALU.subtract).then_inc(h_done, 1)

            def blk(x, d):
                return x[:, bass.ds(d, 1), :].rearrange("p a s -> p (a s)")

            def add_sum(ln, d):
                dve.wait_ge(y_evac, 8 * ln + d + 1)
                if isinstance(d, int) and d == 1:
                    dve.wait_ge(u0_ready, ln + 1)
                    nc.vector.tensor_tensor(usum, u[:, 0, :], u[:, 1, :], ALU.add).then_inc(u_acc, 1)
                else:
                    dve.wait_ge(u_acc, 6 * ln + d - 1)
                    nc.vector.tensor_tensor(usum, usum, blk(u, d), ALU.add).then_inc(u_acc, 1)

            def add_square(ln, d, t):
                dve.wait_ge(sq_done, 8 * ln + d + 1)
                if isinstance(d, int) and d == 1:
                    nc.vector.tensor_tensor(qsum, sq[0], sq[1], ALU.add).then_inc(q_acc, 1)
                else:
                    dve.wait_ge(q_acc, 6 * ln + d - 1)
                    nc.vector.tensor_tensor(qsum, qsum, sq[t], ALU.add).then_inc(q_acc, 1)

            def take_shift(ln):
                dve.wait_ge(y_evac, 8 * ln + 1)
                dve.wait_ge(shift_ready, ln + 1)
                nc.vector.tensor_tensor(u[:, 0, :], u[:, 0, :], shift, ALU.subtract).then_inc(u0_ready, 1)

            def residual_pair(ln, p, n_used, coef, last=False):
                for t in range(2):
                    d = 2 * p + t
                    first = isinstance(d, int) and d == 0
                    if t == 1 and not (isinstance(p, int) and p == 0):
                        add_square(ln, d - 1, 0)
                    res = RES_BASE[ln] + RES_PER[ln] * d
                    src = u if RES_PER[ln] == 1 else xlo[:, :, :].bitcast(F32)
                    if first:
                        nc.vector.tensor_scalar(u[:, 0, :], src[:, 0, :], ALPHA, None, ALU.mult).then_inc(res_done, 1)
                    else:
                        nc.vector.scalar_tensor_tensor(out=blk(u, d), in0=blk(src, d), scalar=ALPHA, in1=shift,
                                                       op0=ALU.mult, op1=ALU.subtract).then_inc(res_done, 1)
                    dve.wait_ge(res_done, res + 1)
                    if RES_PER[ln] == 2:
                        nc.vector.scalar_tensor_tensor(out=blk(u, d), in0=blk(xhi[:, :, :].bitcast(F32), d), scalar=ALPHA,
                                                       in1=blk(u, d), op0=ALU.mult, op1=ALU.add).then_inc(res_done, 1)
                        dve.wait_ge(res_done, res + 2)
                    if t == 0:
                        dve.wait_ge(y_even, EVEN_BASE[ln] + p + 1)
                    else:
                        dve.wait_ge(w_used, n_used)
                    nc.vector.scalar_tensor_tensor(out=blk(u, d), in0=bank[t][:, :], scalar=coef, in1=blk(u, d),
                                                   op0=ALU.mult, op1=ALU.add).then_inc(y_evac, 1)
                    if first:
                        take_shift(ln)
                    elif not (last and t == 1):
                        add_sum(ln, d)
                if not last:
                    add_square(ln, 2 * p + 1, 1)

            def residual(ln, n0, per_pair, coef):
                residual_pair(ln, 0, n0 + per_pair, coef)
                with dve.Fori(1, 3) as p:
                    residual_pair(ln, p, n0 + per_pair * p + per_pair, coef)
                residual_pair(ln, 3, n0 + 4 * per_pair, coef, last=True)

            def norm(ln):
                dve.wait_ge(stats_mm, 2 * ln + 2)
                dve.wait_ge(stats_act, 2 * ln + 2)
                nc.vector.scalar_tensor_tensor(out=sq[0], in0=bank[6][:, :], scalar=1.0 / D, in1=sq[0],
                                               op0=ALU.mult, op1=ALU.subtract).then_inc(var_tmp, 1)
                dve.wait_ge(var_tmp, ln + 1)
                nc.vector.tensor_scalar(sq[0], sq[0], 0.0, LN_EPS, ALU.max, ALU.add).then_inc(var_ready, 1)

                def centre(k):
                    nc.vector.tensor_tensor(u[:, k, :], u[:, k, :], delta, ALU.subtract).then_inc(centred, 1)

                def scale(k):
                    dve.wait_ge(centred, 8 * ln + k + 1)
                    nc.vector.tensor_tensor(u[:, k, :], u[:, k, :], rstd, ALU.mult).then_inc(normed, 1)

                centre(0)
                centre(1)
                dve.wait_ge(sd_ready, ln + 1)
                nc.vector.reciprocal(rstd, qsum).then_inc(rstd_ready, 1)
                dve.wait_ge(rstd_ready, ln + 1)
                for k in range(DK):
                    scale(k)
                    if k + 2 < DK:
                        centre(k + 2)

            def ffn(f):
                ffn_pair(f, 0)
                with dve.Fori(1, FK // 2) as i:
                    ffn_pair(f, i)
                residual(LN_FFN[f], FFN_N[f] + FK, 4, 0.5)
                norm(LN_FFN[f])

            def attention(m):
                pp = pp_of[m]
                probs = pp[:, 0:1024].rearrange("p (b m) -> p b m", b=TB)
                probs_t = pp[:, 1024:2048].rearrange("p (b s) -> p b s", b=MB)
                for h in range(HEADS):
                    g = HEADS * m + h
                    for j in range(2):
                        dve.wait_ge(scores_mm, 2 * g + j + 1)
                        nc.vector.tensor_reduce(row_max[:, 2 * j:2 * j + 2],
                                                bank[4 + j][:, :].rearrange("p (b m) -> p b m", b=2),
                                                AX_X, ALU.max).then_inc(max_done, 1)
                    dve.wait_ge(max_done, 2 * g + 2)
                    nc.vector.tensor_scalar(neg_max, row_max, -MEM_SCALE, None, ALU.mult).then_inc(neg_max_done, 1)
                    dve.wait_ge(p_exp, 4 * g + 4)
                    nc.vector.reciprocal(inv_sum, row_sum).then_inc(inv_done, 1)
                    dve.wait_ge(inv_done, g + 1)
                    for b in range(TB):
                        nc.vector.tensor_scalar(probs[:, b, :], probs[:, b, :], inv_sum[:, b:b + 1], None,
                                                ALU.mult).then_inc(p_norm, 1)
                    dve.wait_ge(pt_mm, 2 * g + 2)
                    if g:
                        dve.wait_ge(mo_mm, g)
                    nc.vector.tensor_copy(probs_t[:, 1, :], bank[7][:, :]).then_inc(pt_evac, 1)
                    dve.wait_ge(mo_hi_done, g + 1)
                    nc.vector.tensor_tensor(mo_lo_of[m][:, h, :], bank[h][:, :], mo_hi_of[m][:, h, :].bitcast(F32),
                                            ALU.subtract).then_inc(mo_done, 1)

            ffn(0)

            dve.wait_ge(x_ready, 8 * (LN_FFN[0] + 2))
            nc.vector.memset(reset, 1.0).then_inc(reset_done, 1)
            dve.wait_ge(reset_done, 1)
            nc.vector.memset(reset[:, 0:SEQ:CHUNK], 0.0).then_inc(gate_chain, 1)
            for h in range(HEADS):
                dve.wait_ge(gate_act, 3 * h + 3)
                nc.vector.tensor_scalar(gate_t, bank[4 + h][:, :], prm[:, ROW_GATE + h:ROW_GATE + h + 1], 0.0,
                                        ALU.add, ALU.min).then_inc(gate_chain, 1)
                dve.wait_ge(gate_chain, 3 * h + 2)
                nc.vector.tensor_tensor(gate_t, gate_t, exp_a, ALU.subtract).then_inc(gate_chain, 1)
                dve.wait_ge(gate_chain, 3 * h + 3)
                nc.vector.tensor_tensor_scan(bk[:, h, :], reset, gate_t, 0.0, ALU.mult, ALU.add).then_inc(gate_chain, 1)
            for h in range(HEADS):
                dve.wait_ge(gate_chain, 3 * HEADS + 1)
                if h == 0:
                    dve.wait_ge(gla_evac, 18)
                if h:
                    dve.wait_ge(exps, 4 * h)
                b_h = bk[:, h, :].rearrange("p (c s) -> p c s", s=CHUNK)
                nc.vector.tensor_tensor(gate_t.rearrange("p (c s) -> p c s", s=CHUNK),
                                        b_h[:, :, CHUNK - 1:CHUNK].to_broadcast([P, NCH, CHUNK]), b_h,
                                        ALU.subtract).then_inc(prods, 1)
                dve.wait_ge(exps, 4 * h + 1)
                nc.vector.scalar_tensor_tensor(out=qkv[:, h, :], in0=qkv[:, h, :], scalar=GLA_SCALE, in1=exp_a,
                                               op0=ALU.mult, op1=ALU.mult).then_inc(prods, 1)
                dve.wait_ge(exps, 4 * h + 2)
                nc.vector.tensor_tensor(ke[:, h, :], qkv[:, 4 + h, :], exp_b, ALU.mult).then_inc(prods, 1)
                dve.wait_ge(exps, 4 * h + 4)
                nc.vector.tensor_tensor(qkv[:, 4 + h, :], qkv[:, 4 + h, :], exp_a, ALU.mult).then_inc(prods, 1)
            attention(0)
            dve.wait_ge(gla_masks, 3)
            for t in range(2):
                nc.vector.memset(att[t], 0.0).then_inc(att_clear, 1)
            dve.wait_ge(att_clear, 2)

            def mask_att(h):
                dve.wait_ge(att_mm, h + 1)
                if h >= 2:
                    dve.wait_ge(o_mm, 2 * (h - 1))
                nc.vector.copy_predicated(att[h % 2], att_mask.rearrange("p (b i) -> p b i", b=TB).bitcast(I32),
                                          bank[5][:, :].rearrange("p (b i) -> p b i", b=TB)).then_inc(att_evac, 1)

            mask_att(0)
            for h in range(HEADS):
                s_h = states[:, h % 2, :, :]
                for c in range(7):
                    dve.wait_ge(ds_mm, 2 * h + c // 4 + 1)
                    if h >= 2 and c == 0:
                        dve.wait_ge(o_mm, 2 * (h - 1))
                    add = bank[6 + c % 2][:, (c // 2 % 2) * 256:(c // 2 % 2) * 256 + 256]
                    if c == 0:
                        nc.vector.tensor_copy(s_h[:, 0, :], add).then_inc(state_done, 1)
                    else:
                        dve.wait_ge(state_done, 7 * h + c)
                        nc.vector.scalar_tensor_tensor(out=s_h[:, c, :], in0=s_h[:, c - 1, :],
                                                       scalar=exp_last[:, h, c:c + 1], in1=add,
                                                       op0=ALU.mult, op1=ALU.add).then_inc(state_done, 1)
                if h + 1 < HEADS:
                    mask_att(h + 1)
                dve.wait_ge(o_read, 4 * h + 4)
                nc.vector.tensor_tensor(ke[:, h, :], exp_a, exp_b, ALU.add).then_inc(ss_done, 1)
            for h in range(HEADS):
                dve.wait_ge(rms_mm, h + 1)
                nc.vector.tensor_scalar(ke[:, h, :], bank[4 + h][:, :], 1.0 / 256, RMS_EPS,
                                        ALU.mult, ALU.add).then_inc(rms_var, 1)
            for h in range(HEADS):
                dve.wait_ge(rms_sd, h + 1)
                nc.vector.reciprocal(ke[:, h, :], ke[:, h, :]).then_inc(rms_ready, 1)
                dve.wait_ge(rms_ready, h + 1)
                for k in (2 * h, 2 * h + 1):
                    g = ROW_ONORM + k % 2
                    nc.vector.scalar_tensor_tensor(out=u[:, k, :], in0=u[:, k, :], scalar=prm[:, g:g + 1],
                                                   in1=ke[:, h, :], op0=ALU.mult, op1=ALU.mult).then_inc(y_scaled, 1)
                for k in (2 * h, 2 * h + 1):
                    dve.wait_ge(y_scaled, k + 1)
                    dve.wait_ge(gla_evac, 21 + k + 1)
                    nc.vector.tensor_tensor(u[:, k, :], u[:, k, :], r_act[:, k, :], ALU.mult).then_inc(y_ready, 1)
                for k in (2 * h, 2 * h + 1):
                    dve.wait_ge(y_hi_done, k + 1)
                    nc.vector.tensor_tensor(y_lo[:, k, :], u[:, k, :], y_hi[:, k, :].bitcast(F32),
                                            ALU.subtract).then_inc(y_done, 1)
            residual(LN_GLA_OUT, GLA_OUT_N, 2, 1.0)
            norm(LN_GLA_OUT)
            ffn(1)
            ffn(2)

            def taps(i):
                dve.wait_ge(glu_done, 2 * i + 2)
                for j in range(WIDTH):
                    for t in range(2):
                        c = 2 * i + t
                        src = conv_in[:, c, j:j + SEQ]
                        w = w_dw[:, c * WIDTH + j:c * WIDTH + j + 1]
                        if j == 0:
                            nc.vector.tensor_scalar(u[:, c, :], src, w, prm[:, ROW_BDW + c:ROW_BDW + c + 1],
                                                    ALU.mult, ALU.add).then_inc(taps_done, 1)
                        else:
                            dve.wait_ge(taps_done, 2 * WIDTH * i + 2 * (j - 1) + t + 1)
                            last = nc.vector.scalar_tensor_tensor(out=u[:, c, :], in0=src, scalar=w, in1=u[:, c, :],
                                                                  op0=ALU.mult, op1=ALU.add)
                            last.then_inc(taps_done, 1)

            def take_out_shift(i):
                for t in range(2):
                    d = 2 * i + t
                    if d == 0:
                        take_shift(LN_CONV)
                        continue
                    if i and t == 1:
                        add_square(LN_CONV, d - 1, 0)
                    nc.vector.tensor_tensor(u[:, d, :], u[:, d, :], shift, ALU.subtract).then_inc(y_evac, 1)
                    if d < DK - 1:
                        add_sum(LN_CONV, d)
                if i < 3:
                    add_square(LN_CONV, 2 * i + 1, 1)

            dve.wait_ge(x_ready, 8 * (LN_FFN[2] + 2))
            dve.wait_ge(conv_pad, 1)
            taps(0)
            dve.wait_ge(taps_done, 2 * WIDTH)
            dve.sem_inc(y_evac, 1)
            taps(1)
            dve.wait_ge(taps_done, 4 * WIDTH)
            take_out_shift(0)
            take_out_shift(1)
            attention(1)
            taps(2)
            dve.wait_ge(taps_done, 6 * WIDTH)
            take_out_shift(2)
            taps(3)
            dve.wait_ge(taps_done, 8 * WIDTH)
            take_out_shift(3)
            norm(LN_CONV)
            dve.wait_ge(x_ready, 8 * (LN_CONV + 2))
            residual(LN_CONV_OUT, CONV_OUT_N, 2, 1.0)
            norm(LN_CONV_OUT)
            ffn(3)

        @block.tensor
        def _(pe):
            def mm3(to, s, k, t, hi, lo, start, stop):
                w = slice(t * P, t * P + P)
                nc.tensor.matmul(to, whi[:, s, k, w], hi, start=start, stop=False)
                nc.tensor.matmul(to, whi[:, s, k, w], lo, start=False, stop=False)
                return nc.tensor.matmul(to, wlo[:, s, k, w], hi, start=False, stop=stop)

            def chunk(n, s, banks, ready=None):
                pe.wait_ge(lo_ready, n + 1)
                for k in range(DK):
                    if ready is not None:
                        pe.wait_ge(x_ready, ready + k + 1)
                    for t, b in enumerate(banks):
                        last = mm3(bank[b][:, :], s, k, t, xhi[:, k, :], xlo[:, k, :], k == 0, k == DK - 1)
                last.then_inc(w_used, 1)

            def ffn_pair(f, i):
                n = FFN_N[f] + 2 * i
                if not isinstance(i, int):
                    pe.wait_ge(silu_done, FK * f + 2 * i)
                chunk(n, 0, (0, 1), 8 * (LN_FFN[f] if f else 0) if isinstance(i, int) else None)
                if not isinstance(i, int):
                    pe.wait_ge(mul_done, FK * f + 2 * i)
                chunk(n + 1, 1, (2, 3))

            def product_pair(ln, n, p, kcs, rhs, ready):
                k0 = 0
                for c, kc in enumerate(kcs):
                    pe.wait_ge(lo_ready, n + c + 1)
                    if ready is not None:
                        ready(k0, kc)
                    for t in range(2):
                        if c == 0 and ready is None:
                            pe.wait_ge(y_evac, 8 * ln + 2 * p - 1 + t)
                        for k in range(k0, k0 + kc):
                            hi, lo = rhs(k)
                            last = mm3(bank[t][:, :], c % 2, k - k0, t, hi, lo, k == 0, k == k0 + kc - 1 and c == len(kcs) - 1)
                        if t == 1:
                            last.then_inc(w_used, 1)
                        elif c == len(kcs) - 1:
                            last.then_inc(y_even, 1)
                    k0 += kc

            def shift_sum(ln):
                pe.wait_ge(y_evac, 8 * ln + 1)
                nc.tensor.matmul(bank[4][:, :], ones[:, :], u[:, 0, :], start=True, stop=True).then_inc(shift_mm, 1)

            def stats(ln):
                pe.wait_ge(u_acc, 6 * ln + 6)
                nc.tensor.matmul(bank[5][:, :], ones[:, :], usum, start=True, stop=False)
                pe.wait_ge(q_acc, 6 * ln + 6)
                nc.tensor.matmul(bank[6][:, :], ones[:, :], qsum, start=True, stop=False)
                pe.wait_ge(y_evac, 8 * ln + 8)
                nc.tensor.matmul(bank[5][:, :], ones[:, :], u[:, DK - 1, :], start=False, stop=True).then_inc(stats_mm, 1)
                pe.wait_ge(sq_done, 8 * ln + 8)
                nc.tensor.matmul(bank[6][:, :], ones[:, :], sq[1], start=False, stop=True).then_inc(stats_mm, 1)

            def product(ln, n0, kcs, rhs, ready):
                product_pair(ln, n0, 0, kcs, rhs, ready)
                shift_sum(ln)
                with pe.Fori(1, 4) as p:
                    product_pair(ln, n0 + len(kcs) * p, p, kcs, rhs, None)
                stats(ln)

            def ffn(f):
                ffn_pair(f, 0)
                with pe.Fori(1, FK // 2) as i:
                    ffn_pair(f, i)

                def ready(k0, kc):
                    pe.wait_ge(h_done, FK * f + k0 + kc)
                    if k0 == 0:
                        pe.wait_ge(silu_done, FK * (f + 1))
                product(LN_FFN[f], FFN_N[f] + FK, DOWN_K, lambda k: (h_hi[:, k, :], h_lo[:, k, :]), ready)

            def attention(m):
                kv = kv_of[m]
                kt = kv[:, 0:1024].rearrange("p (h m) -> p h m", h=HEADS)
                v = kv[:, 1024:2048].rearrange("p (b e) -> p b e", b=MB)
                probs = pp_of[m][:, 0:1024].rearrange("p (b m) -> p b m", b=TB)
                probs_t = pp_of[m][:, 1024:2048].rearrange("p (b s) -> p b s", b=MB)
                pe.wait_ge(kv_loaded, 16 * (m + 1))

                def scores(h):
                    if h:
                        pe.wait_ge(p_exp, 4 * (HEADS * m + h))
                    for b in range(TB):
                        last = nc.tensor.matmul(bank[4 + b // 2][:, (b % 2) * 256:(b % 2) * 256 + 256],
                                                qm_of[m][:, h, b * P:(b + 1) * P], kt[:, h, :], start=True, stop=True)
                        if b % 2:
                            last.then_inc(scores_mm, 1)

                scores(0)
                for h in range(HEADS):
                    g = HEADS * m + h
                    if h + 1 < HEADS:
                        scores(h + 1)
                    pe.wait_ge(p_norm, 4 * g + 4)
                    if h:
                        pe.wait_ge(pt_evac, 2 * g)
                    for j in range(MB):
                        for b in range(TB):
                            last = nc.tensor.transpose(bank[6 + j][:, b * P:(b + 1) * P],
                                                       probs[:, b, j * P:(j + 1) * P], ident[:, :])
                        last.then_inc(pt_mm, 1)
                    pe.wait_ge(pt_evac, 2 * g + 2)
                    for j in range(MB):
                        last = nc.tensor.matmul(bank[h][:, :], v[:, j, h * P:(h + 1) * P], probs_t[:, j, :],
                                                start=(j == 0), stop=(j == MB - 1))
                    last.then_inc(mo_mm, 1)

            pe.wait_ge(consts, 3)
            pe.wait_ge(rows_loaded, 16 * 8)
            nc.tensor.transpose(bank[7][:, 0:ROWS], rows_in[:, :], ident[0:ROWS, 0:ROWS]).then_inc(tr_done, 1)
            for k in range(DK):
                last = nc.tensor.transpose(bank[6][:, k * WIDTH:(k + 1) * WIDTH], dw_in[:, k * P:(k + 1) * P],
                                           ident[0:WIDTH, 0:WIDTH])
            last.then_inc(tr_done, 1)
            pe.wait_ge(mem_loaded, 16)
            pe.wait_ge(tr_evac, 2)
            for k in range(DK):
                if k >= 4:
                    pe.wait_ge(mem_hi_ready, 2 * (k - 4) + 1)
                for b in range(MB):
                    last = nc.tensor.transpose(bank[4 + k % 4][:, b * P:(b + 1) * P], mem_in[:, b, k * P:(k + 1) * P], ident[:, :])
                last.then_inc(tr_done, 1)
            pe.wait_ge(x_loaded, 16)
            for k in range(DK):
                if k < 4:
                    pe.wait_ge(mem_hi_ready, 2 * (k + 4) + 1)
                else:
                    pe.wait_ge(tr_evac, 3 + k - 4)
                for b in range(TB):
                    last = nc.tensor.transpose(bank[4 + k % 4][:, b * P:(b + 1) * P], xin[:, b, k * P:(k + 1) * P], ident[:, :])
                last.then_inc(tr_done, 1)
            for n in range(8):
                pe.wait_ge(lo_ready, n + 1)
                if n == 0:
                    pe.wait_ge(mem_ready, DK)
                if n >= 2:
                    pe.wait_ge(kv_evac, 2 * (n - 1))
                for t in range(2):
                    for k in range(DK):
                        last = mm3(bank[2 * (n % 2) + t][:, 0:NMEM], n % 2, k, t, mem_hi[:, k, :], mem_lo[:, k, :], k == 0, k == DK - 1)
                last.then_inc(w_used, 1)
            pe.wait_ge(kv_evac, 16)
            pe.wait_ge(tr_evac, 10)
            for layer in range(DEPTH):
                for j in range(MB):
                    for h in range(HEADS):
                        last = nc.tensor.transpose(bank[4 + 2 * layer + j][:, h * P:(h + 1) * P],
                                                   kv_t[:, layer, 4 + h, j * P:(j + 1) * P], ident[:, :])
                    last.then_inc(kvv_done, 1)
            ffn(0)

            n0 = GLA_N
            base = 8 * (LN_FFN[0] + 1)
            chunk(n0, 0, (0,), base)
            chunk(n0 + 1, 1, (2,))
            pe.wait_ge(gla_evac, 1)
            pe.wait_ge(gate_w_loaded, 16)
            for h in range(HEADS):
                nc.tensor.matmul(bank[4 + h][:, :], w_gate2[:, h * P:(h + 1) * P], a_t, start=True, stop=True).then_inc(z_mm, 1)
            for i in range(4):
                pe.wait_ge(gla_evac, 1 if i == 0 else 4 * i)
                chunk(n0 + 2 + 2 * i, 0, (0, 1))
                pe.wait_ge(gla_evac, 2 if i == 0 else 4 * i + 2)
                chunk(n0 + 3 + 2 * i, 1, (2, 3))
            pe.wait_ge(gla_evac, 18)
            pe.wait_ge(gate_chain, 13)
            for e in range(8):
                if e >= 4:
                    pe.wait_ge(v_evac, e - 3)
                for b in range(TB):
                    last = nc.tensor.transpose(bank[4 + e % 4][:, b * P:(b + 1) * P], qkv[:, 8 + e, b * P:(b + 1) * P], ident[:, :])
                last.then_inc(vt_mm, 1)
            chunk(n0 + 10, 0, (0, 1))
            chunk(n0 + 11, 1, (2,))
            pe.wait_ge(v_evac, 8)
            pe.wait_ge(gla_evac, 21)
            attention(0)

            def keys_and_att(h):
                pe.wait_ge(prods, 4 * h + 4)
                if h:
                    pe.wait_ge(kdt_evac, h)
                for b in range(TB):
                    last = nc.tensor.transpose(bank[4][:, b * P:(b + 1) * P], qkv[:, 4 + h, b * P:(b + 1) * P], ident[:, :])
                last.then_inc(kdt_mm, 1)
                if h:
                    pe.wait_ge(att_evac, h)
                for b in range(TB):
                    tok = slice(b * P, (b + 1) * P)
                    last = nc.tensor.matmul(bank[5][:, tok], ke[:, h, tok], qkv[:, h, tok], start=True, stop=True)
                last.then_inc(att_mm, 1)

            def state_sums(h, chunks):
                if h or chunks[0]:
                    pe.wait_ge(state_done, 7 * h + chunks[0])
                for c in chunks:
                    rows = slice(64 * (c % 2), 64 * (c % 2) + 64)
                    last = nc.tensor.matmul(bank[6 + c % 2][:, (c // 2 % 2) * 256:(c // 2 % 2) * 256 + 256],
                                            bk[rows, h, (c // 2) * P:(c // 2 + 1) * P],
                                            v_tok[rows, c // 2, h * 256:(h + 1) * 256], start=True, stop=True)
                last.then_inc(ds_mm, 1)

            pe.wait_ge(p_exp, 16)
            pe.wait_ge(mo_done, 4)
            keys_and_att(0)
            for h in range(HEADS):
                pe.wait_ge(kdt_evac, h + 1)
                state_sums(h, range(4))
                if h + 1 < HEADS:
                    keys_and_att(h + 1)
                state_sums(h, range(4, 7))
                pe.wait_ge(att_evac, h + 1)
                for e in range(2):
                    to = bank[2 * (h % 2) + e]
                    if h >= 2:
                        pe.wait_ge(o_read, 4 * (h - 2) + 2 * e + 2)
                    cols = slice(h * 256 + e * P, h * 256 + (e + 1) * P)
                    for b in range(TB):
                        nc.tensor.matmul(to[:, b * P:(b + 1) * P], v_tok[:, b, cols], att[h % 2][:, b, :],
                                         start=(b == 0), stop=False, skip_group_check=True)
                    for c in range(1, NCH):
                        if e == 0:
                            pe.wait_ge(state_done, 7 * h + c)
                        tok = slice(c * CHUNK, (c + 1) * CHUNK)
                        last = nc.tensor.matmul(to[:, tok], states[:, h % 2, c - 1, e * P:(e + 1) * P], qkv[:, h, tok],
                                                start=False, stop=(c == NCH - 1), skip_group_check=True)
                    last.then_inc(o_mm, 1)
            for j in range(4):
                pe.wait_ge(o_read, 12 if j == 0 else 16) if j < 2 else pe.wait_ge(gla_evac, 21 + 2 * (j - 1))
                chunk(n0 + 12 + j, j % 2, (2 * (j % 2), 2 * (j % 2) + 1))
                if j == 0:
                    for h in range(HEADS):
                        pe.wait_ge(ss_done, h + 1)
                        nc.tensor.matmul(bank[4 + h][:, :], ones[:, :], ke[:, h, :], start=True, stop=True).then_inc(rms_mm, 1)

            def y_ready_for(k0, kc):
                pe.wait_ge(gla_evac, 29)
                pe.wait_ge(y_done, min(k0 + kc, 8))
                if k0:
                    pe.wait_ge(mo_done, 4)
            product(LN_GLA_OUT, GLA_OUT_N, PROJ_K,
                    lambda k: (y_hi[:, k, :], y_lo[:, k, :]) if k < 8 else (mo_hi_g[:, k - 8, :], mo_lo_g[:, k - 8, :]),
                    y_ready_for)
            ffn(1)
            ffn(2)

            n0 = CONV_N
            for i in range(4):
                if i:
                    pe.wait_ge(conv_evac, 4 * i - 2)
                chunk(n0 + 2 * i, 0, (0, 1), 8 * (LN_FFN[2] + 1) if i == 0 else None)
                if i:
                    pe.wait_ge(conv_evac, 4 * i)
                chunk(n0 + 2 * i + 1, 1, (2, 3))
            shift_sum(LN_CONV)
            pe.wait_ge(conv_evac, 14)
            chunk(n0 + 8, 0, (0, 1))
            pe.wait_ge(conv_evac, 16)
            chunk(n0 + 9, 1, (2, 3))
            pe.wait_ge(conv_evac, 20)
            pe.wait_ge(shift_ready, LN_CONV + 1)
            attention(1)
            stats(LN_CONV)

            def c_ready_for(k0, kc):
                pe.wait_ge(x_ready, 8 * (LN_CONV + 1) + min(k0 + kc, 8))
                pe.wait_ge(mo_done, 8)
            product(LN_CONV_OUT, CONV_OUT_N, PROJ_K,
                    lambda k: (c_hi[:, k, :], c_lo[:, k, :]) if k < 8 else (mo_hi_c[:, k - 8, :], mo_lo_c[:, k - 8, :]),
                    c_ready_for)
            ffn(3)
            for k in range(DK):
                pe.wait_ge(affine_done, 8 * LN_FFN[3] + k + 1)
                if k >= 4:
                    pe.wait_ge(fin_evac, k - 3)
                for b in range(TB):
                    last = nc.tensor.transpose(bank[k % 4][:, b * P:(b + 1) * P], u[:, k, b * P:(b + 1) * P], ident[:, :])
                last.then_inc(fin_mm, 1)


_INS = ["x", "mem", "ln_g", "ln_b", "ffn1_w_gu", "ffn1_w_down", "ffn2_w_gu", "ffn2_w_down", "mem_w_kv",
        "gla_w_in", "gla_w_gate2", "gla_b_gate", "gla_g_onorm", "gla_w_out",
        "conv_w_in", "conv_w_dw", "conv_b_dw", "conv_ln_g", "conv_ln_b", "conv_w_out"]


def kernel(**inputs):
    import numpy as _np
    import concourse.bacc as _bacc
    from concourse import mybir as _mybir
    from concourse.bass_utils import run_bass_kernel_spmd as _run

    nc = _bacc.Bacc("TRN2", target_bir_lowering=False, num_devices=1)
    arrays, aps = {}, {}
    for name in _INS:
        x = _np.ascontiguousarray(inputs[name])
        arrays[f"in_{name}_dram"] = x
        aps[name] = nc.dram_tensor(f"in_{name}_dram", x.shape, _mybir.dt.from_np(x.dtype), kind="ExternalInput").ap()
    out = nc.dram_tensor("out_0_dram", (1, SEQ, D), _mybir.dt.float32, kind="ExternalOutput").ap()
    build(nc, aps, out)
    r = _run(nc, [arrays], core_ids=[0])
    return r.results[0]["out_0_dram"]
```

```python
from contextlib import ExitStack

import concourse.bass as bass
from concourse import mybir

ALU = mybir.AluOpType
ACT = mybir.ActivationFunctionType
F32 = mybir.dt.float32
F32R = mybir.dt.float32r
I32 = mybir.dt.int32
AX_X = mybir.AxisListType.X

P = 128
SEQ = 512
D = 1024
DK = D // P
TB = SEQ // P
NMEM = 256
MB = NMEM // P
FF = 2816
FK = FF // P
HEADS = 4
DKH = 128
CHUNK = 64
NCH = SEQ // CHUNK
RANK = 16
WIDTH = 31
PAD = WIDTH - 1
DEPTH = 2
ALPHA = (2 * DEPTH) ** 0.25
LN_EPS = 1e-5
RMS_EPS = 1e-6
GATE_NORM = 16.0
MEM_SCALE = P ** -0.5
GLA_SCALE = DKH ** -0.5
OUT_K = 12

ROW_G, ROW_B = 0, DEPTH * 3 * DK
ROW_BDW = 2 * ROW_B
ROW_CG, ROW_CB = ROW_BDW + DK, ROW_BDW + 2 * DK
ROW_GATE = ROW_BDW + 3 * DK
ROW_ONORM = ROW_GATE + HEADS
ROWS = ROW_ONORM + 2

KV_N = 0
N_FFN = FK + 16
FFN_N = [8, 70, 108, 168]
GLA_N, GLA_OUT_N = 46, 62
CONV_N, CONV_OUT_N = 146, 160
DIAG_N = CONV_N + 10
N_CHUNKS = 206
DOWN_K = [6, 6, 6, 4]
A_K, B_K = 4, 8
PE_C = 6
TAPS_K = [8, 8, 8, 7]

LN_FFN = [0, 2, 3, 6]
LN_GLA_OUT, LN_CONV, LN_CONV_OUT = 1, 4, 5
LN_ROW = {0: 0, 1: 1, 2: 2, 3: 3, 5: 4, 6: 5}
EVEN_BASE = [0, 4, 8, 12, 16, 16, 20]
RES_BASE = [0, 8, 24, 32, 40, 40, 56]
RES_PER = {0: 1, 1: 2, 2: 1, 3: 1, 5: 2, 6: 1}


def build(nc, a, out):
    kv_dram = nc.dram_tensor("kv_scratch", (DEPTH, P, 2048), F32, kind="Internal").ap()
    with ExitStack() as ctx:
        def sem(name):
            return ctx.enter_context(nc.semaphore(name))

        def views(*specs):
            got = []
            with ExitStack() as part:
                for n, (name, shape, dt) in enumerate(specs):
                    got.append(part.enter_context(nc.sbuf_tensor(name, shape, dt)))
            return got

        def sb(name, shape, dt=F32):
            return ctx.enter_context(nc.sbuf_tensor(name, shape, dt))

        xhi = sb("xhi", [P, DK, SEQ], F32R)
        xlo = sb("xlo", [P, DK, SEQ], F32R)
        u = sb("u", [P, DK, SEQ])
        raw = sb("raw", [P, 2, 8, 256])
        whi = sb("whi", [P, 2, 8, 256], F32R)
        wlo = sb("wlo", [P, 2, 8, 256], F32R)
        scratch = sb("scratch", [P, 9, SEQ])
        usum, qsum, shift, delta, rstd = (scratch[:, i, :] for i in range(5))
        w_tap_hi = sb("w_tap_hi", [P, 2 * WIDTH], F32R)
        w_tap_lo = sb("w_tap_lo", [P, 2 * WIDTH], F32R)
        sq = [scratch[:, 5, :], scratch[:, 6, :]]
        act_out = [scratch[:, 7, :], scratch[:, 8, :]]
        diag_mean, diag_rstd = delta, rstd
        tiny = sb("tiny", [P, 72])
        mean_sq, sq_mean, var, rs = tiny[:, 0:8], tiny[:, 8:12], tiny[:, 12:16], tiny[:, 16:20]
        rms_v, rms_r, minus_half = tiny[:, 20:36], tiny[:, 36:52], tiny[:, 52:68]
        prm = sb("prm", [P, ROWS])
        w_dw = sb("w_dw", [P, DK * WIDTH])
        ident = sb("ident", [P, P])
        ones = sb("ones", [P, P])
        small = sb("small", [P, 16])
        row_max, neg_max, row_sum, inv_sum = (small[:, 4 * i:4 * i + 4] for i in range(4))
        exp_last = sb("exp_last", [P, HEADS, NCH])

        xin, mem_in, mem_hi, mem_lo, kv_t, kv_v, rows_in, dw_in = views(
            ("xin", [P, TB, D], F32), ("mem_in", [P, MB, D], F32),
            ("mem_hi", [P, DK, NMEM], F32R), ("mem_lo", [P, DK, NMEM], F32R),
            ("kv_t", [P, DEPTH, 8, NMEM], F32), ("kv_v", [P, DEPTH, MB, 512], F32),
            ("rows_in", [ROWS, P], F32), ("dw_in", [WIDTH, D], F32))
        h_hi, h_lo = views(("h_hi", [P, FK, SEQ], F32R), ("h_lo", [P, FK, SEQ], F32R))
        qkv, mo_hi_g, mo_lo_g, qm_g, bk, ke, v_tok = views(
            ("qkv", [P, 16, SEQ], F32), ("mo_hi_g", [P, HEADS, SEQ], F32R), ("mo_lo_g", [P, HEADS, SEQ], F32R),
            ("qm_g", [P, HEADS, SEQ], F32), ("bk", [P, HEADS, SEQ], F32), ("ke", [P, HEADS, SEQ], F32),
            ("v_tok", [P, TB, D], F32))
        _, states, att0 = views(
            ("q_k", [P, 8, SEQ], F32), ("states", [P, 2, 7, 256], F32), ("att0", [P, TB, P], F32))
        _, r_act, _, y_lo, y_hi = views(
            ("q_k2", [P, 8, SEQ], F32), ("r_act", [P, 8, SEQ], F32), ("mo_qm", [P, 12, SEQ], F32),
            ("y_lo", [P, 8, SEQ], F32R), ("y_hi", [P, 8, SEQ], F32R))
        conv_in, qm_c, mo_hi_c, mo_lo_c, kv_c, pp_c, c_lo, cin_hi, cin_lo = views(
            ("conv_in", [P, DK, PAD + SEQ], F32), ("qm_c", [P, HEADS, SEQ], F32),
            ("mo_hi_c", [P, HEADS, SEQ], F32R), ("mo_lo_c", [P, HEADS, SEQ], F32R),
            ("kv_c", [P, 2048], F32), ("pp_c", [P, 2048], F32), ("c_lo", [P, DK, SEQ], F32R),
            ("cin_hi", [P, 2, PAD + SEQ], F32R), ("cin_lo", [P, 2, PAD + SEQ], F32R))
        c_hi, = views(("c_hi", [P, DK, SEQ], F32R))
        out_tok, = views(("out_tok", [P, 4, TB, P], F32))

        Z_BANK = [4, 5, 6, 4]
        att_mask, reset, exp_a, exp_b, gate_t = usum, qsum, shift, delta, rstd
        att = [att0[:, :, :], sq[0].rearrange("p (b i) -> p b i", b=TB)]
        a_t = sq[1][0:RANK, :]
        w_gate2 = act_out[0][0:RANK, :]
        uflat = u[:, :, :].rearrange("p k s -> p (k s)")
        kv_of = [uflat[:, 0:2048], kv_c[:, :]]
        pp_of = [uflat[:, 2048:4096], pp_c[:, :]]
        qm_of = [qm_g, qm_c]
        mo_hi_of, mo_lo_of = [mo_hi_g, mo_hi_c], [mo_lo_g, mo_lo_c]

        bank = [ctx.enter_context(nc.psum_tensor(f"bank{i}", [P, SEQ], F32)) for i in range(8)]

        rows_loaded, mem_loaded, x_loaded, consts, gate_w_loaded = (
            sem(n) for n in ("rows_loaded", "mem_loaded", "x_loaded", "consts", "gate_w_loaded"))
        raw_loaded = [sem("raw_loaded0"), sem("raw_loaded1")]
        hi_ready, lo_ready, w_used = sem("hi_ready"), sem("lo_ready"), sem("w_used")
        tr_done, tr_evac = sem("tr_done"), sem("tr_evac")
        mem_hi_ready, mem_ready = sem("mem_hi_ready"), sem("mem_ready")
        kv_evac, kvv_done, kvv_evac, kv_stored, kv_loaded = (
            sem(n) for n in ("kv_evac", "kvv_done", "kvv_evac", "kv_stored", "kv_loaded"))
        silu_done, mul_done, h_hi_done, h_done = (
            sem(n) for n in ("silu_done", "mul_done", "h_hi_done", "h_done"))
        y_even, y_evac, res_done, u0_ready, u_acc, q_acc, sq_done = (
            sem(n) for n in ("y_even", "y_evac", "res_done", "u0_ready", "u_acc", "q_acc", "sq_done"))
        shift_mm, shift_ready, stats_mm, stat_step, var_ready, rs_ready, mean_diag, rstd_diag, bcast_mm = (
            sem(n) for n in ("shift_mm", "shift_ready", "stats_mm", "stat_step", "var_ready",
                             "rs_ready", "mean_diag", "rstd_diag", "bcast_mm"))
        centred, normed, affine_done, x_hi_ready, x_ready = (
            sem(n) for n in ("centred", "normed", "affine_done", "x_hi_ready", "x_ready"))
        gla_evac, z_mm, gate_act, gate_chain, vt_mm, v_evac, exps, prods = (
            sem(n) for n in ("gla_evac", "z_mm", "gate_act", "gate_chain", "vt_mm", "v_evac",
                             "exps", "prods"))
        scores_mm, max_done, neg_max_done, p_exp, inv_done, p_norm, pt_mm, pt_evac, mo_mm, mo_hi_done, mo_done = (
            sem(n) for n in ("scores_mm", "max_done", "neg_max_done", "p_exp", "inv_done", "p_norm",
                             "pt_mm", "pt_evac", "mo_mm", "mo_hi_done", "mo_done"))
        kdt_mm, kdt_evac, att_mm, att_evac, ds_mm, state_done, o_mm, o_read, ss_done = (
            sem(n) for n in ("kdt_mm", "kdt_evac", "att_mm", "att_evac", "ds_mm", "state_done",
                             "o_mm", "o_read", "ss_done"))
        reset_done, att_clear = sem("reset_done"), sem("att_clear")
        rms_mm, rms_var, rms_rs, rms_diag, rms_bcast, y_scaled, y_ready, y_hi_done, y_done, gla_masks = (
            sem(n) for n in ("rms_mm", "rms_var", "rms_rs", "rms_diag", "rms_bcast", "y_scaled",
                             "y_ready", "y_hi_done", "y_done", "gla_masks"))
        conv_evac, glu_done, taps_done, conv_pad, tap_split, cin_hi_done, cin_done = (
            sem(n) for n in ("conv_evac", "glu_done", "taps_done", "conv_pad", "tap_split",
                             "cin_hi_done", "cin_done"))
        fin_mm, fin_evac, out_stored = sem("fin_mm"), sem("fin_evac"), [sem(f"out_stored{i}") for i in range(4)]

        block = ctx.enter_context(nc.Block())

        @block.sync
        def _(sp):
            def load(n, s, src, free=None):
                if not isinstance(n, int) or n >= 2:
                    sp.wait_ge(lo_ready, n - 1 if free is None else free)
                sp.dma_start(raw[:, s, 0:src.shape[1], 0:src.shape[2]], src).then_inc(raw_loaded[s], 16)

            def cols(w, c0, width=256):
                return w[:, :, bass.ds(c0, width)]

            def ffn(f):
                layer, which = divmod(f, 2)
                w_gu = a["ffn1_w_gu" if which == 0 else "ffn2_w_gu"][layer].rearrange("(k p) n -> p k n", p=P)
                w_dn = a["ffn1_w_down" if which == 0 else "ffn2_w_down"][layer].rearrange("(k p) n -> p k n", p=P)
                n0 = FFN_N[f]
                with sp.Fori(0, FK // 2) as i:
                    load(n0 + 2 * i, 0, cols(w_gu, i * 256))
                    load(n0 + 2 * i + 1, 1, cols(w_gu, i * 256 + FF))
                n0 += FK
                with sp.Fori(0, 4) as p:
                    k = 0
                    for c, kc in enumerate(DOWN_K):
                        load(n0 + 4 * p + c, c % 2, cols(w_dn[:, k:k + kc, :], p * 256))
                        k += kc

            def out_proj(w, n0, free=None):
                w = w.rearrange("(k p) n -> p k n", p=P)
                wa, wb = w[:, B_K:B_K + A_K, :], w[:, 0:B_K, :]
                load(n0, 0, cols(wa, 0), free)
                load(n0 + 1, 1, cols(wa, 256), free)
                load(n0 + 2, 0, cols(wb, 0))
                load(n0 + 3, 1, cols(wb, 256))
                load(n0 + 4, 0, cols(wa, 512))
                load(n0 + 5, 1, cols(wa, 768))
                load(n0 + 6, 0, cols(wb, 512))
                load(n0 + 7, 1, cols(wb, 768))

            def load_parameters():
                r0 = 0
                for name, rows in (("ln_g", DEPTH * 3 * DK), ("ln_b", DEPTH * 3 * DK), ("conv_b_dw", DK),
                                   ("conv_ln_g", DK), ("conv_ln_b", DK), ("gla_b_gate", HEADS), ("gla_g_onorm", 2)):
                    src = a[name]
                    src = (src.rearrange("l w (k p) -> (l w k) p", p=P) if len(src.shape) == 3
                           else src.rearrange("l (k p) -> (l k) p", p=P))
                    sp.dma_start(rows_in[r0:r0 + rows, :], src).then_inc(rows_loaded, 16)
                    r0 += rows
                sp.dma_start(dw_in[:, :], a["conv_w_dw"][0]).then_inc(rows_loaded, 16)

            sp.dma_start(mem_in[:, :, :], a["mem"][0].rearrange("(b p) d -> p b d", p=P)).then_inc(mem_loaded, 16)
            for layer in range(DEPTH):
                w = a["mem_w_kv"][layer].rearrange("(k p) n -> p k n", p=P)
                for c in range(4):
                    n = KV_N + 4 * layer + c
                    load(n, n % 2, cols(w, c * 256))
                    if n == 1:
                        sp.dma_start(xin[:, :, :], a["x"][0].rearrange("(b p) d -> p b d", p=P)).then_inc(x_loaded, 16)
                        load_parameters()
            ffn(0)
            w = a["gla_w_in"][0].rearrange("(k p) n -> p k n", p=P)
            n = GLA_N
            load(n, 0, cols(w, 3072, P))
            load(n + 1, 1, cols(w, 3088, P))
            load(n + 2, 0, cols(w, 3216))
            load(n + 3, 1, cols(w, 3472, P))
            sp.wait_ge(x_ready, 8 * (LN_FFN[0] + 2))
            sp.wait_ge(kv_stored, 64)
            sp.dma_start(kv_of[0], kv_dram[0]).then_inc(kv_loaded, 16)
            with sp.Fori(0, 6) as i:
                load(n + 4 + 2 * i, 0, cols(w, i * 512))
                load(n + 5 + 2 * i, 1, cols(w, i * 512 + 256))
            out_proj(a["gla_w_out"][0], GLA_OUT_N)
            ffn(1)
            ffn(2)
            w = a["conv_w_in"][0].rearrange("(k p) n -> p k n", p=P)
            n = CONV_N
            with sp.Fori(0, 2) as i:
                load(n + 2 * i, 0, cols(w, i * 256))
                load(n + 2 * i + 1, 1, cols(w, i * 256 + D))
            load(n + 4, 0, cols(w, 2 * D))
            load(n + 5, 1, cols(w, 2 * D + 256))
            sp.wait_ge(x_ready, 8 * (LN_FFN[2] + 2))
            sp.dma_start(kv_of[1], kv_dram[1]).then_inc(kv_loaded, 16)
            with sp.Fori(0, 2) as i:
                load(n + 6 + 2 * i, 0, cols(w, i * 256 + 512))
                load(n + 7 + 2 * i, 1, cols(w, i * 256 + 512 + D))
            out_proj(a["conv_w_out"][0], CONV_OUT_N, free=DIAG_N)
            ffn(3)
            for k in range(DK):
                sp.wait_ge(fin_evac, k + 1)
                sp.dma_start(out[0].rearrange("(b p) d -> p b d", p=P)[:, :, k * P:(k + 1) * P],
                             out_tok[:, k % 4, :, :]).then_inc(out_stored[k % 4], 16)
            for i in range(4):
                sp.wait_ge(out_stored[i], 32)

        @block.gpsimd
        def _(pool):
            def split_lo(n, s, kc=8, width=256, after_dve=False):
                pool.wait_ge(hi_ready, n + 1)
                if after_dve:
                    pool.wait_ge(lo_ready, n)
                nc.gpsimd.tensor_tensor(wlo[:, s, 0:kc, 0:width], raw[:, s, 0:kc, 0:width],
                                        whi[:, s, 0:kc, 0:width].bitcast(F32), ALU.subtract).then_inc(lo_ready, 1)

            def lo_of_x(ln, lo, hi):
                if ln >= 0:
                    rsqrt(ln)
                for k in range(DK):
                    pool.wait_ge(x_hi_ready, 8 * (ln + 1) + k + 1)
                    nc.gpsimd.tensor_tensor(lo[:, k, :], u[:, k, :], hi[:, k, 0:SEQ].bitcast(F32),
                                            ALU.subtract).then_inc(x_ready, 1)

            def rsqrt(ln):
                pool.wait_ge(var_ready, ln + 1)
                nc.gpsimd.tensor_tensor(rs, var, minus_half[:, 0:TB], ALU.pow).then_inc(rs_ready, 1)

            def ffn(f):
                n0 = FFN_N[f]
                split_lo(n0 + 2, 0, after_dve=True)
                split_lo(n0 + 3, 1)
                with pool.Fori(1, FK // 2 - 1) as i:
                    split_lo(n0 + 2 * i + 2, 0)
                    split_lo(n0 + 2 * i + 3, 1)
                down(n0 + FK)

            def down(n0):
                split_lo(n0, 0, 6)
                split_lo(n0 + 1, 1, 6)
                with pool.Fori(0, 3) as p:
                    for c in range(4):
                        split_lo(n0 + 4 * p + 2 + c, c % 2, DOWN_K[(c + 2) % 4])
                split_lo(n0 + 14, 0, 6)
                split_lo(n0 + 15, 1, 4)

            nc.gpsimd.memset(ones[:, :], 1.0).then_inc(consts, 1)
            nc.gpsimd.memset(ident[:, :], 0.0).then_inc(consts, 1)
            pool.wait_ge(consts, 2)
            nc.gpsimd.affine_select(out=ident[:, :], in_=ident[:, :], compare_op=ALU.not_equal, fill=1.0,
                                    base=0, pattern=[[-1, P]], channel_multiplier=1).then_inc(consts, 1)
            nc.gpsimd.memset(minus_half, -0.5).then_inc(consts, 1)
            for k in range(DK):
                pool.wait_ge(mem_hi_ready, 2 * k + 2)
                nc.gpsimd.tensor_tensor(mem_lo[:, k, :], kv_t[:, 0, k, :],
                                        mem_hi[:, k, :].bitcast(F32), ALU.subtract).then_inc(mem_ready, 1)
            lo_of_x(-1, xlo, xhi)
            pool.wait_ge(tap_split, 1)
            nc.gpsimd.tensor_tensor(w_tap_lo[:, :], w_dw[:, PE_C * WIDTH:DK * WIDTH], w_tap_hi[:, :].bitcast(F32),
                                    ALU.subtract).then_inc(tap_split, 1)
            ffn(0)
            split_lo(GLA_N, 0, 8, P)
            lo_of_x(LN_FFN[0], xlo, xhi)
            nc.gpsimd.memset(att_mask, 1.0).then_inc(gla_masks, 1)
            pool.wait_ge(gla_masks, 1)
            m = att_mask.rearrange("p (b i) -> p b i", b=TB)
            nc.gpsimd.affine_select(out=m, in_=m, compare_op=ALU.is_ge, fill=0.0, base=0,
                                    pattern=[[0, TB], [1, P]], channel_multiplier=-1).then_inc(gla_masks, 1)
            pool.wait_ge(gla_masks, 2)
            nc.gpsimd.memset(m[0:CHUNK, :, CHUNK:P], 0.0).then_inc(gla_masks, 1)
            split_lo(GLA_N + 2, 0, after_dve=True)
            split_lo(GLA_N + 3, 1, 8, P)
            with pool.Fori(0, 5) as i:
                split_lo(GLA_N + 4 + 2 * i, 0)
                split_lo(GLA_N + 5 + 2 * i, 1)
            split_lo(GLA_N + 14, 0)
            pool.wait_ge(rms_var, 1)
            nc.gpsimd.tensor_tensor(rms_r, rms_v, minus_half, ALU.pow).then_inc(rms_rs, 1)
            split_lo(GLA_N + 15, 1)
            with pool.Fori(0, 2) as q:
                for c in range(4):
                    split_lo(GLA_OUT_N + 4 * q + c, c % 2, (A_K, A_K, B_K, B_K)[c])
            split_lo(FFN_N[1], 0)
            lo_of_x(LN_GLA_OUT, xlo, xhi)
            ffn(1)
            split_lo(FFN_N[2], 0)
            lo_of_x(LN_FFN[1], xlo, xhi)
            ffn(2)
            split_lo(CONV_N, 0)
            lo_of_x(LN_FFN[2], xlo, xhi)
            nc.gpsimd.memset(conv_in[:, :, 0:PAD], 0.0).then_inc(conv_pad, 1)

            def glu(i, c_evac):
                pool.wait_ge(conv_evac, c_evac)
                for t in range(2):
                    nc.gpsimd.tensor_tensor(conv_in[:, 2 * i + t, PAD:PAD + SEQ], conv_in[:, 2 * i + t, PAD:PAD + SEQ],
                                            act_out[t], ALU.mult).then_inc(glu_done, 1)

            n0 = CONV_N
            split_lo(n0 + 2, 0, after_dve=True)
            split_lo(n0 + 3, 1)
            glu(0, 4)
            split_lo(n0 + 4, 0)
            split_lo(n0 + 5, 1)
            glu(1, 8)
            split_lo(n0 + 6, 0)
            split_lo(n0 + 7, 1)
            split_lo(n0 + 8, 0)
            split_lo(n0 + 9, 1)
            glu(2, 16)

            def diag_lo(g):
                kc = TAPS_K[g]
                pool.wait_ge(hi_ready, DIAG_N + g + 1)
                taps = w_tap_lo[:, :].bitcast(F32).rearrange("p (t j) -> p j t", t=2)[:, 8 * g:8 * g + kc, :]
                for t in range(2):
                    last = nc.gpsimd.tensor_tensor(
                        wlo[:, g % 2, 0:kc, t * P:(t + 1) * P],
                        ident[:, :].rearrange("p (a c) -> p a c", a=1).to_broadcast([P, kc, P]),
                        taps[:, :, t:t + 1].to_broadcast([P, kc, P]), ALU.mult)
                last.then_inc(lo_ready, 1)

            diag_lo(0)
            glu(3, 20)
            for t in range(2):
                pool.wait_ge(cin_hi_done, t + 1)
                nc.gpsimd.tensor_tensor(cin_lo[:, t, :], conv_in[:, PE_C + t, :], cin_hi[:, t, :].bitcast(F32),
                                        ALU.subtract).then_inc(cin_done, 1)
            diag_lo(1)
            diag_lo(2)
            diag_lo(3)
            for c in range(4):
                split_lo(CONV_OUT_N + c, c % 2, (A_K, A_K, B_K, B_K)[c])
            lo_of_x(LN_CONV, c_lo, c_hi)
            for c in range(4):
                split_lo(CONV_OUT_N + 4 + c, c % 2, (A_K, A_K, B_K, B_K)[c])
            split_lo(FFN_N[3], 0)
            lo_of_x(LN_CONV_OUT, xlo, xhi)
            ffn(3)
            rsqrt(LN_FFN[3])

        @block.scalar
        def _(act):
            def split_hi(turn, s, kc=8, width=256, late=False):
                n = 2 * turn + s
                if isinstance(n, int) and n >= N_CHUNKS:
                    return
                if not isinstance(n, int) or n >= 2:
                    act.wait_ge(w_used, n - 1)
                loads = turn + 1 if not isinstance(turn, int) or n < DIAG_N else turn - 1
                if late:
                    loads = turn - 1
                act.wait_ge(raw_loaded[s], 16 * loads)
                nc.scalar.copy(whi[:, s, 0:kc, 0:width], raw[:, s, 0:kc, 0:width]).then_inc(hi_ready, 1)

            def ffn_pair(f, i, nxt):
                t0 = FFN_N[f] // 2
                act.wait_ge(w_used, FFN_N[f] + 2 * i + 1)
                split_hi(t0 + i + 1, 0, 8 if nxt else DOWN_K[0], late=f == 3)
                for t in range(2):
                    if not isinstance(i, int) or f + i > 0:
                        act.wait_ge(h_done, FK * f + 2 * i)
                    nc.scalar.activation(act_out[t], bank[t][:, :], ACT.Silu).then_inc(silu_done, 1)
                act.wait_ge(w_used, FFN_N[f] + 2 * i + 2)
                split_hi(t0 + i + 1, 1, 8 if nxt else DOWN_K[1], late=f == 3)
                if isinstance(i, int) and f + i == 0:
                    act.wait_ge(kv_stored, 64)
                for t in range(2):
                    act.wait_ge(mul_done, FK * f + 2 * i + t + 1)
                    nc.scalar.copy(h_hi[:, bass.ds(2 * i + t, 1), :], act_out[t].rearrange("p (a s) -> p a s", a=1)).then_inc(h_hi_done, 1)

            def squares(ln, p):
                for t in range(2):
                    d = 2 * p + t
                    if isinstance(p, int) and d == 0:
                        act.wait_ge(u0_ready, ln + 1)
                    else:
                        act.wait_ge(y_evac, 8 * ln + d + 1)
                    if not isinstance(p, int) or d >= 2:
                        act.wait_ge(q_acc, 6 * ln + d - 1 - t)
                    nc.scalar.activation(sq[t], u[:, bass.ds(d, 1), :].rearrange("p a s -> p (a s)"), ACT.Square).then_inc(sq_done, 1)

            def shift_copy(ln):
                act.wait_ge(shift_mm, ln + 1)
                nc.scalar.activation(shift, bank[4][:, :], ACT.Copy, scale=1.0 / P).then_inc(shift_ready, 1)

            def down_pair(f, p, last=False):
                t0 = (FFN_N[f] + FK) // 2 + 2 * p
                for c in range(3):
                    kc = 8 if last and c >= 2 else DOWN_K[(c + 2) % 4]
                    width = P if last and c == 2 and f in (0,) else 256
                    split_hi(t0 + 1 + c // 2, c % 2, kc, width, late=f == 3)
                if isinstance(p, int) and p == 0:
                    shift_copy(LN_FFN[f])
                squares(LN_FFN[f], p)
                split_hi(t0 + 2, 1, 8 if last else DOWN_K[1], P if last and f == 0 else 256, late=f == 3)

            def out_proj(ln, n0):
                for q in range(2):
                    t0 = n0 // 2 + 2 * q
                    if ln == LN_GLA_OUT or q:
                        split_hi(t0 + 1, 0, B_K)
                        split_hi(t0 + 1, 1, B_K)
                    if q == 0:
                        shift_copy(ln)
                    squares(ln, 2 * q)
                    split_hi(t0 + 2, 0, A_K if q == 0 else 8)
                    squares(ln, 2 * q + 1)
                    split_hi(t0 + 2, 1, A_K if q == 0 else 8)
                norm(ln)

            def affine(ln, hi, g_row, b_row, func=ACT.Identity):
                def one(k):
                    act.wait_ge(normed, 8 * ln + k + 1)
                    nc.scalar.activation(u[:, k, :], u[:, k, :], func, scale=prm[:, g_row + k:g_row + k + 1],
                                         bias=prm[:, b_row + k:b_row + k + 1]).then_inc(affine_done, 1)
                one(0)
                for k in range(DK):
                    if k + 1 < DK:
                        one(k + 1)
                    if hi is not None:
                        act.wait_ge(affine_done, 8 * ln + k + 1)
                        nc.scalar.copy(hi[:, k, 0:SEQ], u[:, k, :]).then_inc(x_hi_ready, 1)

            def norm(ln, hi=xhi):
                affine(ln, hi, ROW_G + LN_ROW[ln] * DK, ROW_B + LN_ROW[ln] * DK)

            def ffn(f):
                ffn_pair(f, 0, True)
                with act.Fori(1, FK // 2 - 1) as i:
                    ffn_pair(f, i, True)
                ffn_pair(f, FK // 2 - 1, False)
                down_pair(f, 0)
                with act.Fori(1, 3) as p:
                    down_pair(f, p)
                down_pair(f, 3, last=True)
                if f < 3:
                    norm(LN_FFN[f])

            def exps_of(m, h):
                g = HEADS * m + h
                probs = pp_of[m][:, 0:1024].rearrange("p (b m) -> p b m", b=TB)
                act.wait_ge(neg_max_done, g + 1)
                if g:
                    act.wait_ge(pt_mm, 2 * g)
                for b in range(TB):
                    nc.scalar.activation(probs[:, b, :], bank[4 + b // 2][:, (b % 2) * 256:(b % 2) * 256 + 256],
                                         ACT.Exp, scale=MEM_SCALE, bias=neg_max[:, b:b + 1],
                                         accum_out=row_sum[:, b:b + 1]).then_inc(p_exp, 1)

            def probs_back(m, h):
                g = HEADS * m + h
                probs_t = pp_of[m][:, 1024:2048].rearrange("p (b s) -> p b s", b=MB)
                act.wait_ge(pt_mm, 2 * g + 1)
                if g:
                    act.wait_ge(mo_mm, g)
                nc.scalar.copy(probs_t[:, 0, :], bank[6][:, :]).then_inc(pt_evac, 1)

            def mo_hi_copy(m, h):
                g = HEADS * m + h
                act.wait_ge(mo_mm, g + 1)
                nc.scalar.copy(mo_hi_of[m][:, h, :], bank[7][:, :]).then_inc(mo_hi_done, 1)

            split_hi(0, 0)
            split_hi(0, 1)
            for k in range(DK):
                act.wait_ge(tr_done, 1 + k)
                nc.scalar.copy(kv_t[:, 0, k, :], bank[4 + k % 4][:, 0:NMEM]).then_inc(mem_hi_ready, 1)
                act.wait_ge(mem_hi_ready, 2 * k + 1)
                nc.scalar.copy(mem_hi[:, k, :], kv_t[:, 0, k, :]).then_inc(mem_hi_ready, 1)
            for k in range(DK):
                act.wait_ge(tr_done, 1 + DK + k)
                nc.scalar.copy(u[:, k, :], bank[4 + k % 4][:, :]).then_inc(tr_evac, 1)
                act.wait_ge(tr_evac, 1 + k)
                nc.scalar.copy(xhi[:, k, :], u[:, k, :]).then_inc(x_hi_ready, 1)
            act.wait_ge(tr_done, 2 * DK + 1)
            nc.scalar.copy(prm[:, :], bank[4][:, 0:ROWS]).then_inc(tr_evac, 1)
            act.wait_ge(tr_done, 2 * DK + 2)
            nc.scalar.copy(w_dw[:, :], bank[5][:, 0:DK * WIDTH]).then_inc(tr_evac, 1)
            act.wait_ge(tr_evac, DK + 2)
            nc.scalar.copy(w_tap_hi[:, :], w_dw[:, PE_C * WIDTH:DK * WIDTH]).then_inc(tap_split, 1)
            for n in range(8):
                act.wait_ge(w_used, n + 1)
                split_hi(n // 2 + 1, n % 2)
                for t in range(2):
                    if n == 0 and t == 0:
                        act.wait_ge(mem_ready, DK)
                    nc.scalar.copy(kv_t[:, n // 4, 2 * (n % 4) + t, :], bank[2 * (n % 2) + t][:, 0:NMEM]).then_inc(kv_evac, 1)
            for j in range(4):
                act.wait_ge(kvv_done, j + 1)
                nc.scalar.copy(kv_v[:, j // 2, j % 2, :], bank[4 + j][:, :]).then_inc(kvv_evac, 1)
            act.wait_ge(kvv_evac, 4)
            for layer in range(DEPTH):
                act.dma_start(kv_dram[layer, :, 0:1024],
                              kv_t[:, layer, 0:4, :].rearrange("p h m -> p (h m)")).then_inc(kv_stored, 16)
                act.dma_start(kv_dram[layer, :, 1024:2048],
                              kv_v[:, layer, :, :].rearrange("p b e -> p (b e)")).then_inc(kv_stored, 16)
            ffn(0)

            t0, n0 = GLA_N // 2, GLA_N
            act.dma_start(w_gate2, a["gla_w_gate2"][0]).then_inc(gate_w_loaded, 16)

            def step(j, kc=8, width=256):
                act.wait_ge(w_used, GLA_N + j + 1)
                split_hi(t0 + (j + 2) // 2, j % 2, kc, width)

            def gate(h):
                act.wait_ge(z_mm, h + 1)
                act.wait_ge(gate_chain, 3 * h + 1)
                nc.scalar.activation(exp_a, bank[Z_BANK[h]][:, :], ACT.Abs,
                                     bias=prm[:, ROW_GATE + h:ROW_GATE + h + 1]).then_inc(gate_act, 1)
                act.wait_ge(gate_act, 3 * h + 1)
                nc.scalar.activation(exp_a, exp_a, ACT.Exp, scale=-1.0).then_inc(gate_act, 1)
                act.wait_ge(gate_act, 3 * h + 2)
                nc.scalar.activation(exp_a, exp_a, ACT.Ln, bias=1.0).then_inc(gate_act, 1)

            def decays(h):
                b_h = bk[:, h, :]
                if h:
                    act.wait_ge(prods, 4 * h)
                act.wait_ge(gate_chain, 3 * HEADS + 1)
                nc.scalar.activation(exp_a, b_h, ACT.Exp, scale=1.0 / GATE_NORM).then_inc(exps, 1)
                nc.scalar.activation(exp_b, b_h, ACT.Exp, scale=-1.0 / GATE_NORM).then_inc(exps, 1)
                nc.scalar.activation(exp_last[:, h, :], bk[:, h, CHUNK - 1:SEQ:CHUNK], ACT.Exp,
                                     scale=1.0 / GATE_NORM).then_inc(exps, 1)
                act.wait_ge(prods, 4 * h + 2)
                nc.scalar.activation(exp_a, gate_t, ACT.Exp, scale=1.0 / GATE_NORM).then_inc(exps, 1)

            def to_sbuf(dst, b):
                nc.scalar.copy(dst, bank[b][:, :]).then_inc(gla_evac, 1)

            step(0)
            nc.scalar.copy(a_t, bank[0][0:RANK, :]).then_inc(gla_evac, 1)
            step(1, 8, P)
            to_sbuf(qm_g[:, 0, :], 2)
            gate(0)
            step(2)
            to_sbuf(qm_g[:, 1, :], 0)
            to_sbuf(qm_g[:, 2, :], 1)
            gate(1)
            step(3)
            to_sbuf(qm_g[:, 3, :], 2)
            gate(2)
            exps_of(0, 0)
            for j in range(8):
                step(4 + j)
                for t in range(2):
                    to_sbuf(qkv[:, 2 * j + t, :], 2 * (j % 2) + t)
                h = j // 2
                if j % 2 == 0:
                    probs_back(0, h)
                    if j == 0:
                        gate(3)
                else:
                    mo_hi_copy(0, h)
                    if h + 1 < HEADS:
                        exps_of(0, h + 1)
                if j >= 3 and j < 7:
                    decays(j - 3)
            for e in range(8):
                act.wait_ge(vt_mm, e + 1)
                nc.scalar.copy(v_tok[:, :, e * P:(e + 1) * P],
                               bank[4 + e % 4][:, :].rearrange("p (b e) -> p b e", b=TB)).then_inc(v_evac, 1)

            def kd_evac(h):
                act.wait_ge(kdt_mm, h + 1)
                nc.scalar.copy(bk[:, h, :], bank[4][:, :]).then_inc(kdt_evac, 1)

            kd_evac(0)
            for h in range(HEADS):
                if h + 1 < HEADS:
                    kd_evac(h + 1)
                for e, tmp in ((0, exp_a), (1, exp_b)):
                    b = bank[2 * (h % 2) + e][:, :]
                    act.wait_ge(o_mm, 2 * h + e + 1)
                    nc.scalar.copy(u[:, 2 * h + e, :], b).then_inc(o_read, 1)
                    if h:
                        act.wait_ge(ss_done, h)
                    nc.scalar.activation(tmp, b, ACT.Square).then_inc(o_read, 1)
            for j in range(4):
                step(12 + j, 8 if j < 2 else A_K)
                for t in range(2):
                    nc.scalar.activation(r_act[:, 2 * j + t, :], bank[2 * (j % 2) + t][:, :], ACT.Silu).then_inc(gla_evac, 1)
                for k in (range(0, 4) if j == 2 else range(4, 8) if j == 3 else ()):
                    act.wait_ge(y_ready, k + 1)
                    nc.scalar.copy(y_hi[:, k, :], u[:, k, :]).then_inc(y_hi_done, 1)
            out_proj(LN_GLA_OUT, GLA_OUT_N)
            ffn(1)
            ffn(2)

            t0 = CONV_N // 2

            def conv_step(j, kc=8):
                act.wait_ge(w_used, CONV_N + j + 1)
                split_hi(t0 + (j + 2) // 2, j % 2, kc)

            def diag_hi(g):
                act.wait_ge(w_used, DIAG_N + g - 1)
                for j in range(TAPS_K[g]):
                    for t in range(2):
                        w = w_tap_hi[:, t * WIDTH + 8 * g + j:t * WIDTH + 8 * g + j + 1].bitcast(F32)
                        last = nc.scalar.activation(whi[:, g % 2, j, t * P:(t + 1) * P], ident[:, :], ACT.Copy, scale=w)
                last.then_inc(hi_ready, 1)

            def a_copies(i):
                for t in range(2):
                    nc.scalar.copy(conv_in[:, 2 * i + t, PAD:PAD + SEQ], bank[t][:, :]).then_inc(conv_evac, 1)

            def sigmoids(i):
                if i:
                    act.wait_ge(glu_done, 2 * i)
                for t in range(2):
                    nc.scalar.activation(act_out[t], bank[2 + t][:, :], ACT.Sigmoid).then_inc(conv_evac, 1)

            for i in range(2):
                conv_step(2 * i)
                a_copies(i)
                conv_step(2 * i + 1)
                sigmoids(i)
            for c in range(2):
                conv_step(4 + c)
                for t in range(2):
                    nc.scalar.copy(qm_c[:, 2 * c + t, :], bank[2 * c + t][:, :]).then_inc(conv_evac, 1)
            shift_copy(LN_CONV)
            exps_of(1, 0)
            conv_step(6)
            a_copies(2)
            probs_back(1, 0)
            conv_step(7)
            sigmoids(2)
            mo_hi_copy(1, 0)
            exps_of(1, 1)
            diag_hi(0)
            a_copies(3)
            probs_back(1, 1)
            diag_hi(1)
            sigmoids(3)
            mo_hi_copy(1, 1)
            for t in range(2):
                act.wait_ge(glu_done, PE_C + t + 1)
                nc.scalar.copy(cin_hi[:, t, :], conv_in[:, PE_C + t, :]).then_inc(cin_hi_done, 1)
            exps_of(1, 2)
            squares(LN_CONV, 0)
            diag_hi(2)
            probs_back(1, 2)
            squares(LN_CONV, 1)
            diag_hi(3)
            mo_hi_copy(1, 2)
            exps_of(1, 3)
            split_hi(CONV_OUT_N // 2, 0, A_K)
            probs_back(1, 3)
            split_hi(CONV_OUT_N // 2, 1, A_K)
            for t in range(2):
                c = PE_C + t
                nc.scalar.activation(u[:, c, :], bank[2 + t][:, :], ACT.Identity,
                                     bias=prm[:, ROW_BDW + c:ROW_BDW + c + 1]).then_inc(conv_evac, 1)
            mo_hi_copy(1, 3)
            squares(LN_CONV, 2)
            squares(LN_CONV, 3)
            split_hi(CONV_OUT_N // 2 + 1, 0, B_K)
            split_hi(CONV_OUT_N // 2 + 1, 1, B_K)
            affine(LN_CONV, c_hi, ROW_CG, ROW_CB, ACT.Silu)
            out_proj(LN_CONV_OUT, CONV_OUT_N)
            ffn(3)
            ln = LN_FFN[3]
            for k in range(DK + 1):
                if k < DK:
                    g, b = ROW_G + LN_ROW[ln] * DK + k, ROW_B + LN_ROW[ln] * DK + k
                    act.wait_ge(normed, 8 * ln + k + 1)
                    nc.scalar.activation(u[:, k, :], u[:, k, :], ACT.Identity, scale=prm[:, g:g + 1],
                                         bias=prm[:, b:b + 1]).then_inc(affine_done, 1)
                if k:
                    j = k - 1
                    act.wait_ge(fin_mm, j + 1)
                    if j >= 4:
                        act.wait_ge(out_stored[j % 4], 16)
                    nc.scalar.copy(out_tok[:, j % 4, :, :],
                                   bank[j % 4][:, :].rearrange("p (b e) -> p b e", b=TB)).then_inc(fin_evac, 1)

        @block.vector
        def _(dve):
            def split_lo(n, s, kc=8, width=256):
                dve.wait_ge(hi_ready, n + 1)
                if n:
                    dve.wait_ge(lo_ready, n)
                nc.vector.tensor_tensor(wlo[:, s, 0:kc, 0:width], raw[:, s, 0:kc, 0:width],
                                        whi[:, s, 0:kc, 0:width].bitcast(F32), ALU.subtract).then_inc(lo_ready, 1)

            def ffn_pair(f, i):
                for t in range(2):
                    dve.wait_ge(w_used, FFN_N[f] + 2 * i + 2)
                    dve.wait_ge(silu_done, FK * f + 2 * i + t + 1)
                    nc.vector.tensor_tensor(act_out[t], act_out[t], bank[2 + t][:, :], ALU.mult).then_inc(mul_done, 1)
                for t in range(2):
                    dve.wait_ge(h_hi_done, FK * f + 2 * i + t + 1)
                    nc.vector.tensor_tensor(h_lo[:, bass.ds(2 * i + t, 1), :], act_out[t].rearrange("p (a s) -> p a s", a=1),
                                            h_hi[:, bass.ds(2 * i + t, 1), :].bitcast(F32),
                                            ALU.subtract).then_inc(h_done, 1)

            def blk(x, d):
                return x[:, bass.ds(d, 1), :].rearrange("p a s -> p (a s)")

            def add_sum(ln, d):
                dve.wait_ge(y_evac, 8 * ln + d + 1)
                if isinstance(d, int) and d == 1:
                    dve.wait_ge(u0_ready, ln + 1)
                    nc.vector.tensor_tensor(usum, u[:, 0, :], u[:, 1, :], ALU.add).then_inc(u_acc, 1)
                else:
                    dve.wait_ge(u_acc, 6 * ln + d - 1)
                    nc.vector.tensor_tensor(usum, usum, blk(u, d), ALU.add).then_inc(u_acc, 1)

            def add_square(ln, d, t):
                dve.wait_ge(sq_done, 8 * ln + d + 1)
                if isinstance(d, int) and d == 1:
                    nc.vector.tensor_tensor(qsum, sq[0], sq[1], ALU.add).then_inc(q_acc, 1)
                else:
                    dve.wait_ge(q_acc, 6 * ln + d - 1)
                    nc.vector.tensor_tensor(qsum, qsum, sq[t], ALU.add).then_inc(q_acc, 1)

            def take_shift(ln):
                dve.wait_ge(y_evac, 8 * ln + 1)
                dve.wait_ge(shift_ready, ln + 1)
                nc.vector.tensor_tensor(u[:, 0, :], u[:, 0, :], shift, ALU.subtract).then_inc(u0_ready, 1)

            def residual_pair(ln, p, n_used, coef, b0=0, last=False):
                for t in range(2):
                    d = 2 * p + t
                    first = isinstance(d, int) and d == 0
                    if t == 1 and not (isinstance(p, int) and p == 0):
                        add_square(ln, d - 1, 0)
                    res = RES_BASE[ln] + RES_PER[ln] * d
                    src = u if RES_PER[ln] == 1 else xlo[:, :, :].bitcast(F32)
                    if first:
                        nc.vector.tensor_scalar(u[:, 0, :], src[:, 0, :], ALPHA, None, ALU.mult).then_inc(res_done, 1)
                    else:
                        nc.vector.scalar_tensor_tensor(out=blk(u, d), in0=blk(src, d), scalar=ALPHA, in1=shift,
                                                       op0=ALU.mult, op1=ALU.subtract).then_inc(res_done, 1)
                    dve.wait_ge(res_done, res + 1)
                    if RES_PER[ln] == 2:
                        nc.vector.scalar_tensor_tensor(out=blk(u, d), in0=blk(xhi[:, :, :].bitcast(F32), d), scalar=ALPHA,
                                                       in1=blk(u, d), op0=ALU.mult, op1=ALU.add).then_inc(res_done, 1)
                        dve.wait_ge(res_done, res + 2)
                    if t == 0:
                        dve.wait_ge(y_even, EVEN_BASE[ln] + p + 1)
                    else:
                        dve.wait_ge(w_used, n_used)
                    nc.vector.scalar_tensor_tensor(out=blk(u, d), in0=bank[b0 + t][:, :], scalar=coef, in1=blk(u, d),
                                                   op0=ALU.mult, op1=ALU.add).then_inc(y_evac, 1)
                    if first:
                        take_shift(ln)
                    elif not (last and t == 1):
                        add_sum(ln, d)
                if not last:
                    add_square(ln, 2 * p + 1, 1)

            def residual_ffn(ln, n0):
                residual_pair(ln, 0, n0 + 4, 0.5)
                with dve.Fori(1, 3) as p:
                    residual_pair(ln, p, n0 + 4 * p + 4, 0.5)
                residual_pair(ln, 3, n0 + 16, 0.5, last=True)

            def residual_out(ln, n0):
                for p in range(4):
                    residual_pair(ln, p, n0 + 4 * (p // 2) + 3 + p % 2, 1.0, b0=2 * (p % 2), last=p == 3)

            def diagonals(to, values, done):
                for b in range(TB):
                    last = nc.vector.tensor_scalar(to[:, b * P:(b + 1) * P], ident[:, :], values[:, b:b + 1], None, ALU.mult)
                last.then_inc(done, 1)

            def norm(ln):
                dve.wait_ge(stats_mm, ln + 1)
                nc.vector.tensor_scalar(mean_sq, bank[5][:, 0:8], 1.0 / D, None, ALU.mult).then_inc(stat_step, 1)
                dve.wait_ge(stat_step, 3 * ln + 1)
                nc.vector.tensor_tensor(sq_mean, mean_sq[:, 0:TB], mean_sq[:, 0:TB], ALU.mult).then_inc(stat_step, 1)
                dve.wait_ge(stat_step, 3 * ln + 2)
                nc.vector.tensor_tensor(var, mean_sq[:, TB:2 * TB], sq_mean, ALU.subtract).then_inc(stat_step, 1)
                dve.wait_ge(stat_step, 3 * ln + 3)
                nc.vector.tensor_scalar(var, var, 0.0, LN_EPS, ALU.max, ALU.add).then_inc(var_ready, 1)
                diagonals(diag_mean, mean_sq, mean_diag)
                dve.wait_ge(rs_ready, ln + 1)
                diagonals(diag_rstd, rs, rstd_diag)

                def centre(k):
                    nc.vector.tensor_tensor(u[:, k, :], u[:, k, :], bank[6][:, :], ALU.subtract).then_inc(centred, 1)

                def scale(k):
                    dve.wait_ge(centred, 8 * ln + k + 1)
                    nc.vector.tensor_tensor(u[:, k, :], u[:, k, :], bank[7][:, :], ALU.mult).then_inc(normed, 1)

                dve.wait_ge(bcast_mm, 2 * ln + 1)
                centre(0)
                centre(1)
                dve.wait_ge(bcast_mm, 2 * ln + 2)
                for k in range(DK):
                    scale(k)
                    if k + 2 < DK:
                        centre(k + 2)

            def ffn(f):
                ffn_pair(f, 0)
                with dve.Fori(1, FK // 2) as i:
                    ffn_pair(f, i)
                residual_ffn(LN_FFN[f], FFN_N[f] + FK)
                norm(LN_FFN[f])

            def maxima(m, h):
                g = HEADS * m + h
                for j in range(2):
                    dve.wait_ge(scores_mm, 2 * g + j + 1)
                    nc.vector.tensor_reduce(row_max[:, 2 * j:2 * j + 2],
                                            bank[4 + j][:, :].rearrange("p (b m) -> p b m", b=2),
                                            AX_X, ALU.max).then_inc(max_done, 1)
                dve.wait_ge(max_done, 2 * g + 2)
                nc.vector.tensor_scalar(neg_max, row_max, -MEM_SCALE, None, ALU.mult).then_inc(neg_max_done, 1)

            def normalise(m, h):
                g = HEADS * m + h
                probs = pp_of[m][:, 0:1024].rearrange("p (b m) -> p b m", b=TB)
                dve.wait_ge(p_exp, 4 * g + 4)
                nc.vector.reciprocal(inv_sum, row_sum).then_inc(inv_done, 1)
                dve.wait_ge(inv_done, g + 1)
                for b in range(TB):
                    nc.vector.tensor_scalar(probs[:, b, :], probs[:, b, :], inv_sum[:, b:b + 1], None,
                                            ALU.mult).then_inc(p_norm, 1)

            def probs_back(m, h):
                g = HEADS * m + h
                probs_t = pp_of[m][:, 1024:2048].rearrange("p (b s) -> p b s", b=MB)
                dve.wait_ge(pt_mm, 2 * g + 2)
                if g:
                    dve.wait_ge(mo_mm, g)
                nc.vector.tensor_copy(probs_t[:, 1, :], bank[7][:, :]).then_inc(pt_evac, 1)

            def mo_lo_part(m, h):
                dve.wait_ge(mo_hi_done, HEADS * m + h + 1)
                nc.vector.tensor_tensor(mo_lo_of[m][:, h, :], bank[7][:, :], mo_hi_of[m][:, h, :].bitcast(F32),
                                        ALU.subtract).then_inc(mo_done, 1)

            for n in range(10):
                split_lo(n, n % 2)
            ffn(0)
            split_lo(GLA_N + 1, 1, 8, P)

            dve.wait_ge(x_ready, 8 * (LN_FFN[0] + 2))
            nc.vector.memset(reset, 1.0).then_inc(reset_done, 1)
            dve.wait_ge(reset_done, 1)
            nc.vector.memset(reset[:, 0:SEQ:CHUNK], 0.0).then_inc(gate_chain, 1)

            def gate(h):
                dve.wait_ge(gate_act, 3 * h + 3)
                nc.vector.tensor_scalar(gate_t, bank[Z_BANK[h]][:, :], prm[:, ROW_GATE + h:ROW_GATE + h + 1], 0.0,
                                        ALU.add, ALU.min).then_inc(gate_chain, 1)
                dve.wait_ge(gate_chain, 3 * h + 2)
                nc.vector.tensor_tensor(gate_t, gate_t, exp_a, ALU.subtract).then_inc(gate_chain, 1)
                dve.wait_ge(gate_chain, 3 * h + 3)
                nc.vector.tensor_tensor_scan(bk[:, h, :], reset, gate_t, 0.0, ALU.mult, ALU.add).then_inc(gate_chain, 1)

            def decayed(h):
                dve.wait_ge(gate_chain, 3 * HEADS + 1)
                if h == 0:
                    dve.wait_ge(gla_evac, 5 + 8)
                else:
                    dve.wait_ge(exps, 4 * h)
                b_h = bk[:, h, :].rearrange("p (c s) -> p c s", s=CHUNK)
                nc.vector.tensor_tensor(gate_t.rearrange("p (c s) -> p c s", s=CHUNK),
                                        b_h[:, :, CHUNK - 1:CHUNK].to_broadcast([P, NCH, CHUNK]), b_h,
                                        ALU.subtract).then_inc(prods, 1)
                dve.wait_ge(exps, 4 * h + 1)
                nc.vector.scalar_tensor_tensor(out=qkv[:, h, :], in0=qkv[:, h, :], scalar=GLA_SCALE, in1=exp_a,
                                               op0=ALU.mult, op1=ALU.mult).then_inc(prods, 1)
                dve.wait_ge(exps, 4 * h + 2)
                nc.vector.tensor_tensor(ke[:, h, :], qkv[:, 4 + h, :], exp_b, ALU.mult).then_inc(prods, 1)
                dve.wait_ge(exps, 4 * h + 4)
                nc.vector.tensor_tensor(qkv[:, 4 + h, :], qkv[:, 4 + h, :], exp_a, ALU.mult).then_inc(prods, 1)

            gate(0)
            gate(1)
            gate(2)
            maxima(0, 0)
            normalise(0, 0)
            probs_back(0, 0)
            gate(3)
            mo_lo_part(0, 0)
            maxima(0, 1)
            normalise(0, 1)
            probs_back(0, 1)
            mo_lo_part(0, 1)
            maxima(0, 2)
            normalise(0, 2)
            decayed(0)
            probs_back(0, 2)
            decayed(1)
            mo_lo_part(0, 2)
            maxima(0, 3)
            normalise(0, 3)
            decayed(2)
            probs_back(0, 3)
            decayed(3)
            mo_lo_part(0, 3)
            dve.wait_ge(gla_masks, 3)
            dve.wait_ge(vt_mm, 8)
            for t in range(2):
                nc.vector.memset(att[t], 0.0).then_inc(att_clear, 1)
            dve.wait_ge(att_clear, 2)

            def mask_att(h):
                dve.wait_ge(att_mm, h + 1)
                if h >= 2:
                    dve.wait_ge(o_mm, 2 * (h - 1))
                nc.vector.copy_predicated(att[h % 2], att_mask.rearrange("p (b i) -> p b i", b=TB).bitcast(I32),
                                          bank[5][:, :].rearrange("p (b i) -> p b i", b=TB)).then_inc(att_evac, 1)

            mask_att(0)
            for h in range(HEADS):
                s_h = states[:, h % 2, :, :]
                for c in range(7):
                    dve.wait_ge(ds_mm, 2 * h + c // 4 + 1)
                    if h >= 2 and c == 0:
                        dve.wait_ge(o_mm, 2 * (h - 1))
                    add = bank[6 + c % 2][:, (c // 2 % 2) * 256:(c // 2 % 2) * 256 + 256]
                    if c == 0:
                        nc.vector.tensor_copy(s_h[:, 0, :], add).then_inc(state_done, 1)
                    else:
                        dve.wait_ge(state_done, 7 * h + c)
                        nc.vector.scalar_tensor_tensor(out=s_h[:, c, :], in0=s_h[:, c - 1, :],
                                                       scalar=exp_last[:, h, c:c + 1], in1=add,
                                                       op0=ALU.mult, op1=ALU.add).then_inc(state_done, 1)
                if h + 1 < HEADS:
                    mask_att(h + 1)
                dve.wait_ge(o_read, 4 * h + 4)
                nc.vector.tensor_tensor(ke[:, h, :], exp_a, exp_b, ALU.add).then_inc(ss_done, 1)
            dve.wait_ge(rms_mm, 1)
            nc.vector.tensor_scalar(rms_v, bank[4][:, 0:16], 1.0 / 256, RMS_EPS, ALU.mult, ALU.add).then_inc(rms_var, 1)
            dve.wait_ge(rms_rs, 1)
            for h in range(HEADS):
                diagonals(ke[:, h, :], rms_r[:, TB * h:TB * h + TB], rms_diag)
            for h in range(HEADS):
                dve.wait_ge(rms_bcast, h + 1)
                for k in (2 * h, 2 * h + 1):
                    g = ROW_ONORM + k % 2
                    nc.vector.scalar_tensor_tensor(out=u[:, k, :], in0=u[:, k, :], scalar=prm[:, g:g + 1],
                                                   in1=bank[4 + h][:, :], op0=ALU.mult, op1=ALU.mult).then_inc(y_scaled, 1)
                for k in (2 * h, 2 * h + 1):
                    dve.wait_ge(y_scaled, k + 1)
                    dve.wait_ge(gla_evac, 21 + k + 1)
                    nc.vector.tensor_tensor(u[:, k, :], u[:, k, :], r_act[:, k, :], ALU.mult).then_inc(y_ready, 1)
                for k in (2 * h, 2 * h + 1):
                    dve.wait_ge(y_hi_done, k + 1)
                    nc.vector.tensor_tensor(y_lo[:, k, :], u[:, k, :], y_hi[:, k, :].bitcast(F32),
                                            ALU.subtract).then_inc(y_done, 1)
            residual_out(LN_GLA_OUT, GLA_OUT_N)
            norm(LN_GLA_OUT)
            split_lo(FFN_N[1] + 1, 1)
            ffn(1)
            split_lo(FFN_N[2] + 1, 1)
            ffn(2)
            split_lo(CONV_N + 1, 1)

            def taps(i, between):
                dve.wait_ge(glu_done, 2 * i + 2)
                for j in range(WIDTH):
                    for t in range(2):
                        c = 2 * i + t
                        src = conv_in[:, c, j:j + SEQ]
                        w = w_dw[:, c * WIDTH + j:c * WIDTH + j + 1]
                        if j == 0:
                            nc.vector.tensor_scalar(u[:, c, :], src, w, prm[:, ROW_BDW + c:ROW_BDW + c + 1],
                                                    ALU.mult, ALU.add).then_inc(taps_done, 1)
                        else:
                            dve.wait_ge(taps_done, 2 * WIDTH * i + 2 * (j - 1) + t + 1)
                            nc.vector.scalar_tensor_tensor(out=u[:, c, :], in0=src, scalar=w, in1=u[:, c, :],
                                                           op0=ALU.mult, op1=ALU.add).then_inc(taps_done, 1)
                    for step, *which in between.get(j, ()):
                        step(*which)

            def take_out_shift(i):
                for t in range(2):
                    d = 2 * i + t
                    if d == 0:
                        take_shift(LN_CONV)
                        continue
                    nc.vector.tensor_tensor(u[:, d, :], u[:, d, :], shift, ALU.subtract).then_inc(y_evac, 1)
                    if d < DK - 1:
                        add_sum(LN_CONV, d)

            def add_squares(i):
                if i:
                    add_square(LN_CONV, 2 * i, 0)
                if i < 3:
                    add_square(LN_CONV, 2 * i + 1, 1)

            dve.wait_ge(x_ready, 8 * (LN_FFN[2] + 2))
            dve.wait_ge(conv_pad, 1)
            taps(0, {})
            dve.wait_ge(taps_done, 2 * WIDTH)
            dve.sem_inc(y_evac, 1)
            taps(1, {4: [(maxima, 1, 0)], 7: [(normalise, 1, 0)], 13: [(probs_back, 1, 0)],
                     22: [(mo_lo_part, 1, 0), (maxima, 1, 1)], 25: [(normalise, 1, 1)], 30: [(probs_back, 1, 1)]})
            dve.wait_ge(taps_done, 4 * WIDTH)
            take_out_shift(0)
            take_out_shift(1)
            taps(2, {1: [(mo_lo_part, 1, 1), (maxima, 1, 2)], 4: [(normalise, 1, 2)],
                     9: [(probs_back, 1, 2), (add_squares, 0)], 17: [(add_squares, 1), (mo_lo_part, 1, 2), (maxima, 1, 3)],
                     20: [(normalise, 1, 3)], 27: [(probs_back, 1, 3)]})
            dve.wait_ge(taps_done, 6 * WIDTH)
            take_out_shift(2)
            mo_lo_part(1, 3)
            dve.wait_ge(conv_evac, 22)
            take_out_shift(3)
            add_squares(2)
            add_squares(3)
            norm(LN_CONV)
            dve.wait_ge(x_ready, 8 * (LN_CONV + 2))
            residual_out(LN_CONV_OUT, CONV_OUT_N)
            norm(LN_CONV_OUT)
            split_lo(FFN_N[3] + 1, 1)
            ffn(3)

        @block.tensor
        def _(pe):
            def mm3(to, s, k, t, hi, lo, start, stop):
                w = slice(t * P, t * P + P)
                nc.tensor.matmul(to, whi[:, s, k, w], hi, start=start, stop=False)
                nc.tensor.matmul(to, whi[:, s, k, w], lo, start=False, stop=False)
                return nc.tensor.matmul(to, wlo[:, s, k, w], hi, start=False, stop=stop)

            def chunk(n, s, banks, ready=None):
                pe.wait_ge(lo_ready, n + 1)
                for k in range(DK):
                    if ready is not None:
                        pe.wait_ge(x_ready, ready + k + 1)
                    for t, b in enumerate(banks):
                        last = mm3(bank[b][:, :], s, k, t, xhi[:, k, :], xlo[:, k, :], k == 0, k == DK - 1)
                last.then_inc(w_used, 1)

            def ffn_pair(f, i):
                n = FFN_N[f] + 2 * i
                if not isinstance(i, int):
                    pe.wait_ge(silu_done, FK * f + 2 * i)
                chunk(n, 0, (0, 1), 8 * (LN_FFN[f] if f else 0) if isinstance(i, int) else None)
                if not isinstance(i, int):
                    pe.wait_ge(mul_done, FK * f + 2 * i)
                chunk(n + 1, 1, (2, 3))

            def down_pair(f, p):
                ln, n = LN_FFN[f], FFN_N[f] + FK + 4 * p
                first = isinstance(p, int)
                k0 = 0
                for c, kc in enumerate(DOWN_K):
                    pe.wait_ge(lo_ready, n + c + 1)
                    if first:
                        pe.wait_ge(h_done, FK * f + k0 + kc)
                        if c == 0:
                            pe.wait_ge(silu_done, FK * (f + 1))
                    for t in range(2):
                        if c == 0 and not first:
                            pe.wait_ge(y_evac, 8 * ln + 2 * p - 1 + t)
                        for k in range(k0, k0 + kc):
                            last = mm3(bank[t][:, :], c % 2, k - k0, t, h_hi[:, k, :], h_lo[:, k, :], k == 0, k == FK - 1)
                        if t == 1:
                            last.then_inc(w_used, 1)
                        elif c == len(DOWN_K) - 1:
                            last.then_inc(y_even, 1)
                    k0 += kc

            def shift_sum(ln):
                pe.wait_ge(y_evac, 8 * ln + 1)
                nc.tensor.matmul(bank[4][:, :], ones[:, :], u[:, 0, :], start=True, stop=True).then_inc(shift_mm, 1)

            def column_sums(c0, x, start, stop):
                for b in range(TB):
                    last = nc.tensor.matmul(bank[5][:, c0 + b:c0 + b + 1], x[:, b * P:(b + 1) * P], ones[:, 0:1],
                                            start=(start and b == 0), stop=(stop and b == TB - 1), skip_group_check=True)
                return last

            def stats(ln):
                pe.wait_ge(u_acc, 6 * ln + 6)
                column_sums(0, usum, True, False)
                pe.wait_ge(q_acc, 6 * ln + 6)
                column_sums(TB, qsum, False, False)
                pe.wait_ge(y_evac, 8 * ln + 8)
                column_sums(0, u[:, DK - 1, :], False, False)
                pe.wait_ge(sq_done, 8 * ln + 8)
                column_sums(TB, sq[1], False, True).then_inc(stats_mm, 1)
                pe.wait_ge(mean_diag, ln + 1)
                nc.tensor.matmul(bank[6][:, :], ones[:, :], diag_mean, start=True, stop=True).then_inc(bcast_mm, 1)
                pe.wait_ge(rstd_diag, ln + 1)
                nc.tensor.matmul(bank[7][:, :], ones[:, :], diag_rstd, start=True, stop=True).then_inc(bcast_mm, 1)

            def ffn(f):
                ffn_pair(f, 0)
                with pe.Fori(1, FK // 2) as i:
                    ffn_pair(f, i)
                down_pair(f, 0)
                shift_sum(LN_FFN[f])
                with pe.Fori(1, 4) as p:
                    down_pair(f, p)
                stats(LN_FFN[f])

            def out_a(ln, n0, p, m, mo_hi, mo_lo):
                n, b0 = n0 + 4 * (p // 2) + p % 2, 2 * (p % 2)
                pe.wait_ge(lo_ready, n + 1)
                pe.wait_ge(mo_done, HEADS * (m + 1))
                if p >= 2:
                    pe.wait_ge(y_evac, 8 * ln + 2 * (p - 2) + 2)
                for t in range(2):
                    for k in range(A_K):
                        last = mm3(bank[b0 + t][:, :], p % 2, k, t, mo_hi[:, k, :], mo_lo[:, k, :], k == 0, False)
                last.then_inc(w_used, 1)

            def out_b(ln, n0, p, y_h, y_l, done, base):
                n, b0 = n0 + 4 * (p // 2) + 2 + p % 2, 2 * (p % 2)
                pe.wait_ge(lo_ready, n + 1)
                for t in range(2):
                    for k in range(B_K):
                        if p == 0 and t == 0:
                            pe.wait_ge(done, base + k + 1)
                        last = mm3(bank[b0 + t][:, :], p % 2, k, t, y_h[:, k, :], y_l[:, k, :], False, k == B_K - 1)
                    last.then_inc(w_used if t else y_even, 1)

            def scores(m, h):
                g = HEADS * m + h
                kt = kv_of[m][:, 0:1024].rearrange("p (h m) -> p h m", h=HEADS)
                pe.wait_ge(kv_loaded, 16 * (m + 1))
                if g:
                    pe.wait_ge(p_exp, 4 * g)
                for b in range(TB):
                    last = nc.tensor.matmul(bank[4 + b // 2][:, (b % 2) * 256:(b % 2) * 256 + 256],
                                            qm_of[m][:, h, b * P:(b + 1) * P], kt[:, h, :], start=True, stop=True)
                    if b % 2:
                        last.then_inc(scores_mm, 1)

            def transposes(m, h):
                g = HEADS * m + h
                probs = pp_of[m][:, 0:1024].rearrange("p (b m) -> p b m", b=TB)
                pe.wait_ge(p_norm, 4 * g + 4)
                if g:
                    pe.wait_ge(pt_evac, 2 * g)
                    pe.wait_ge(mo_done, g)
                for j in range(MB):
                    for b in range(TB):
                        last = nc.tensor.transpose(bank[6 + j][:, b * P:(b + 1) * P],
                                                   probs[:, b, j * P:(j + 1) * P], ident[:, :])
                    last.then_inc(pt_mm, 1)

            def outputs(m, h):
                g = HEADS * m + h
                v = kv_of[m][:, 1024:2048].rearrange("p (b e) -> p b e", b=MB)
                probs_t = pp_of[m][:, 1024:2048].rearrange("p (b s) -> p b s", b=MB)
                pe.wait_ge(pt_evac, 2 * g + 2)
                for j in range(MB):
                    last = nc.tensor.matmul(bank[7][:, :], v[:, j, h * P:(h + 1) * P], probs_t[:, j, :],
                                            start=(j == 0), stop=(j == MB - 1))
                last.then_inc(mo_mm, 1)

            pe.wait_ge(consts, 3)
            pe.wait_ge(mem_loaded, 16)
            for k in range(DK):
                if k >= 4:
                    pe.wait_ge(mem_hi_ready, 2 * (k - 4) + 1)
                for b in range(MB):
                    last = nc.tensor.transpose(bank[4 + k % 4][:, b * P:(b + 1) * P], mem_in[:, b, k * P:(k + 1) * P], ident[:, :])
                last.then_inc(tr_done, 1)
            pe.wait_ge(x_loaded, 16)
            for k in range(DK):
                if k < 4:
                    pe.wait_ge(mem_hi_ready, 2 * (k + 4) + 1)
                else:
                    pe.wait_ge(tr_evac, k - 3)
                for b in range(TB):
                    last = nc.tensor.transpose(bank[4 + k % 4][:, b * P:(b + 1) * P], xin[:, b, k * P:(k + 1) * P], ident[:, :])
                last.then_inc(tr_done, 1)
            pe.wait_ge(rows_loaded, 16 * 8)
            pe.wait_ge(tr_evac, 5)
            nc.tensor.transpose(bank[4][:, 0:ROWS], rows_in[:, :], ident[0:ROWS, 0:ROWS]).then_inc(tr_done, 1)
            pe.wait_ge(tr_evac, 6)
            for k in range(DK):
                last = nc.tensor.transpose(bank[5][:, k * WIDTH:(k + 1) * WIDTH], dw_in[:, k * P:(k + 1) * P],
                                           ident[0:WIDTH, 0:WIDTH])
            last.then_inc(tr_done, 1)
            for n in range(8):
                pe.wait_ge(lo_ready, n + 1)
                if n == 0:
                    pe.wait_ge(mem_ready, DK)
                if n >= 2:
                    pe.wait_ge(kv_evac, 2 * (n - 1))
                for t in range(2):
                    for k in range(DK):
                        last = mm3(bank[2 * (n % 2) + t][:, 0:NMEM], n % 2, k, t, mem_hi[:, k, :], mem_lo[:, k, :], k == 0, k == DK - 1)
                last.then_inc(w_used, 1)
            pe.wait_ge(kv_evac, 16)
            pe.wait_ge(tr_evac, 10)
            for layer in range(DEPTH):
                for j in range(MB):
                    for h in range(HEADS):
                        last = nc.tensor.transpose(bank[4 + 2 * layer + j][:, h * P:(h + 1) * P],
                                                   kv_t[:, layer, 4 + h, j * P:(j + 1) * P], ident[:, :])
                    last.then_inc(kvv_done, 1)
            ffn(0)

            n0 = GLA_N

            def gate(h):
                nc.tensor.matmul(bank[Z_BANK[h]][:, :], w_gate2[:, h * P:(h + 1) * P], a_t, start=True, stop=True).then_inc(z_mm, 1)

            def qkv_chunk(j):
                pe.wait_ge(gla_evac, (4, 5)[j] if j < 2 else 5 + 2 * (j - 1))
                chunk(n0 + 4 + j, j % 2, (2 * (j % 2), 2 * (j % 2) + 1))

            chunk(n0, 0, (0,), 8 * (LN_FFN[0] + 1))
            chunk(n0 + 1, 1, (2,))
            pe.wait_ge(gla_evac, 1)
            pe.wait_ge(gate_w_loaded, 16)
            gate(0)
            chunk(n0 + 2, 0, (0, 1))
            gate(1)
            pe.wait_ge(gla_evac, 2)
            chunk(n0 + 3, 1, (2,))
            gate(2)
            pe.wait_ge(gate_chain, 7)
            scores(0, 0)
            qkv_chunk(0)
            qkv_chunk(1)
            pe.wait_ge(p_exp, 4)
            gate(3)
            pe.wait_ge(gate_chain, 10)
            transposes(0, 0)
            qkv_chunk(2)
            outputs(0, 0)
            pe.wait_ge(gate_chain, 13)
            scores(0, 1)
            qkv_chunk(3)
            transposes(0, 1)
            qkv_chunk(4)
            outputs(0, 1)
            scores(0, 2)
            qkv_chunk(5)
            transposes(0, 2)
            qkv_chunk(6)
            outputs(0, 2)
            scores(0, 3)
            qkv_chunk(7)
            transposes(0, 3)
            pe.wait_ge(gla_evac, 21)
            pe.wait_ge(p_exp, 16)
            for e in range(8):
                if e == 2:
                    outputs(0, 3)
                if e == 3:
                    pe.wait_ge(mo_done, 4)
                if e >= 4:
                    pe.wait_ge(v_evac, e - 3)
                for b in range(TB):
                    last = nc.tensor.transpose(bank[4 + e % 4][:, b * P:(b + 1) * P], qkv[:, 8 + e, b * P:(b + 1) * P], ident[:, :])
                last.then_inc(vt_mm, 1)

            def keys_and_att(h):
                pe.wait_ge(prods, 4 * h + 4)
                if h:
                    pe.wait_ge(kdt_evac, h)
                for b in range(TB):
                    last = nc.tensor.transpose(bank[4][:, b * P:(b + 1) * P], qkv[:, 4 + h, b * P:(b + 1) * P], ident[:, :])
                last.then_inc(kdt_mm, 1)
                if h:
                    pe.wait_ge(att_evac, h)
                for b in range(TB):
                    tok = slice(b * P, (b + 1) * P)
                    last = nc.tensor.matmul(bank[5][:, tok], ke[:, h, tok], qkv[:, h, tok], start=True, stop=True)
                last.then_inc(att_mm, 1)

            def state_sums(h, chunks):
                if h or chunks[0]:
                    pe.wait_ge(state_done, 7 * h + chunks[0])
                for c in chunks:
                    rows = slice(64 * (c % 2), 64 * (c % 2) + 64)
                    last = nc.tensor.matmul(bank[6 + c % 2][:, (c // 2 % 2) * 256:(c // 2 % 2) * 256 + 256],
                                            bk[rows, h, (c // 2) * P:(c // 2 + 1) * P],
                                            v_tok[rows, c // 2, h * 256:(h + 1) * 256], start=True, stop=True)
                last.then_inc(ds_mm, 1)

            pe.wait_ge(v_evac, 8)
            keys_and_att(0)
            for h in range(HEADS):
                pe.wait_ge(kdt_evac, h + 1)
                state_sums(h, range(4))
                if h + 1 < HEADS:
                    keys_and_att(h + 1)
                state_sums(h, range(4, 7))
                pe.wait_ge(att_evac, h + 1)
                for e in range(2):
                    to = bank[2 * (h % 2) + e]
                    if h >= 2:
                        pe.wait_ge(o_read, 4 * (h - 2) + 2 * e + 2)
                    cols = slice(h * 256 + e * P, h * 256 + (e + 1) * P)
                    for b in range(TB):
                        nc.tensor.matmul(to[:, b * P:(b + 1) * P], v_tok[:, b, cols], att[h % 2][:, b, :],
                                         start=(b == 0), stop=False, skip_group_check=True)
                    for c in range(1, NCH):
                        if e == 0:
                            pe.wait_ge(state_done, 7 * h + c)
                        tok = slice(c * CHUNK, (c + 1) * CHUNK)
                        last = nc.tensor.matmul(to[:, tok], states[:, h % 2, c - 1, e * P:(e + 1) * P], qkv[:, h, tok],
                                                start=False, stop=(c == NCH - 1), skip_group_check=True)
                    last.then_inc(o_mm, 1)
            for j in range(4):
                if j < 2:
                    pe.wait_ge(o_read, (12, 16)[j])
                else:
                    pe.wait_ge(gla_evac, 21 + 2 * (j - 1))
                chunk(n0 + 12 + j, j % 2, (2 * (j % 2), 2 * (j % 2) + 1))
                if j == 0:
                    for h in range(HEADS):
                        pe.wait_ge(ss_done, h + 1)
                        for b in range(TB):
                            last = nc.tensor.matmul(bank[4][:, TB * h + b:TB * h + b + 1], ke[:, h, b * P:(b + 1) * P],
                                                    ones[:, 0:1], start=True, stop=True)
                    last.then_inc(rms_mm, 1)
                if j == 1:
                    for h in range(HEADS):
                        pe.wait_ge(rms_diag, h + 1)
                        nc.tensor.matmul(bank[4 + h][:, :], ones[:, :], ke[:, h, :], start=True, stop=True).then_inc(rms_bcast, 1)
            pe.wait_ge(gla_evac, 29)
            for q in range(2):
                for p in (2 * q, 2 * q + 1):
                    out_a(LN_GLA_OUT, GLA_OUT_N, p, 0, mo_hi_g, mo_lo_g)
                for p in (2 * q, 2 * q + 1):
                    out_b(LN_GLA_OUT, GLA_OUT_N, p, y_hi, y_lo, y_done, 0)
                    if p == 0:
                        shift_sum(LN_GLA_OUT)
            stats(LN_GLA_OUT)
            ffn(1)
            ffn(2)

            n0 = CONV_N

            def diag_chunk(g):
                pe.wait_ge(lo_ready, DIAG_N + g + 1)
                if g == 0:
                    pe.wait_ge(cin_done, 2)
                    pe.wait_ge(conv_evac, 20)
                for j in range(TAPS_K[g]):
                    tap = 8 * g + j
                    for t in range(2):
                        last = mm3(bank[2 + t][:, :], g % 2, j, t, cin_hi[:, t, tap:tap + SEQ], cin_lo[:, t, tap:tap + SEQ],
                                   tap == 0, tap == WIDTH - 1)
                last.then_inc(w_used, 1)

            def conv_chunk(j, read=None):
                if read is not None:
                    pe.wait_ge(conv_evac, read)
                chunk(n0 + j, j % 2, (2 * (j % 2), 2 * (j % 2) + 1), 8 * (LN_FFN[2] + 1) if j == 0 else None)

            for j in range(6):
                conv_chunk(j, 2 * (j - 1) if j >= 2 else None)
            shift_sum(LN_CONV)
            pe.wait_ge(conv_evac, 12)
            pe.wait_ge(shift_ready, LN_CONV + 1)
            scores(1, 0)
            conv_chunk(6)
            transposes(1, 0)
            conv_chunk(7)
            outputs(1, 0)
            scores(1, 1)
            conv_chunk(8, 14)
            transposes(1, 1)
            conv_chunk(9, 16)
            outputs(1, 1)
            scores(1, 2)
            diag_chunk(0)
            transposes(1, 2)
            diag_chunk(1)
            outputs(1, 2)
            scores(1, 3)
            diag_chunk(2)
            transposes(1, 3)
            diag_chunk(3)
            outputs(1, 3)
            out_a(LN_CONV_OUT, CONV_OUT_N, 0, 1, mo_hi_c, mo_lo_c)
            pe.wait_ge(conv_evac, 22)
            out_a(LN_CONV_OUT, CONV_OUT_N, 1, 1, mo_hi_c, mo_lo_c)
            stats(LN_CONV)
            for q in range(2):
                if q:
                    for p in (2, 3):
                        out_a(LN_CONV_OUT, CONV_OUT_N, p, 1, mo_hi_c, mo_lo_c)
                for p in (2 * q, 2 * q + 1):
                    out_b(LN_CONV_OUT, CONV_OUT_N, p, c_hi, c_lo, x_ready, 8 * (LN_CONV + 1))
                    if p == 0:
                        shift_sum(LN_CONV_OUT)
            stats(LN_CONV_OUT)
            ffn(3)
            for k in range(DK):
                pe.wait_ge(affine_done, 8 * LN_FFN[3] + k + 1)
                if k >= 4:
                    pe.wait_ge(fin_evac, k - 3)
                for b in range(TB):
                    last = nc.tensor.transpose(bank[k % 4][:, b * P:(b + 1) * P], u[:, k, b * P:(b + 1) * P], ident[:, :])
                last.then_inc(fin_mm, 1)


_INS = ["x", "mem", "ln_g", "ln_b", "ffn1_w_gu", "ffn1_w_down", "ffn2_w_gu", "ffn2_w_down", "mem_w_kv",
        "gla_w_in", "gla_w_gate2", "gla_b_gate", "gla_g_onorm", "gla_w_out",
        "conv_w_in", "conv_w_dw", "conv_b_dw", "conv_ln_g", "conv_ln_b", "conv_w_out"]


def kernel(**inputs):
    import numpy as _np
    import concourse.bacc as _bacc
    from concourse import mybir as _mybir
    from concourse.bass_utils import run_bass_kernel_spmd as _run

    nc = _bacc.Bacc("TRN2", target_bir_lowering=False, num_devices=1)
    arrays, aps = {}, {}
    for name in _INS:
        x = _np.ascontiguousarray(inputs[name])
        arrays[f"in_{name}_dram"] = x
        aps[name] = nc.dram_tensor(f"in_{name}_dram", x.shape, _mybir.dt.from_np(x.dtype), kind="ExternalInput").ap()
    out = nc.dram_tensor("out_0_dram", (1, SEQ, D), _mybir.dt.float32, kind="ExternalOutput").ap()
    build(nc, aps, out)
    r = _run(nc, [arrays], core_ids=[0])
    return r.results[0]["out_0_dram"]
```

```python
from contextlib import ExitStack

import concourse.bass as bass
from concourse import mybir

ALU = mybir.AluOpType
ACT = mybir.ActivationFunctionType
F32 = mybir.dt.float32
F32R = mybir.dt.float32r
I32 = mybir.dt.int32
AX_X = mybir.AxisListType.X

P = 128
SEQ = 512
D = 1024
DK = D // P
TB = SEQ // P
NMEM = 256
MB = NMEM // P
FF = 2816
FK = FF // P
HEADS = 4
DKH = 128
CHUNK = 64
NCH = SEQ // CHUNK
RANK = 16
WIDTH = 31
PAD = WIDTH - 1
DEPTH = 2
ALPHA = (2 * DEPTH) ** 0.25
LN_EPS = 1e-5
RMS_EPS = 1e-6
GATE_NORM = 16.0
MEM_SCALE = P ** -0.5
GLA_SCALE = DKH ** -0.5
OUT_K = 12

ROW_G, ROW_B = 0, DEPTH * 3 * DK
ROW_BDW = 2 * ROW_B
ROW_CG, ROW_CB = ROW_BDW + DK, ROW_BDW + 2 * DK
ROW_GATE = ROW_BDW + 3 * DK
ROW_ONORM = ROW_GATE + HEADS
ROWS = ROW_ONORM + 2

KV_N = 0
N_FFN = FK + 16
FFN_N = [8, 70, 108, 168]
GLA_N, GLA_OUT_N = 46, 62
CONV_N, CONV_OUT_N = 146, 160
DIAG_N = CONV_N + 10
N_CHUNKS = 206
DOWN_K = [6, 6, 6, 4]
A_K, B_K = 4, 8
PE_C = 6
TAPS_K = [8, 8, 8, 7]
DVE_TAPS = [WIDTH, WIDTH, WIDTH - 5]

LN_FFN = [0, 2, 3, 6]
LN_GLA_OUT, LN_CONV, LN_CONV_OUT = 1, 4, 5
LN_ROW = {0: 0, 1: 1, 2: 2, 3: 3, 5: 4, 6: 5}
EVEN_BASE = [0, 4, 8, 12, 16, 16, 20]
RES_BASE = [0, 8, 24, 32, 40, 40, 56]
RES_PER = {0: 1, 1: 2, 2: 1, 3: 1, 5: 2, 6: 1}


def build(nc, a, out):
    kv_dram = nc.dram_tensor("kv_scratch", (DEPTH, P, 2048), F32, kind="Internal").ap()
    with ExitStack() as ctx:
        def sem(name):
            return ctx.enter_context(nc.semaphore(name))

        def views(*specs):
            got = []
            with ExitStack() as part:
                for n, (name, shape, dt) in enumerate(specs):
                    got.append(part.enter_context(nc.sbuf_tensor(name, shape, dt)))
            return got

        def sb(name, shape, dt=F32):
            return ctx.enter_context(nc.sbuf_tensor(name, shape, dt))

        xhi = sb("xhi", [P, DK, SEQ], F32R)
        xlo = sb("xlo", [P, DK, SEQ], F32R)
        u = sb("u", [P, DK, SEQ])
        raw = sb("raw", [P, 2, 8, 256])
        whi = sb("whi", [P, 2, 8, 256], F32R)
        wlo = sb("wlo", [P, 2, 8, 256], F32R)
        scratch = sb("scratch", [P, 9, SEQ])
        usum, qsum, shift, delta, rstd = (scratch[:, i, :] for i in range(5))
        w_tap_hi = sb("w_tap_hi", [P, 2 * WIDTH], F32R)
        w_tap_lo = sb("w_tap_lo", [P, 2 * WIDTH], F32R)
        sq = [scratch[:, 5, :], scratch[:, 6, :]]
        act_out = [scratch[:, 7, :], scratch[:, 8, :]]
        diag_mean, diag_rstd = delta, rstd
        tiny = sb("tiny", [P, 72])
        mean_sq, sq_mean, var, rs = tiny[:, 0:8], tiny[:, 8:12], tiny[:, 12:16], tiny[:, 16:20]
        rms_v, rms_r, minus_half = tiny[:, 20:36], tiny[:, 36:52], tiny[:, 52:68]
        prm = sb("prm", [P, ROWS])
        w_dw = sb("w_dw", [P, DK * WIDTH])
        ident = sb("ident", [P, P])
        ones = sb("ones", [P, P])
        small = sb("small", [P, 16])
        row_max, neg_max, row_sum, inv_sum = (small[:, 4 * i:4 * i + 4] for i in range(4))
        exp_last = sb("exp_last", [P, HEADS, NCH])

        xin, mem_in, mem_hi, mem_lo, kv_t, kv_v, rows_in, dw_in = views(
            ("xin", [P, TB, D], F32), ("mem_in", [P, MB, D], F32),
            ("mem_hi", [P, DK, NMEM], F32R), ("mem_lo", [P, DK, NMEM], F32R),
            ("kv_t", [P, DEPTH, 8, NMEM], F32), ("kv_v", [P, DEPTH, MB, 512], F32),
            ("rows_in", [ROWS, P], F32), ("dw_in", [WIDTH, D], F32))
        h_hi, h_lo = views(("h_hi", [P, FK, SEQ], F32R), ("h_lo", [P, FK, SEQ], F32R))
        qkv, mo_hi_g, mo_lo_g, qm_g, bk, ke, v_tok = views(
            ("qkv", [P, 16, SEQ], F32), ("mo_hi_g", [P, HEADS, SEQ], F32R), ("mo_lo_g", [P, HEADS, SEQ], F32R),
            ("qm_g", [P, HEADS, SEQ], F32), ("bk", [P, HEADS, SEQ], F32), ("ke", [P, HEADS, SEQ], F32),
            ("v_tok", [P, TB, D], F32))
        _, states, att0 = views(
            ("q_k", [P, 8, SEQ], F32), ("states", [P, 2, 7, 256], F32), ("att0", [P, TB, P], F32))
        _, r_act, _, y_lo, y_hi = views(
            ("q_k2", [P, 8, SEQ], F32), ("r_act", [P, 8, SEQ], F32), ("mo_qm", [P, 12, SEQ], F32),
            ("y_lo", [P, 8, SEQ], F32R), ("y_hi", [P, 8, SEQ], F32R))
        conv_in, qm_c, mo_hi_c, mo_lo_c, kv_c, pp_c, c_lo, cin_hi, cin_lo = views(
            ("conv_in", [P, DK, PAD + SEQ], F32), ("qm_c", [P, HEADS, SEQ], F32),
            ("mo_hi_c", [P, HEADS, SEQ], F32R), ("mo_lo_c", [P, HEADS, SEQ], F32R),
            ("kv_c", [P, 2048], F32), ("pp_c", [P, 2048], F32), ("c_lo", [P, DK, SEQ], F32R),
            ("cin_hi", [P, 2, PAD + SEQ], F32R), ("cin_lo", [P, 2, PAD + SEQ], F32R))
        c_hi, = views(("c_hi", [P, DK, SEQ], F32R))
        out_tok, = views(("out_tok", [P, 4, TB, P], F32))

        Z_BANK = [6, 7, 3, 4]
        V_BANK = [4, 5, 0, 1, 4, 5, 6, 7]
        att_mask, reset, exp_a, exp_b, gate_t = usum, qsum, shift, delta, rstd
        att = [att0[:, :, :], sq[0].rearrange("p (b i) -> p b i", b=TB)]
        a_t = sq[1][0:RANK, :]
        w_gate2 = act_out[0][0:RANK, :]
        uflat = u[:, :, :].rearrange("p k s -> p (k s)")
        tap_sum = [qm_c[:, 0, :], qm_c[:, 1, :]]
        kv_of = [uflat[:, 0:2048], kv_c[:, :]]
        pp_of = [uflat[:, 2048:4096], pp_c[:, :]]
        qm_of = [qm_g, qm_c]
        mo_hi_of, mo_lo_of = [mo_hi_g, mo_hi_c], [mo_lo_g, mo_lo_c]

        bank = [ctx.enter_context(nc.psum_tensor(f"bank{i}", [P, SEQ], F32)) for i in range(8)]

        rows_loaded, mem_loaded, x_loaded, consts, gate_w_loaded = (
            sem(n) for n in ("rows_loaded", "mem_loaded", "x_loaded", "consts", "gate_w_loaded"))
        raw_loaded = [sem("raw_loaded0"), sem("raw_loaded1")]
        hi_ready, lo_ready, w_used = sem("hi_ready"), sem("lo_ready"), sem("w_used")
        tr_done, tr_evac = sem("tr_done"), sem("tr_evac")
        mem_hi_ready, mem_ready = sem("mem_hi_ready"), sem("mem_ready")
        kv_evac, kvv_done, kvv_evac, kv_stored, kv_loaded = (
            sem(n) for n in ("kv_evac", "kvv_done", "kvv_evac", "kv_stored", "kv_loaded"))
        silu_done, mul_done, h_hi_done, h_done = (
            sem(n) for n in ("silu_done", "mul_done", "h_hi_done", "h_done"))
        y_even, y_evac, res_done, u0_ready, u_acc, q_acc, sq_done = (
            sem(n) for n in ("y_even", "y_evac", "res_done", "u0_ready", "u_acc", "q_acc", "sq_done"))
        shift_mm, shift_ready, stats_mm, stat_step, var_ready, rs_ready, mean_diag, rstd_diag, bcast_mm = (
            sem(n) for n in ("shift_mm", "shift_ready", "stats_mm", "stat_step", "var_ready",
                             "rs_ready", "mean_diag", "rstd_diag", "bcast_mm"))
        centred, normed, affine_done, x_hi_ready, x_ready = (
            sem(n) for n in ("centred", "normed", "affine_done", "x_hi_ready", "x_ready"))
        gla_evac, z_mm, gate_act, gate_chain, vt_mm, v_evac, exps, prods = (
            sem(n) for n in ("gla_evac", "z_mm", "gate_act", "gate_chain", "vt_mm", "v_evac",
                             "exps", "prods"))
        scores_mm, max_done, neg_max_done, p_exp, inv_done, p_norm, pt_mm, pt_evac, mo_mm, mo_hi_done, mo_done = (
            sem(n) for n in ("scores_mm", "max_done", "neg_max_done", "p_exp", "inv_done", "p_norm",
                             "pt_mm", "pt_evac", "mo_mm", "mo_hi_done", "mo_done"))
        kdt_mm, kdt_evac, att_mm, att_evac, ds_mm, state_done, o_mm, o_read, ss_done = (
            sem(n) for n in ("kdt_mm", "kdt_evac", "att_mm", "att_evac", "ds_mm", "state_done",
                             "o_mm", "o_read", "ss_done"))
        reset_done, att_clear = sem("reset_done"), sem("att_clear")
        rms_mm, rms_var, rms_rs, rms_diag, rms_bcast, y_scaled, y_ready, y_hi_done, y_done, gla_masks = (
            sem(n) for n in ("rms_mm", "rms_var", "rms_rs", "rms_diag", "rms_bcast", "y_scaled",
                             "y_ready", "y_hi_done", "y_done", "gla_masks"))
        conv_evac, glu_done, taps_done, conv_pad, tap_split, cin_hi_done, cin_done = (
            sem(n) for n in ("conv_evac", "glu_done", "taps_done", "conv_pad", "tap_split",
                             "cin_hi_done", "cin_done"))
        tap_mul, tap_add = sem("tap_mul"), sem("tap_add")
        fin_mm, fin_evac, out_stored = sem("fin_mm"), sem("fin_evac"), [sem(f"out_stored{i}") for i in range(4)]

        block = ctx.enter_context(nc.Block())

        @block.sync
        def _(sp):
            def load(n, s, src, free=None):
                if not isinstance(n, int) or n >= 2:
                    sp.wait_ge(lo_ready, n - 1 if free is None else free)
                sp.dma_start(raw[:, s, 0:src.shape[1], 0:src.shape[2]], src).then_inc(raw_loaded[s], 16)

            def cols(w, c0, width=256):
                return w[:, :, bass.ds(c0, width)]

            def ffn(f):
                layer, which = divmod(f, 2)
                w_gu = a["ffn1_w_gu" if which == 0 else "ffn2_w_gu"][layer].rearrange("(k p) n -> p k n", p=P)
                w_dn = a["ffn1_w_down" if which == 0 else "ffn2_w_down"][layer].rearrange("(k p) n -> p k n", p=P)
                n0 = FFN_N[f]
                with sp.Fori(0, FK // 2) as i:
                    load(n0 + 2 * i, 0, cols(w_gu, i * 256))
                    load(n0 + 2 * i + 1, 1, cols(w_gu, i * 256 + FF))
                n0 += FK
                with sp.Fori(0, 4) as p:
                    k = 0
                    for c, kc in enumerate(DOWN_K):
                        load(n0 + 4 * p + c, c % 2, cols(w_dn[:, k:k + kc, :], p * 256))
                        k += kc

            def out_proj(w, n0, free=None):
                w = w.rearrange("(k p) n -> p k n", p=P)
                wa, wb = w[:, B_K:B_K + A_K, :], w[:, 0:B_K, :]
                load(n0, 0, cols(wa, 0), free)
                load(n0 + 1, 1, cols(wa, 256), free)
                load(n0 + 2, 0, cols(wb, 0))
                load(n0 + 3, 1, cols(wb, 256))
                load(n0 + 4, 0, cols(wa, 512))
                load(n0 + 5, 1, cols(wa, 768))
                load(n0 + 6, 0, cols(wb, 512))
                load(n0 + 7, 1, cols(wb, 768))

            def load_parameters():
                r0 = 0
                for name, rows in (("ln_g", DEPTH * 3 * DK), ("ln_b", DEPTH * 3 * DK), ("conv_b_dw", DK),
                                   ("conv_ln_g", DK), ("conv_ln_b", DK), ("gla_b_gate", HEADS), ("gla_g_onorm", 2)):
                    src = a[name]
                    src = (src.rearrange("l w (k p) -> (l w k) p", p=P) if len(src.shape) == 3
                           else src.rearrange("l (k p) -> (l k) p", p=P))
                    sp.dma_start(rows_in[r0:r0 + rows, :], src).then_inc(rows_loaded, 16)
                    r0 += rows
                sp.dma_start(dw_in[:, :], a["conv_w_dw"][0]).then_inc(rows_loaded, 16)

            sp.dma_start(mem_in[:, :, :], a["mem"][0].rearrange("(b p) d -> p b d", p=P)).then_inc(mem_loaded, 16)
            for layer in range(DEPTH):
                w = a["mem_w_kv"][layer].rearrange("(k p) n -> p k n", p=P)
                for c in range(4):
                    n = KV_N + 4 * layer + c
                    load(n, n % 2, cols(w, c * 256))
                    if n == 1:
                        sp.dma_start(xin[:, :, :], a["x"][0].rearrange("(b p) d -> p b d", p=P)).then_inc(x_loaded, 16)
                        load_parameters()
            ffn(0)
            w = a["gla_w_in"][0].rearrange("(k p) n -> p k n", p=P)
            n = GLA_N
            load(n, 0, cols(w, 3072, P))
            load(n + 1, 1, cols(w, 3088, P))
            load(n + 2, 0, cols(w, 3216))
            load(n + 3, 1, cols(w, 3472, P))
            sp.wait_ge(x_ready, 8 * (LN_FFN[0] + 2))
            sp.wait_ge(kv_stored, 64)
            sp.dma_start(kv_of[0], kv_dram[0]).then_inc(kv_loaded, 16)
            with sp.Fori(0, 6) as i:
                load(n + 4 + 2 * i, 0, cols(w, i * 512))
                load(n + 5 + 2 * i, 1, cols(w, i * 512 + 256))
            out_proj(a["gla_w_out"][0], GLA_OUT_N)
            ffn(1)
            ffn(2)
            w = a["conv_w_in"][0].rearrange("(k p) n -> p k n", p=P)
            n = CONV_N
            with sp.Fori(0, 2) as i:
                load(n + 2 * i, 0, cols(w, i * 256))
                load(n + 2 * i + 1, 1, cols(w, i * 256 + D))
            load(n + 4, 0, cols(w, 2 * D))
            load(n + 5, 1, cols(w, 2 * D + 256))
            sp.wait_ge(x_ready, 8 * (LN_FFN[2] + 2))
            sp.dma_start(kv_of[1], kv_dram[1]).then_inc(kv_loaded, 16)
            load(n + 6, 0, cols(w, 768))
            load(n + 7, 1, cols(w, 768 + D))
            load(n + 8, 0, cols(w, 512))
            load(n + 9, 1, cols(w, 512 + D))
            out_proj(a["conv_w_out"][0], CONV_OUT_N, free=DIAG_N)
            ffn(3)
            for k in range(DK):
                sp.wait_ge(fin_evac, k + 1)
                sp.dma_start(out[0].rearrange("(b p) d -> p b d", p=P)[:, :, k * P:(k + 1) * P],
                             out_tok[:, k % 4, :, :]).then_inc(out_stored[k % 4], 16)
            for i in range(4):
                sp.wait_ge(out_stored[i], 32)

        @block.gpsimd
        def _(pool):
            def split_lo(n, s, kc=8, width=256, after_dve=False):
                pool.wait_ge(hi_ready, n + 1)
                if after_dve:
                    pool.wait_ge(lo_ready, n)
                nc.gpsimd.tensor_tensor(wlo[:, s, 0:kc, 0:width], raw[:, s, 0:kc, 0:width],
                                        whi[:, s, 0:kc, 0:width].bitcast(F32), ALU.subtract).then_inc(lo_ready, 1)

            def lo_of_x(ln, lo, hi):
                if ln >= 0 and ln != LN_CONV:
                    rsqrt(ln)
                for k in range(DK):
                    pool.wait_ge(x_hi_ready, 8 * (ln + 1) + k + 1)
                    if ln >= 0:
                        pool.wait_ge(affine_done, 8 * ln + k + 1)
                    nc.gpsimd.tensor_tensor(lo[:, k, :], u[:, k, :], hi[:, k, 0:SEQ].bitcast(F32),
                                            ALU.subtract).then_inc(x_ready, 1)

            def rsqrt(ln):
                pool.wait_ge(var_ready, ln + 1)
                nc.gpsimd.tensor_tensor(rs, var, minus_half[:, 0:TB], ALU.pow).then_inc(rs_ready, 1)

            def ffn(f):
                n0 = FFN_N[f]
                split_lo(n0 + 2, 0, after_dve=True)
                split_lo(n0 + 3, 1)
                with pool.Fori(1, FK // 2 - 1) as i:
                    split_lo(n0 + 2 * i + 2, 0)
                    split_lo(n0 + 2 * i + 3, 1)
                down(n0 + FK)

            def down(n0):
                split_lo(n0, 0, 6)
                split_lo(n0 + 1, 1, 6)
                with pool.Fori(0, 3) as p:
                    for c in range(4):
                        split_lo(n0 + 4 * p + 2 + c, c % 2, DOWN_K[(c + 2) % 4])
                split_lo(n0 + 14, 0, 6)
                split_lo(n0 + 15, 1, 4)

            nc.gpsimd.memset(ones[:, :], 1.0).then_inc(consts, 1)
            nc.gpsimd.memset(ident[:, :], 0.0).then_inc(consts, 1)
            pool.wait_ge(consts, 2)
            nc.gpsimd.affine_select(out=ident[:, :], in_=ident[:, :], compare_op=ALU.not_equal, fill=1.0,
                                    base=0, pattern=[[-1, P]], channel_multiplier=1).then_inc(consts, 1)
            nc.gpsimd.memset(minus_half, -0.5).then_inc(consts, 1)
            for k in range(DK):
                pool.wait_ge(mem_hi_ready, 2 * k + 2)
                nc.gpsimd.tensor_tensor(mem_lo[:, k, :], kv_t[:, 0, k, :],
                                        mem_hi[:, k, :].bitcast(F32), ALU.subtract).then_inc(mem_ready, 1)
            lo_of_x(-1, xlo, xhi)
            pool.wait_ge(tap_split, 1)
            nc.gpsimd.tensor_tensor(w_tap_lo[:, :], w_dw[:, PE_C * WIDTH:DK * WIDTH], w_tap_hi[:, :].bitcast(F32),
                                    ALU.subtract).then_inc(tap_split, 1)
            ffn(0)
            split_lo(GLA_N, 0, 8, P)
            lo_of_x(LN_FFN[0], xlo, xhi)
            nc.gpsimd.memset(att_mask, 1.0).then_inc(gla_masks, 1)
            pool.wait_ge(gla_masks, 1)
            m = att_mask.rearrange("p (b i) -> p b i", b=TB)
            nc.gpsimd.affine_select(out=m, in_=m, compare_op=ALU.is_ge, fill=0.0, base=0,
                                    pattern=[[0, TB], [1, P]], channel_multiplier=-1).then_inc(gla_masks, 1)
            pool.wait_ge(gla_masks, 2)
            nc.gpsimd.memset(m[0:CHUNK, :, CHUNK:P], 0.0).then_inc(gla_masks, 1)
            split_lo(GLA_N + 2, 0, after_dve=True)
            split_lo(GLA_N + 3, 1, 8, P)
            with pool.Fori(0, 5) as i:
                split_lo(GLA_N + 4 + 2 * i, 0)
                split_lo(GLA_N + 5 + 2 * i, 1)
            split_lo(GLA_N + 14, 0)
            pool.wait_ge(rms_var, 1)
            nc.gpsimd.tensor_tensor(rms_r, rms_v, minus_half, ALU.pow).then_inc(rms_rs, 1)
            split_lo(GLA_N + 15, 1)
            with pool.Fori(0, 2) as q:
                split_lo(GLA_OUT_N + 4 * q, 0, A_K)
                split_lo(GLA_OUT_N + 4 * q + 1, 1, A_K)
                split_lo(GLA_OUT_N + 4 * q + 3, 1, B_K, after_dve=True)
            split_lo(FFN_N[1], 0)
            lo_of_x(LN_GLA_OUT, xlo, xhi)
            ffn(1)
            split_lo(FFN_N[2], 0)
            lo_of_x(LN_FFN[1], xlo, xhi)
            ffn(2)
            split_lo(CONV_N, 0)
            lo_of_x(LN_FFN[2], xlo, xhi)
            nc.gpsimd.memset(conv_in[:, :, 0:PAD], 0.0).then_inc(conv_pad, 1)

            def glu(i, c_evac):
                pool.wait_ge(conv_evac, c_evac)
                for t in range(2):
                    nc.gpsimd.tensor_tensor(conv_in[:, 2 * i + t, PAD:PAD + SEQ], conv_in[:, 2 * i + t, PAD:PAD + SEQ],
                                            act_out[t], ALU.mult).then_inc(glu_done, 1)

            n0 = CONV_N
            split_lo(n0 + 2, 0, after_dve=True)
            split_lo(n0 + 3, 1)
            glu(0, 4)
            split_lo(n0 + 4, 0)
            split_lo(n0 + 5, 1)
            glu(1, 8)
            split_lo(n0 + 6, 0)
            split_lo(n0 + 7, 1)
            split_lo(n0 + 8, 0)
            split_lo(n0 + 9, 1)
            glu(3, 16)
            for t in range(2):
                pool.wait_ge(cin_hi_done, t + 1)
                nc.gpsimd.tensor_tensor(cin_lo[:, t, :], conv_in[:, PE_C + t, :], cin_hi[:, t, :].bitcast(F32),
                                        ALU.subtract).then_inc(cin_done, 1)

            def diag_lo(g):
                kc = TAPS_K[g]
                pool.wait_ge(hi_ready, DIAG_N + g + 1)
                taps = w_tap_lo[:, :].bitcast(F32).rearrange("p (t j) -> p j t", t=2)[:, 8 * g:8 * g + kc, :]
                for t in range(2):
                    last = nc.gpsimd.tensor_tensor(
                        wlo[:, g % 2, 0:kc, t * P:(t + 1) * P],
                        ident[:, :].rearrange("p (a c) -> p a c", a=1).to_broadcast([P, kc, P]),
                        taps[:, :, t:t + 1].to_broadcast([P, kc, P]), ALU.mult)
                last.then_inc(lo_ready, 1)

            diag_lo(0)
            glu(2, 20)

            def add_taps(i):
                for t in range(2):
                    pool.wait_ge(tap_mul, 2 * i + t + 1)
                    if i > 1:
                        pool.wait_ge(tap_add, 2 * (i - 2) + t + 1)
                    nc.gpsimd.tensor_tensor(tap_sum[t], tap_sum[t], act_out[t], ALU.add).then_inc(tap_add, 1)

            diag_lo(1)
            add_taps(1)
            diag_lo(2)
            add_taps(2)
            diag_lo(3)
            add_taps(3)
            split_lo(CONV_OUT_N, 0, A_K)
            add_taps(4)
            split_lo(CONV_OUT_N + 1, 1, A_K)
            split_lo(CONV_OUT_N + 2, 0, B_K)
            rsqrt(LN_CONV)
            split_lo(CONV_OUT_N + 3, 1, B_K)
            lo_of_x(LN_CONV, c_lo, c_hi)
            split_lo(CONV_OUT_N + 4, 0, A_K)
            split_lo(CONV_OUT_N + 5, 1, A_K)
            split_lo(CONV_OUT_N + 7, 1, B_K, after_dve=True)
            split_lo(FFN_N[3], 0)
            lo_of_x(LN_CONV_OUT, xlo, xhi)
            ffn(3)
            rsqrt(LN_FFN[3])

        @block.scalar
        def _(act):
            def split_hi(turn, s, kc=8, width=256, late=False):
                n = 2 * turn + s
                if isinstance(n, int) and n >= N_CHUNKS:
                    return
                if not isinstance(n, int) or n >= 2:
                    act.wait_ge(w_used, n - 1)
                loads = turn + 1 if not isinstance(turn, int) or n < DIAG_N else turn - 1
                if late:
                    loads = turn - 1
                act.wait_ge(raw_loaded[s], 16 * loads)
                nc.scalar.copy(whi[:, s, 0:kc, 0:width], raw[:, s, 0:kc, 0:width]).then_inc(hi_ready, 1)

            def ffn_pair(f, i, nxt):
                t0 = FFN_N[f] // 2
                act.wait_ge(w_used, FFN_N[f] + 2 * i + 1)
                split_hi(t0 + i + 1, 0, 8 if nxt else DOWN_K[0], late=f == 3)
                for t in range(2):
                    if not isinstance(i, int) or f + i > 0:
                        act.wait_ge(h_done, FK * f + 2 * i)
                    nc.scalar.activation(act_out[t], bank[t][:, :], ACT.Silu).then_inc(silu_done, 1)
                act.wait_ge(w_used, FFN_N[f] + 2 * i + 2)
                split_hi(t0 + i + 1, 1, 8 if nxt else DOWN_K[1], late=f == 3)
                if isinstance(i, int) and f + i == 0:
                    act.wait_ge(kv_stored, 64)
                for t in range(2):
                    act.wait_ge(mul_done, FK * f + 2 * i + t + 1)
                    nc.scalar.copy(h_hi[:, bass.ds(2 * i + t, 1), :], act_out[t].rearrange("p (a s) -> p a s", a=1)).then_inc(h_hi_done, 1)

            def squares(ln, p):
                for t in range(2):
                    d = 2 * p + t
                    if isinstance(p, int) and d == 0:
                        act.wait_ge(u0_ready, ln + 1)
                    else:
                        act.wait_ge(y_evac, 8 * ln + d + 1)
                    if not isinstance(p, int) or d >= 2:
                        act.wait_ge(q_acc, 6 * ln + d - 1 - t)
                    nc.scalar.activation(sq[t], u[:, bass.ds(d, 1), :].rearrange("p a s -> p (a s)"), ACT.Square).then_inc(sq_done, 1)

            def shift_copy(ln):
                act.wait_ge(shift_mm, ln + 1)
                nc.scalar.activation(shift, bank[4][:, :], ACT.Copy, scale=1.0 / P).then_inc(shift_ready, 1)

            def down_pair(f, p, last=False):
                t0 = (FFN_N[f] + FK) // 2 + 2 * p
                for c in range(3):
                    kc = 8 if last and c >= 2 else DOWN_K[(c + 2) % 4]
                    width = P if last and c == 2 and f in (0,) else 256
                    split_hi(t0 + 1 + c // 2, c % 2, kc, width, late=f == 3)
                if isinstance(p, int) and p == 0:
                    shift_copy(LN_FFN[f])
                squares(LN_FFN[f], p)
                split_hi(t0 + 2, 1, 8 if last else DOWN_K[1], P if last and f == 0 else 256, late=f == 3)

            def out_proj(ln, n0):
                for q in range(2):
                    t0 = n0 // 2 + 2 * q
                    if q:
                        split_hi(t0 + 1, 0, B_K)
                    if ln == LN_GLA_OUT or q:
                        split_hi(t0 + 1, 1, B_K)
                    if q == 0:
                        shift_copy(ln)
                    squares(ln, 2 * q)
                    split_hi(t0 + 2, 0, A_K if q == 0 else 8)
                    squares(ln, 2 * q + 1)
                    split_hi(t0 + 2, 1, A_K if q == 0 else 8)
                norm(ln)

            def affine(ln, hi, g_row, b_row, func=ACT.Identity):
                def of(k, to):
                    return nc.scalar.activation(to[:, k, 0:SEQ], u[:, k, :], func, scale=prm[:, g_row + k:g_row + k + 1],
                                                bias=prm[:, b_row + k:b_row + k + 1])

                def rounded(k):
                    act.wait_ge(affine_done, 8 * ln + k + 1)
                    nc.scalar.copy(hi[:, k, 0:SEQ], u[:, k, :]).then_inc(x_hi_ready, 1)

                for k in range(2):
                    act.wait_ge(normed, 8 * ln + k + 1)
                    of(k, hi).then_inc(x_hi_ready, 1)
                    act.wait_ge(x_hi_ready, 8 * (ln + 1) + k + 1)
                    of(k, u).then_inc(affine_done, 1)
                for k in range(2, DK):
                    act.wait_ge(normed, 8 * ln + k + 1)
                    of(k, u).then_inc(affine_done, 1)
                    if k > 4:
                        rounded(k - 1)
                    elif k < 4:
                        rounded(k)
                rounded(DK - 1)

            def norm(ln, hi=xhi):
                affine(ln, hi, ROW_G + LN_ROW[ln] * DK, ROW_B + LN_ROW[ln] * DK)

            def ffn(f):
                ffn_pair(f, 0, True)
                with act.Fori(1, FK // 2 - 1) as i:
                    ffn_pair(f, i, True)
                ffn_pair(f, FK // 2 - 1, False)
                down_pair(f, 0)
                with act.Fori(1, 3) as p:
                    down_pair(f, p)
                down_pair(f, 3, last=True)
                if f < 3:
                    norm(LN_FFN[f])

            def exps_of(m, h):
                g = HEADS * m + h
                probs = pp_of[m][:, 0:1024].rearrange("p (b m) -> p b m", b=TB)
                act.wait_ge(neg_max_done, g + 1)
                if g:
                    act.wait_ge(pt_mm, 2 * g)
                for b in range(TB):
                    nc.scalar.activation(probs[:, b, :], bank[4 + b // 2][:, (b % 2) * 256:(b % 2) * 256 + 256],
                                         ACT.Exp, scale=MEM_SCALE, bias=neg_max[:, b:b + 1],
                                         accum_out=row_sum[:, b:b + 1]).then_inc(p_exp, 1)

            def probs_back(m, h):
                g = HEADS * m + h
                probs_t = pp_of[m][:, 1024:2048].rearrange("p (b s) -> p b s", b=MB)
                act.wait_ge(pt_mm, 2 * g + 1)
                if g:
                    act.wait_ge(mo_mm, g)
                nc.scalar.copy(probs_t[:, 0, :], bank[6][:, :]).then_inc(pt_evac, 1)
                if m == 1:
                    act.wait_ge(pt_mm, 2 * g + 2)
                    nc.scalar.copy(probs_t[:, 1, :], bank[7][:, :]).then_inc(pt_evac, 1)

            def mo_hi_copy(m, h):
                g = HEADS * m + h
                act.wait_ge(mo_mm, g + 1)
                nc.scalar.copy(mo_hi_of[m][:, h, :], bank[7][:, :]).then_inc(mo_hi_done, 1)

            def x_part(k0):
                for k in range(k0, k0 + 4):
                    act.wait_ge(tr_done, 1 + DK + k)
                    nc.scalar.copy(u[:, k, :], bank[4 + k % 4][:, :]).then_inc(tr_evac, 1)
                    act.wait_ge(tr_evac, 1 + k)
                    nc.scalar.copy(xhi[:, k, :], u[:, k, :]).then_inc(x_hi_ready, 1)

            for k in range(DK):
                act.wait_ge(tr_done, 1 + k)
                nc.scalar.copy(kv_t[:, 0, k, :], bank[4 + k % 4][:, 0:NMEM]).then_inc(mem_hi_ready, 1)
                act.wait_ge(mem_hi_ready, 2 * k + 1)
                nc.scalar.copy(mem_hi[:, k, :], kv_t[:, 0, k, :]).then_inc(mem_hi_ready, 1)
                if k % 4 == 3:
                    split_hi(0, k // 4)
            for n in range(8):
                act.wait_ge(w_used, n + 1)
                split_hi(n // 2 + 1, n % 2)
                for t in range(2):
                    if n == 0 and t == 0:
                        act.wait_ge(mem_ready, DK)
                    nc.scalar.copy(kv_t[:, n // 4, 2 * (n % 4) + t, :], bank[2 * (n % 2) + t][:, 0:NMEM]).then_inc(kv_evac, 1)
                if n < 2:
                    x_part(4 * n)
                if n == 2:
                    act.wait_ge(tr_done, 2 * DK + 1)
                    nc.scalar.copy(prm[:, :], bank[4][:, 0:ROWS]).then_inc(tr_evac, 1)
                    act.wait_ge(tr_done, 2 * DK + 2)
                    nc.scalar.copy(w_dw[:, :], bank[5][:, 0:DK * WIDTH]).then_inc(tr_evac, 1)
                    act.wait_ge(tr_evac, DK + 2)
                    nc.scalar.copy(w_tap_hi[:, :], w_dw[:, PE_C * WIDTH:DK * WIDTH]).then_inc(tap_split, 1)
            for j in range(4):
                act.wait_ge(kvv_done, j + 1)
                nc.scalar.copy(kv_v[:, j // 2, j % 2, :], bank[4 + j][:, :]).then_inc(kvv_evac, 1)
            act.wait_ge(kvv_evac, 4)
            for layer in range(DEPTH):
                act.dma_start(kv_dram[layer, :, 0:1024],
                              kv_t[:, layer, 0:4, :].rearrange("p h m -> p (h m)")).then_inc(kv_stored, 16)
                act.dma_start(kv_dram[layer, :, 1024:2048],
                              kv_v[:, layer, :, :].rearrange("p b e -> p (b e)")).then_inc(kv_stored, 16)
            ffn(0)

            t0, n0 = GLA_N // 2, GLA_N
            act.dma_start(w_gate2, a["gla_w_gate2"][0]).then_inc(gate_w_loaded, 16)

            def step(j, kc=8, width=256):
                act.wait_ge(w_used, GLA_N + j + 1)
                split_hi(t0 + (j + 2) // 2, j % 2, kc, width)

            def gate(h):
                act.wait_ge(z_mm, h + 1)
                act.wait_ge(gate_chain, 3 * h + 1)
                nc.scalar.activation(exp_a, bank[Z_BANK[h]][:, :], ACT.Abs,
                                     bias=prm[:, ROW_GATE + h:ROW_GATE + h + 1]).then_inc(gate_act, 1)
                act.wait_ge(gate_act, 3 * h + 1)
                nc.scalar.activation(exp_a, exp_a, ACT.Exp, scale=-1.0).then_inc(gate_act, 1)
                act.wait_ge(gate_act, 3 * h + 2)
                nc.scalar.activation(exp_a, exp_a, ACT.Ln, bias=1.0).then_inc(gate_act, 1)

            def decays(h):
                b_h = bk[:, h, :]
                if h:
                    act.wait_ge(prods, 4 * h)
                act.wait_ge(gate_chain, 3 * HEADS + 1)
                nc.scalar.activation(exp_a, b_h, ACT.Exp, scale=1.0 / GATE_NORM).then_inc(exps, 1)
                nc.scalar.activation(exp_b, b_h, ACT.Exp, scale=-1.0 / GATE_NORM).then_inc(exps, 1)
                nc.scalar.activation(exp_last[:, h, :], bk[:, h, CHUNK - 1:SEQ:CHUNK], ACT.Exp,
                                     scale=1.0 / GATE_NORM).then_inc(exps, 1)
                act.wait_ge(prods, 4 * h + 2)
                nc.scalar.activation(exp_a, gate_t, ACT.Exp, scale=1.0 / GATE_NORM).then_inc(exps, 1)

            def to_sbuf(dst, b):
                nc.scalar.copy(dst, bank[b][:, :]).then_inc(gla_evac, 1)

            step(0)
            nc.scalar.copy(a_t, bank[0][0:RANK, :]).then_inc(gla_evac, 1)
            step(1, 8, P)
            to_sbuf(qm_g[:, 0, :], 2)
            gate(0)
            step(2)
            to_sbuf(qm_g[:, 1, :], 0)
            to_sbuf(qm_g[:, 2, :], 1)
            gate(1)
            step(3)
            to_sbuf(qm_g[:, 3, :], 2)
            gate(2)
            exps_of(0, 0)
            for j in range(8):
                if j < 6:
                    step(4 + j)
                else:
                    act.wait_ge(w_used, GLA_N + 4 + j + 1)
                for t in range(2):
                    to_sbuf(qkv[:, 2 * j + t, :], 2 * (j % 2) + t)
                if j >= 6:
                    step(4 + j)
                if j % 2:
                    probs_back(0, j // 2)
                    if j == 1:
                        gate(3)
                elif j:
                    mo_hi_copy(0, j // 2 - 1)
                    exps_of(0, j // 2)
                if j >= 3 and j < 7:
                    decays(j - 3)
            for e in range(8):
                if e == 6:
                    mo_hi_copy(0, 3)
                act.wait_ge(vt_mm, e + 1)
                nc.scalar.copy(v_tok[:, :, e * P:(e + 1) * P],
                               bank[V_BANK[e]][:, :].rearrange("p (b e) -> p b e", b=TB)).then_inc(v_evac, 1)

            def kd_evac(h):
                act.wait_ge(kdt_mm, h + 1)
                nc.scalar.copy(bk[:, h, :], bank[4][:, :]).then_inc(kdt_evac, 1)

            kd_evac(0)
            for h in range(HEADS):
                if h + 1 < HEADS:
                    kd_evac(h + 1)
                for e, tmp in ((0, exp_a), (1, exp_b)):
                    b = bank[2 * (h % 2) + e][:, :]
                    act.wait_ge(o_mm, 2 * h + e + 1)
                    nc.scalar.copy(u[:, 2 * h + e, :], b).then_inc(o_read, 1)
                    if h:
                        act.wait_ge(ss_done, h)
                    nc.scalar.activation(tmp, b, ACT.Square).then_inc(o_read, 1)
            for j in range(4):
                step(12 + j, 8 if j < 2 else A_K)
                for t in range(2):
                    nc.scalar.activation(r_act[:, 2 * j + t, :], bank[2 * (j % 2) + t][:, :], ACT.Silu).then_inc(gla_evac, 1)
                for k in (range(0, 4) if j == 2 else range(4, 8) if j == 3 else ()):
                    if k == 6:
                        split_hi(GLA_OUT_N // 2 + 1, 0, B_K)
                    act.wait_ge(y_ready, k + 1)
                    nc.scalar.copy(y_hi[:, k, :], u[:, k, :]).then_inc(y_hi_done, 1)
            out_proj(LN_GLA_OUT, GLA_OUT_N)
            ffn(1)
            ffn(2)

            t0 = CONV_N // 2

            def conv_step(j, kc=8):
                act.wait_ge(w_used, CONV_N + j + 1)
                split_hi(t0 + (j + 2) // 2, j % 2, kc)

            def diag_hi(g):
                act.wait_ge(w_used, DIAG_N + g - 1)
                for j in range(TAPS_K[g]):
                    for t in range(2):
                        w = w_tap_hi[:, t * WIDTH + 8 * g + j:t * WIDTH + 8 * g + j + 1].bitcast(F32)
                        last = nc.scalar.activation(whi[:, g % 2, j, t * P:(t + 1) * P], ident[:, :], ACT.Copy, scale=w)
                last.then_inc(hi_ready, 1)

            def tap_products(i):
                if i == 1:
                    act.wait_ge(glu_done, DK)
                elif i > 1:
                    act.wait_ge(tap_add, 2 * (i - 1))
                for t in range(2):
                    c, j = 4 + t, DVE_TAPS[2] + i
                    if i == 0:
                        act.wait_ge(scores_mm, 2 * HEADS + 4)
                        act.wait_ge(glu_done, DK)
                    nc.scalar.activation(tap_sum[t] if i == 0 else act_out[t], conv_in[:, c, j:j + SEQ], ACT.Copy,
                                         scale=w_dw[:, c * WIDTH + j:c * WIDTH + j + 1]).then_inc(tap_mul, 1)

            def a_copies(i):
                for t in range(2):
                    nc.scalar.copy(conv_in[:, 2 * i + t, PAD:PAD + SEQ], bank[t][:, :]).then_inc(conv_evac, 1)

            def sigmoids(i):
                if i:
                    act.wait_ge(glu_done, 2 * i)
                for t in range(2):
                    nc.scalar.activation(act_out[t], bank[2 + t][:, :], ACT.Sigmoid).then_inc(conv_evac, 1)

            for i in range(2):
                conv_step(2 * i)
                a_copies(i)
                conv_step(2 * i + 1)
                sigmoids(i)
            for c in range(2):
                conv_step(4 + c)
                for t in range(2):
                    nc.scalar.copy(qm_c[:, 2 * c + t, :], bank[2 * c + t][:, :]).then_inc(conv_evac, 1)
            exps_of(1, 0)
            conv_step(6)
            a_copies(3)
            probs_back(1, 0)
            shift_copy(LN_CONV)
            conv_step(7)
            sigmoids(2)
            mo_hi_copy(1, 0)
            exps_of(1, 1)
            for t in range(2):
                act.wait_ge(glu_done, 4 + t + 1)
                nc.scalar.copy(cin_hi[:, t, :], conv_in[:, PE_C + t, :]).then_inc(cin_hi_done, 1)
            diag_hi(0)
            a_copies(2)
            probs_back(1, 1)
            act.wait_ge(w_used, DIAG_N)
            sigmoids(3)
            diag_hi(1)
            mo_hi_copy(1, 1)
            exps_of(1, 2)
            squares(LN_CONV, 0)
            tap_products(0)
            tap_products(1)
            diag_hi(2)
            probs_back(1, 2)
            squares(LN_CONV, 1)
            tap_products(2)
            diag_hi(3)
            mo_hi_copy(1, 2)
            exps_of(1, 3)
            tap_products(3)
            split_hi(CONV_OUT_N // 2, 0, A_K)
            tap_products(4)
            probs_back(1, 3)
            split_hi(CONV_OUT_N // 2, 1, A_K)
            for t in range(2):
                c = PE_C + t
                nc.scalar.activation(u[:, c, :], bank[2 + t][:, :], ACT.Identity,
                                     bias=prm[:, ROW_BDW + c:ROW_BDW + c + 1]).then_inc(conv_evac, 1)
            mo_hi_copy(1, 3)
            squares(LN_CONV, 2)
            split_hi(CONV_OUT_N // 2 + 1, 0, B_K)
            squares(LN_CONV, 3)
            split_hi(CONV_OUT_N // 2 + 1, 1, B_K)
            affine(LN_CONV, c_hi, ROW_CG, ROW_CB, ACT.Silu)
            out_proj(LN_CONV_OUT, CONV_OUT_N)
            ffn(3)
            ln = LN_FFN[3]
            for k in range(DK + 1):
                if k < DK:
                    g, b = ROW_G + LN_ROW[ln] * DK + k, ROW_B + LN_ROW[ln] * DK + k
                    act.wait_ge(normed, 8 * ln + k + 1)
                    nc.scalar.activation(u[:, k, :], u[:, k, :], ACT.Identity, scale=prm[:, g:g + 1],
                                         bias=prm[:, b:b + 1]).then_inc(affine_done, 1)
                if k:
                    j = k - 1
                    act.wait_ge(fin_mm, j + 1)
                    if j >= 4:
                        act.wait_ge(out_stored[j % 4], 16)
                    nc.scalar.copy(out_tok[:, j % 4, :, :],
                                   bank[j % 4][:, :].rearrange("p (b e) -> p b e", b=TB)).then_inc(fin_evac, 1)

        @block.vector
        def _(dve):
            def split_lo(n, s, kc=8, width=256):
                dve.wait_ge(hi_ready, n + 1)
                if n:
                    dve.wait_ge(lo_ready, n)
                nc.vector.tensor_tensor(wlo[:, s, 0:kc, 0:width], raw[:, s, 0:kc, 0:width],
                                        whi[:, s, 0:kc, 0:width].bitcast(F32), ALU.subtract).then_inc(lo_ready, 1)

            def ffn_pair(f, i):
                for t in range(2):
                    dve.wait_ge(w_used, FFN_N[f] + 2 * i + 2)
                    dve.wait_ge(silu_done, FK * f + 2 * i + t + 1)
                    nc.vector.tensor_tensor(act_out[t], act_out[t], bank[2 + t][:, :], ALU.mult).then_inc(mul_done, 1)
                for t in range(2):
                    dve.wait_ge(h_hi_done, FK * f + 2 * i + t + 1)
                    nc.vector.tensor_tensor(h_lo[:, bass.ds(2 * i + t, 1), :], act_out[t].rearrange("p (a s) -> p a s", a=1),
                                            h_hi[:, bass.ds(2 * i + t, 1), :].bitcast(F32),
                                            ALU.subtract).then_inc(h_done, 1)

            def blk(x, d):
                return x[:, bass.ds(d, 1), :].rearrange("p a s -> p (a s)")

            def add_sum(ln, d):
                dve.wait_ge(y_evac, 8 * ln + d + 1)
                if isinstance(d, int) and d == 1:
                    dve.wait_ge(u0_ready, ln + 1)
                    nc.vector.tensor_tensor(usum, u[:, 0, :], u[:, 1, :], ALU.add).then_inc(u_acc, 1)
                else:
                    dve.wait_ge(u_acc, 6 * ln + d - 1)
                    nc.vector.tensor_tensor(usum, usum, blk(u, d), ALU.add).then_inc(u_acc, 1)

            def add_square(ln, d, t):
                dve.wait_ge(sq_done, 8 * ln + d + 1)
                if isinstance(d, int) and d == 1:
                    nc.vector.tensor_tensor(qsum, sq[0], sq[1], ALU.add).then_inc(q_acc, 1)
                else:
                    dve.wait_ge(q_acc, 6 * ln + d - 1)
                    nc.vector.tensor_tensor(qsum, qsum, sq[t], ALU.add).then_inc(q_acc, 1)

            def take_shift(ln):
                dve.wait_ge(y_evac, 8 * ln + 1)
                dve.wait_ge(shift_ready, ln + 1)
                nc.vector.tensor_tensor(u[:, 0, :], u[:, 0, :], shift, ALU.subtract).then_inc(u0_ready, 1)

            def residual_pair(ln, p, n_used, coef, b0=0, last=False):
                for t in range(2):
                    d = 2 * p + t
                    first = isinstance(d, int) and d == 0
                    if t == 1 and not (isinstance(p, int) and p == 0):
                        add_square(ln, d - 1, 0)
                    res = RES_BASE[ln] + RES_PER[ln] * d
                    src = u if RES_PER[ln] == 1 else xlo[:, :, :].bitcast(F32)
                    if first:
                        nc.vector.tensor_scalar(u[:, 0, :], src[:, 0, :], ALPHA, None, ALU.mult).then_inc(res_done, 1)
                    else:
                        nc.vector.scalar_tensor_tensor(out=blk(u, d), in0=blk(src, d), scalar=ALPHA, in1=shift,
                                                       op0=ALU.mult, op1=ALU.subtract).then_inc(res_done, 1)
                    dve.wait_ge(res_done, res + 1)
                    if RES_PER[ln] == 2:
                        nc.vector.scalar_tensor_tensor(out=blk(u, d), in0=blk(xhi[:, :, :].bitcast(F32), d), scalar=ALPHA,
                                                       in1=blk(u, d), op0=ALU.mult, op1=ALU.add).then_inc(res_done, 1)
                        dve.wait_ge(res_done, res + 2)
                    if t == 0:
                        dve.wait_ge(y_even, EVEN_BASE[ln] + p + 1)
                    else:
                        dve.wait_ge(w_used, n_used)
                    nc.vector.scalar_tensor_tensor(out=blk(u, d), in0=bank[b0 + t][:, :], scalar=coef, in1=blk(u, d),
                                                   op0=ALU.mult, op1=ALU.add).then_inc(y_evac, 1)
                    if first:
                        take_shift(ln)
                    elif not (last and t == 1):
                        add_sum(ln, d)
                if not last:
                    add_square(ln, 2 * p + 1, 1)

            def residual_ffn(ln, n0):
                residual_pair(ln, 0, n0 + 4, 0.5)
                with dve.Fori(1, 3) as p:
                    residual_pair(ln, p, n0 + 4 * p + 4, 0.5)
                residual_pair(ln, 3, n0 + 16, 0.5, last=True)

            def residual_out(ln, n0):
                for p in range(4):
                    residual_pair(ln, p, n0 + 4 * (p // 2) + 3 + p % 2, 1.0, b0=2 * (p % 2), last=p == 3)
                    if p == 1:
                        split_lo(n0 + 6, 0)

            def diagonal(to, values, b):
                return nc.vector.tensor_scalar(to[:, b * P:(b + 1) * P], ident[:, :], values[:, b:b + 1], None, ALU.mult)

            def diagonals(to, values, done):
                for b in range(TB):
                    last = diagonal(to, values, b)
                last.then_inc(done, 1)

            def norm(ln):
                dve.wait_ge(stats_mm, ln + 1)
                nc.vector.tensor_scalar(mean_sq, bank[5][:, 0:8], 1.0 / D, None, ALU.mult).then_inc(stat_step, 1)
                dve.wait_ge(stat_step, 3 * ln + 1)
                nc.vector.tensor_tensor(sq_mean, mean_sq[:, 0:TB], mean_sq[:, 0:TB], ALU.mult).then_inc(stat_step, 1)
                diagonal(diag_mean, mean_sq, 0)
                dve.wait_ge(stat_step, 3 * ln + 2)
                nc.vector.tensor_tensor(var, mean_sq[:, TB:2 * TB], sq_mean, ALU.subtract).then_inc(stat_step, 1)
                diagonal(diag_mean, mean_sq, 1)
                dve.wait_ge(stat_step, 3 * ln + 3)
                nc.vector.tensor_scalar(var, var, 0.0, LN_EPS, ALU.max, ALU.add).then_inc(var_ready, 1)
                diagonal(diag_mean, mean_sq, 2)
                diagonal(diag_mean, mean_sq, 3).then_inc(mean_diag, 1)
                dve.wait_ge(rs_ready, ln + 1)
                diagonals(diag_rstd, rs, rstd_diag)

                def centre(k):
                    nc.vector.tensor_tensor(u[:, k, :], u[:, k, :], bank[6][:, :], ALU.subtract).then_inc(centred, 1)

                def scale(k):
                    dve.wait_ge(centred, 8 * ln + k + 1)
                    nc.vector.tensor_tensor(u[:, k, :], u[:, k, :], bank[7][:, :], ALU.mult).then_inc(normed, 1)

                dve.wait_ge(bcast_mm, 2 * ln + 1)
                centre(0)
                centre(1)
                dve.wait_ge(bcast_mm, 2 * ln + 2)
                for k in range(DK):
                    scale(k)
                    if k + 2 < DK:
                        centre(k + 2)

            def ffn(f):
                ffn_pair(f, 0)
                with dve.Fori(1, FK // 2) as i:
                    ffn_pair(f, i)
                residual_ffn(LN_FFN[f], FFN_N[f] + FK)
                norm(LN_FFN[f])

            def maxima(m, h):
                g = HEADS * m + h
                for j in range(2):
                    dve.wait_ge(scores_mm, 2 * g + j + 1)
                    nc.vector.tensor_reduce(row_max[:, 2 * j:2 * j + 2],
                                            bank[4 + j][:, :].rearrange("p (b m) -> p b m", b=2),
                                            AX_X, ALU.max).then_inc(max_done, 1)
                dve.wait_ge(max_done, 2 * g + 2)
                nc.vector.tensor_scalar(neg_max, row_max, -MEM_SCALE, None, ALU.mult).then_inc(neg_max_done, 1)

            def normalise(m, h):
                g = HEADS * m + h
                probs = pp_of[m][:, 0:1024].rearrange("p (b m) -> p b m", b=TB)
                dve.wait_ge(p_exp, 4 * g + 4)
                nc.vector.reciprocal(inv_sum, row_sum).then_inc(inv_done, 1)
                dve.wait_ge(inv_done, g + 1)
                for b in range(TB):
                    nc.vector.tensor_scalar(probs[:, b, :], probs[:, b, :], inv_sum[:, b:b + 1], None,
                                            ALU.mult).then_inc(p_norm, 1)

            def probs_back(m, h):
                g = HEADS * m + h
                probs_t = pp_of[m][:, 1024:2048].rearrange("p (b s) -> p b s", b=MB)
                dve.wait_ge(pt_mm, 2 * g + 2)
                if g:
                    dve.wait_ge(mo_mm, g)
                nc.vector.tensor_copy(probs_t[:, 1, :], bank[7][:, :]).then_inc(pt_evac, 1)

            def mo_lo_part(m, h):
                dve.wait_ge(mo_hi_done, HEADS * m + h + 1)
                nc.vector.tensor_tensor(mo_lo_of[m][:, h, :], bank[7][:, :], mo_hi_of[m][:, h, :].bitcast(F32),
                                        ALU.subtract).then_inc(mo_done, 1)

            for n in range(10):
                split_lo(n, n % 2)
            ffn(0)
            split_lo(GLA_N + 1, 1, 8, P)

            dve.wait_ge(x_ready, 8 * (LN_FFN[0] + 2))
            nc.vector.memset(reset, 1.0).then_inc(reset_done, 1)
            dve.wait_ge(reset_done, 1)
            nc.vector.memset(reset[:, 0:SEQ:CHUNK], 0.0).then_inc(gate_chain, 1)

            def gate(h):
                dve.wait_ge(gate_act, 3 * h + 3)
                nc.vector.tensor_scalar(gate_t, bank[Z_BANK[h]][:, :], prm[:, ROW_GATE + h:ROW_GATE + h + 1], 0.0,
                                        ALU.add, ALU.min).then_inc(gate_chain, 1)
                dve.wait_ge(gate_chain, 3 * h + 2)
                nc.vector.tensor_tensor(gate_t, gate_t, exp_a, ALU.subtract).then_inc(gate_chain, 1)
                dve.wait_ge(gate_chain, 3 * h + 3)
                nc.vector.tensor_tensor_scan(bk[:, h, :], reset, gate_t, 0.0, ALU.mult, ALU.add).then_inc(gate_chain, 1)

            def decayed(h):
                dve.wait_ge(gate_chain, 3 * HEADS + 1)
                if h == 0:
                    dve.wait_ge(gla_evac, 5 + 8)
                else:
                    dve.wait_ge(exps, 4 * h)
                b_h = bk[:, h, :].rearrange("p (c s) -> p c s", s=CHUNK)
                nc.vector.tensor_tensor(gate_t.rearrange("p (c s) -> p c s", s=CHUNK),
                                        b_h[:, :, CHUNK - 1:CHUNK].to_broadcast([P, NCH, CHUNK]), b_h,
                                        ALU.subtract).then_inc(prods, 1)
                dve.wait_ge(exps, 4 * h + 1)
                nc.vector.scalar_tensor_tensor(out=qkv[:, h, :], in0=qkv[:, h, :], scalar=GLA_SCALE, in1=exp_a,
                                               op0=ALU.mult, op1=ALU.mult).then_inc(prods, 1)
                dve.wait_ge(exps, 4 * h + 2)
                nc.vector.tensor_tensor(ke[:, h, :], qkv[:, 4 + h, :], exp_b, ALU.mult).then_inc(prods, 1)
                dve.wait_ge(exps, 4 * h + 4)
                nc.vector.tensor_tensor(qkv[:, 4 + h, :], qkv[:, 4 + h, :], exp_a, ALU.mult).then_inc(prods, 1)

            gate(0)
            gate(1)
            gate(2)
            for h in range(HEADS):
                maxima(0, h)
                normalise(0, h)
                if h == 2:
                    decayed(1)
                elif h == 3:
                    decayed(3)
                probs_back(0, h)
                if h == 0:
                    gate(3)
                elif h == 1:
                    decayed(0)
                elif h == 2:
                    decayed(2)
                mo_lo_part(0, h)
            dve.wait_ge(gla_masks, 3)
            dve.wait_ge(vt_mm, 8)
            for t in range(2):
                nc.vector.memset(att[t], 0.0).then_inc(att_clear, 1)
            dve.wait_ge(att_clear, 2)

            def mask_att(h):
                dve.wait_ge(att_mm, h + 1)
                if h >= 2:
                    dve.wait_ge(o_mm, 2 * (h - 1))
                nc.vector.copy_predicated(att[h % 2], att_mask.rearrange("p (b i) -> p b i", b=TB).bitcast(I32),
                                          bank[5][:, :].rearrange("p (b i) -> p b i", b=TB)).then_inc(att_evac, 1)

            mask_att(0)
            for h in range(HEADS):
                s_h = states[:, h % 2, :, :]
                for c in range(7):
                    dve.wait_ge(ds_mm, 2 * h + c // 4 + 1)
                    if h >= 2 and c == 0:
                        dve.wait_ge(o_mm, 2 * (h - 1))
                    add = bank[6 + c % 2][:, (c // 2 % 2) * 256:(c // 2 % 2) * 256 + 256]
                    if c == 0:
                        nc.vector.tensor_copy(s_h[:, 0, :], add).then_inc(state_done, 1)
                    else:
                        dve.wait_ge(state_done, 7 * h + c)
                        nc.vector.scalar_tensor_tensor(out=s_h[:, c, :], in0=s_h[:, c - 1, :],
                                                       scalar=exp_last[:, h, c:c + 1], in1=add,
                                                       op0=ALU.mult, op1=ALU.add).then_inc(state_done, 1)
                if h + 1 < HEADS:
                    mask_att(h + 1)
                dve.wait_ge(o_read, 4 * h + 4)
                nc.vector.tensor_tensor(ke[:, h, :], exp_a, exp_b, ALU.add).then_inc(ss_done, 1)
            dve.wait_ge(rms_mm, 1)
            nc.vector.tensor_scalar(rms_v, bank[4][:, 0:16], 1.0 / 256, RMS_EPS, ALU.mult, ALU.add).then_inc(rms_var, 1)
            dve.wait_ge(rms_rs, 1)
            for h in range(HEADS):
                diagonals(ke[:, h, :], rms_r[:, TB * h:TB * h + TB], rms_diag)
            for h in range(HEADS):
                dve.wait_ge(rms_bcast, h + 1)
                for k in (2 * h, 2 * h + 1):
                    g = ROW_ONORM + k % 2
                    nc.vector.scalar_tensor_tensor(out=u[:, k, :], in0=u[:, k, :], scalar=prm[:, g:g + 1],
                                                   in1=bank[4 + h][:, :], op0=ALU.mult, op1=ALU.mult).then_inc(y_scaled, 1)
                for k in (2 * h, 2 * h + 1):
                    dve.wait_ge(y_scaled, k + 1)
                    dve.wait_ge(gla_evac, 21 + k + 1)
                    nc.vector.tensor_tensor(u[:, k, :], u[:, k, :], r_act[:, k, :], ALU.mult).then_inc(y_ready, 1)
                for k in (2 * h, 2 * h + 1):
                    dve.wait_ge(y_hi_done, k + 1)
                    nc.vector.tensor_tensor(y_lo[:, k, :], u[:, k, :], y_hi[:, k, :].bitcast(F32),
                                            ALU.subtract).then_inc(y_done, 1)
            split_lo(GLA_OUT_N + 2, 0)
            residual_out(LN_GLA_OUT, GLA_OUT_N)
            norm(LN_GLA_OUT)
            split_lo(FFN_N[1] + 1, 1)
            ffn(1)
            split_lo(FFN_N[2] + 1, 1)
            ffn(2)
            split_lo(CONV_N + 1, 1)

            def taps(i, between):
                dve.wait_ge(glu_done, 2 * i + 2 if i < 2 else DK)
                for j in range(DVE_TAPS[i]):
                    for t in range(2):
                        c = 2 * i + t
                        src = conv_in[:, c, j:j + SEQ]
                        w = w_dw[:, c * WIDTH + j:c * WIDTH + j + 1]
                        if j == 0:
                            nc.vector.tensor_scalar(u[:, c, :], src, w, prm[:, ROW_BDW + c:ROW_BDW + c + 1],
                                                    ALU.mult, ALU.add).then_inc(taps_done, 1)
                        else:
                            dve.wait_ge(taps_done, 2 * WIDTH * i + 2 * (j - 1) + t + 1)
                            nc.vector.scalar_tensor_tensor(out=u[:, c, :], in0=src, scalar=w, in1=u[:, c, :],
                                                           op0=ALU.mult, op1=ALU.add).then_inc(taps_done, 1)
                    for step, *which in between.get(j, ()):
                        step(*which)

            def take_out_shift(i):
                for t in range(2):
                    d = 2 * i + t
                    if d == 0:
                        take_shift(LN_CONV)
                        continue
                    nc.vector.tensor_tensor(u[:, d, :], u[:, d, :], shift, ALU.subtract).then_inc(y_evac, 1)
                    if d < DK - 1:
                        add_sum(LN_CONV, d)

            def add_squares(i):
                if i:
                    add_square(LN_CONV, 2 * i, 0)
                if i < 3:
                    add_square(LN_CONV, 2 * i + 1, 1)

            dve.wait_ge(x_ready, 8 * (LN_FFN[2] + 2))
            dve.wait_ge(conv_pad, 1)
            taps(0, {27: [(maxima, 1, 0)], 30: [(normalise, 1, 0)]})
            dve.wait_ge(taps_done, 2 * WIDTH)
            dve.sem_inc(y_evac, 1)
            taps(1, {14: [(mo_lo_part, 1, 0), (maxima, 1, 1)], 17: [(normalise, 1, 1)]})
            dve.wait_ge(taps_done, 4 * WIDTH)
            mo_lo_part(1, 1)
            maxima(1, 2)
            take_out_shift(0)
            take_out_shift(1)
            normalise(1, 2)
            taps(2, {4: [(add_squares, 0)], 10: [(add_squares, 1), (mo_lo_part, 1, 2), (maxima, 1, 3)],
                     13: [(normalise, 1, 3)], 23: [(mo_lo_part, 1, 3)]})
            dve.wait_ge(taps_done, 2 * sum(DVE_TAPS))
            dve.wait_ge(tap_add, 8)
            for t in range(2):
                nc.vector.tensor_tensor(u[:, 4 + t, :], u[:, 4 + t, :], tap_sum[t], ALU.add).then_inc(taps_done, 1)
            dve.wait_ge(taps_done, 2 * sum(DVE_TAPS) + 2)
            take_out_shift(2)
            dve.wait_ge(conv_evac, 22)
            take_out_shift(3)
            add_squares(2)
            add_squares(3)
            norm(LN_CONV)
            dve.wait_ge(x_ready, 8 * (LN_CONV + 2))
            residual_out(LN_CONV_OUT, CONV_OUT_N)
            norm(LN_CONV_OUT)
            split_lo(FFN_N[3] + 1, 1)
            ffn(3)

        @block.tensor
        def _(pe):
            def mm3(to, s, k, t, hi, lo, start, stop):
                w = slice(t * P, t * P + P)
                nc.tensor.matmul(to, whi[:, s, k, w], hi, start=start, stop=False)
                nc.tensor.matmul(to, whi[:, s, k, w], lo, start=False, stop=False)
                return nc.tensor.matmul(to, wlo[:, s, k, w], hi, start=False, stop=stop)

            def chunk(n, s, banks, ready=None):
                pe.wait_ge(lo_ready, n + 1)
                if ready is not None:
                    last = by_halves(s, banks, xhi, xlo, ready, True)
                else:
                    for k in range(DK):
                        for t, b in enumerate(banks):
                            last = mm3(bank[b][:, :], s, k, t, xhi[:, k, :], xlo[:, k, :], k == 0, k == DK - 1)
                last.then_inc(w_used, 1)

            def by_halves(s, banks, hi, lo, ready, start):
                for k in range(DK + 1):
                    if k < DK:
                        pe.wait_ge(x_hi_ready, ready + k + 1)
                        for t, b in enumerate(banks):
                            for half in (whi, wlo):
                                nc.tensor.matmul(bank[b][:, :], half[:, s, k, t * P:t * P + P], hi[:, k, 0:SEQ],
                                                 start=(start and k == 0 and half is whi), stop=False)
                    if k:
                        pe.wait_ge(x_ready, ready + k)
                        for t, b in enumerate(banks):
                            last = nc.tensor.matmul(bank[b][:, :], whi[:, s, k - 1, t * P:t * P + P], lo[:, k - 1, :],
                                                    start=False, stop=(k == DK))
                            if k == DK and t == 0 and not start:
                                last.then_inc(y_even, 1)
                return last

            def ffn_pair(f, i, between=None):
                n = FFN_N[f] + 2 * i
                if not isinstance(i, int):
                    pe.wait_ge(silu_done, FK * f + 2 * i)
                chunk(n, 0, (0, 1), 8 * (LN_FFN[f] if f else 0) if isinstance(i, int) else None)
                if between is not None:
                    between()
                if not isinstance(i, int):
                    pe.wait_ge(mul_done, FK * f + 2 * i)
                chunk(n + 1, 1, (2, 3))

            def down_pair(f, p):
                ln, n = LN_FFN[f], FFN_N[f] + FK + 4 * p
                first = isinstance(p, int)
                k0 = 0
                for c, kc in enumerate(DOWN_K):
                    pe.wait_ge(lo_ready, n + c + 1)
                    if first and p == 0:
                        pe.wait_ge(h_done, FK * f + k0 + kc)
                        if c == 0:
                            pe.wait_ge(silu_done, FK * (f + 1))
                    for t in range(2):
                        if c == 0 and not (first and p == 0):
                            pe.wait_ge(y_evac, 8 * ln + 2 * p - 1 + t)
                        for k in range(k0, k0 + kc):
                            if first and p == 3 and t == 1 and k == FK - 1:
                                sums_u(ln)
                            last = mm3(bank[t][:, :], c % 2, k - k0, t, h_hi[:, k, :], h_lo[:, k, :], k == 0, k == FK - 1)
                        if t == 1:
                            last.then_inc(w_used, 1)
                        elif c == len(DOWN_K) - 1:
                            last.then_inc(y_even, 1)
                    k0 += kc

            def shift_sum(ln):
                pe.wait_ge(y_evac, 8 * ln + 1)
                nc.tensor.matmul(bank[4][:, :], ones[:, :], u[:, 0, :], start=True, stop=True).then_inc(shift_mm, 1)

            def column_sums(c0, x, start, stop):
                for b in range(TB):
                    last = nc.tensor.matmul(bank[5][:, c0 + b:c0 + b + 1], x[:, b * P:(b + 1) * P], ones[:, 0:1],
                                            start=(start and b == 0), stop=(stop and b == TB - 1), skip_group_check=True)
                return last

            def keep_busy(count, w=xhi[:, 0, 0:P], x=xhi[:, 0, :]):
                for _ in range(count):
                    nc.tensor.matmul(bank[4][:, :], w, x, start=True, stop=True)

            def sums_u(ln):
                pe.wait_ge(u_acc, 6 * ln + 6)
                column_sums(0, usum, True, False)

            def stats(ln, n):
                pe.wait_ge(q_acc, 6 * ln + 6)
                column_sums(TB, qsum, False, False)
                keep_busy(2)
                pe.wait_ge(y_evac, 8 * ln + 8)
                column_sums(0, u[:, DK - 1, :], False, False)
                keep_busy(1)
                pe.wait_ge(sq_done, 8 * ln + 8)
                column_sums(TB, sq[1], False, True).then_inc(stats_mm, 1)
                keep_busy(2)
                pe.wait_ge(mean_diag, ln + 1)
                nc.tensor.matmul(bank[6][:, :], ones[:, :], diag_mean, start=True, stop=True).then_inc(bcast_mm, 1)
                pe.wait_ge(rstd_diag, ln + 1)
                nc.tensor.matmul(bank[7][:, :], ones[:, :], diag_rstd, start=True, stop=True).then_inc(bcast_mm, 1)
                if n is not None:
                    pe.wait_ge(lo_ready, n + 1)
                    keep_busy(4, whi[:, 0, 0, 0:P], whi[:, 0, 0:2, :])

            def ffn(f, between=None):
                ffn_pair(f, 0, between)
                with pe.Fori(1, FK // 2) as i:
                    ffn_pair(f, i)
                down_pair(f, 0)
                shift_sum(LN_FFN[f])
                with pe.Fori(1, 3) as p:
                    down_pair(f, p)
                down_pair(f, 3)
                stats(LN_FFN[f], (GLA_N, FFN_N[2], CONV_N, None)[f])

            def out_a(ln, n0, p, m, mo_hi, mo_lo):
                n, b0 = n0 + 4 * (p // 2) + p % 2, 2 * (p % 2)
                pe.wait_ge(lo_ready, n + 1)
                pe.wait_ge(mo_done, HEADS * (m + 1))
                if p >= 2:
                    pe.wait_ge(y_evac, 8 * ln + 2 * (p - 2) + 2)
                for t in range(2):
                    for k in range(A_K):
                        last = mm3(bank[b0 + t][:, :], p % 2, k, t, mo_hi[:, k, :], mo_lo[:, k, :], k == 0, False)
                last.then_inc(w_used, 1)

            def out_b(ln, n0, p, y_h, y_l, base):
                n, b0 = n0 + 4 * (p // 2) + 2 + p % 2, 2 * (p % 2)
                pe.wait_ge(lo_ready, n + 1)
                if p == 0 and base is not None:
                    by_halves(0, (0, 1), y_h, y_l, base, False).then_inc(w_used, 1)
                    return
                for t in range(2):
                    for k in range(B_K):
                        if p == 0 and t == 0:
                            pe.wait_ge(y_done, k + 1)
                        if p == 3 and t == 1 and k == B_K - 1:
                            sums_u(ln)
                        last = mm3(bank[b0 + t][:, :], p % 2, k, t, y_h[:, k, :], y_l[:, k, :], False, k == B_K - 1)
                    last.then_inc(w_used if t else y_even, 1)

            def scores(m, h):
                g = HEADS * m + h
                kt = kv_of[m][:, 0:1024].rearrange("p (h m) -> p h m", h=HEADS)
                pe.wait_ge(kv_loaded, 16 * (m + 1))
                if g:
                    pe.wait_ge(p_exp, 4 * g)
                for b in range(TB):
                    last = nc.tensor.matmul(bank[4 + b // 2][:, (b % 2) * 256:(b % 2) * 256 + 256],
                                            qm_of[m][:, h, b * P:(b + 1) * P], kt[:, h, :], start=True, stop=True)
                    if b % 2:
                        last.then_inc(scores_mm, 1)

            def transposes(m, h):
                g = HEADS * m + h
                probs = pp_of[m][:, 0:1024].rearrange("p (b m) -> p b m", b=TB)
                pe.wait_ge(p_norm, 4 * g + 4)
                if g:
                    pe.wait_ge(pt_evac, 2 * g)
                    pe.wait_ge(mo_done, g)
                for j in range(MB):
                    for b in range(TB):
                        last = nc.tensor.transpose(bank[6 + j][:, b * P:(b + 1) * P],
                                                   probs[:, b, j * P:(j + 1) * P], ident[:, :])
                    last.then_inc(pt_mm, 1)

            def outputs(m, h):
                g = HEADS * m + h
                v = kv_of[m][:, 1024:2048].rearrange("p (b e) -> p b e", b=MB)
                probs_t = pp_of[m][:, 1024:2048].rearrange("p (b s) -> p b s", b=MB)
                pe.wait_ge(pt_evac, 2 * g + 2)
                for j in range(MB):
                    last = nc.tensor.matmul(bank[7][:, :], v[:, j, h * P:(h + 1) * P], probs_t[:, j, :],
                                            start=(j == 0), stop=(j == MB - 1))
                last.then_inc(mo_mm, 1)

            pe.wait_ge(consts, 3)
            pe.wait_ge(mem_loaded, 16)
            for k in range(DK):
                if k >= 4:
                    pe.wait_ge(mem_hi_ready, 2 * (k - 4) + 1)
                for b in range(MB):
                    last = nc.tensor.transpose(bank[4 + k % 4][:, b * P:(b + 1) * P], mem_in[:, b, k * P:(k + 1) * P], ident[:, :])
                last.then_inc(tr_done, 1)

            def x_part(k0):
                pe.wait_ge(x_loaded, 16)
                for k in range(k0, k0 + 4):
                    if k < 4:
                        pe.wait_ge(mem_hi_ready, 2 * (k + 4) + 1)
                    else:
                        pe.wait_ge(tr_evac, k - 3)
                    for b in range(TB):
                        last = nc.tensor.transpose(bank[4 + k % 4][:, b * P:(b + 1) * P], xin[:, b, k * P:(k + 1) * P], ident[:, :])
                    last.then_inc(tr_done, 1)

            def parameters():
                pe.wait_ge(rows_loaded, 16 * 8)
                pe.wait_ge(tr_evac, 5)
                nc.tensor.transpose(bank[4][:, 0:ROWS], rows_in[:, :], ident[0:ROWS, 0:ROWS]).then_inc(tr_done, 1)
                pe.wait_ge(tr_evac, 6)
                for k in range(DK):
                    last = nc.tensor.transpose(bank[5][:, k * WIDTH:(k + 1) * WIDTH], dw_in[:, k * P:(k + 1) * P],
                                               ident[0:WIDTH, 0:WIDTH])
                last.then_inc(tr_done, 1)

            for n in range(8):
                pe.wait_ge(lo_ready, n + 1)
                if n >= 2:
                    pe.wait_ge(kv_evac, 2 * (n - 1))
                for k in range(DK):
                    if n == 0:
                        pe.wait_ge(mem_ready, k + 1)
                    for t in range(2):
                        last = mm3(bank[2 * (n % 2) + t][:, 0:NMEM], n % 2, k, t, mem_hi[:, k, :], mem_lo[:, k, :], k == 0, k == DK - 1)
                last.then_inc(w_used, 1)
                if n < 2:
                    x_part(4 * n)
                if n == 2:
                    parameters()
            def kv_values():
                pe.wait_ge(kv_evac, 16)
                pe.wait_ge(tr_evac, 10)
                for layer in range(DEPTH):
                    for j in range(MB):
                        for h in range(HEADS):
                            last = nc.tensor.transpose(bank[4 + 2 * layer + j][:, h * P:(h + 1) * P],
                                                       kv_t[:, layer, 4 + h, j * P:(j + 1) * P], ident[:, :])
                        last.then_inc(kvv_done, 1)

            pe.wait_ge(kv_evac, 14)
            ffn(0, kv_values)

            n0 = GLA_N

            def gate(h):
                nc.tensor.matmul(bank[Z_BANK[h]][:, :], w_gate2[:, h * P:(h + 1) * P], a_t, start=True, stop=True).then_inc(z_mm, 1)

            def qkv_chunk(j):
                pe.wait_ge(gla_evac, (4, 5)[j] if j < 2 else 5 + 2 * (j - 1))
                chunk(n0 + 4 + j, j % 2, (2 * (j % 2), 2 * (j % 2) + 1))

            chunk(n0, 0, (0,), 8 * (LN_FFN[0] + 1))
            chunk(n0 + 1, 1, (2,))
            pe.wait_ge(gla_evac, 1)
            pe.wait_ge(gate_w_loaded, 16)
            gate(0)
            chunk(n0 + 2, 0, (0, 1))
            gate(1)
            pe.wait_ge(gla_evac, 2)
            chunk(n0 + 3, 1, (2,))
            gate(2)
            scores(0, 0)
            qkv_chunk(0)
            pe.wait_ge(gate_chain, 10)
            qkv_chunk(1)
            pe.wait_ge(p_exp, 4)
            gate(3)
            transposes(0, 0)
            qkv_chunk(2)
            outputs(0, 0)
            pe.wait_ge(gate_chain, 13)
            scores(0, 1)
            qkv_chunk(3)
            transposes(0, 1)
            qkv_chunk(4)
            outputs(0, 1)
            scores(0, 2)
            qkv_chunk(5)
            transposes(0, 2)
            qkv_chunk(6)
            outputs(0, 2)
            scores(0, 3)
            qkv_chunk(7)
            transposes(0, 3)
            pe.wait_ge(p_exp, 16)
            for e in range(8):
                pe.wait_ge(gla_evac, 5 + 8 + e + 1 if e < 2 else max(5 + 8 + e + 1, 19))
                if 4 <= e < 6:
                    pe.wait_ge(v_evac, e - 3)
                if e == 6:
                    outputs(0, 3)
                if e == 7:
                    pe.wait_ge(mo_done, 4)
                for b in range(TB):
                    last = nc.tensor.transpose(bank[V_BANK[e]][:, b * P:(b + 1) * P], qkv[:, 8 + e, b * P:(b + 1) * P], ident[:, :])
                last.then_inc(vt_mm, 1)

            def keys_and_att(h):
                pe.wait_ge(prods, 4 * h + 4)
                if h:
                    pe.wait_ge(kdt_evac, h)
                for b in range(TB):
                    last = nc.tensor.transpose(bank[4][:, b * P:(b + 1) * P], qkv[:, 4 + h, b * P:(b + 1) * P], ident[:, :])
                last.then_inc(kdt_mm, 1)
                if h:
                    pe.wait_ge(att_evac, h)
                for b in range(TB):
                    tok = slice(b * P, (b + 1) * P)
                    last = nc.tensor.matmul(bank[5][:, tok], ke[:, h, tok], qkv[:, h, tok], start=True, stop=True)
                last.then_inc(att_mm, 1)

            def state_sums(h, chunks):
                if h or chunks[0]:
                    pe.wait_ge(state_done, 7 * h + chunks[0])
                for c in chunks:
                    rows = slice(64 * (c % 2), 64 * (c % 2) + 64)
                    last = nc.tensor.matmul(bank[6 + c % 2][:, (c // 2 % 2) * 256:(c // 2 % 2) * 256 + 256],
                                            bk[rows, h, (c // 2) * P:(c // 2 + 1) * P],
                                            v_tok[rows, c // 2, h * 256:(h + 1) * 256], start=True, stop=True)
                last.then_inc(ds_mm, 1)

            pe.wait_ge(v_evac, 8)
            keys_and_att(0)
            for h in range(HEADS):
                pe.wait_ge(kdt_evac, h + 1)
                state_sums(h, range(4))
                if h + 1 < HEADS:
                    keys_and_att(h + 1)
                state_sums(h, range(4, 7))
                pe.wait_ge(att_evac, h + 1)
                for e in range(2):
                    to = bank[2 * (h % 2) + e]
                    if h >= 2:
                        pe.wait_ge(o_read, 4 * (h - 2) + 2 * e + 2)
                    cols = slice(h * 256 + e * P, h * 256 + (e + 1) * P)
                    for b in range(TB):
                        nc.tensor.matmul(to[:, b * P:(b + 1) * P], v_tok[:, b, cols], att[h % 2][:, b, :],
                                         start=(b == 0), stop=False, skip_group_check=True)
                    for c in range(1, NCH):
                        if e == 0:
                            pe.wait_ge(state_done, 7 * h + c)
                        tok = slice(c * CHUNK, (c + 1) * CHUNK)
                        last = nc.tensor.matmul(to[:, tok], states[:, h % 2, c - 1, e * P:(e + 1) * P], qkv[:, h, tok],
                                                start=False, stop=(c == NCH - 1), skip_group_check=True)
                    last.then_inc(o_mm, 1)
            for j in range(4):
                if j < 2:
                    pe.wait_ge(o_read, (12, 16)[j])
                else:
                    pe.wait_ge(gla_evac, 21 + 2 * (j - 1))
                chunk(n0 + 12 + j, j % 2, (2 * (j % 2), 2 * (j % 2) + 1))
                if j == 0:
                    for h in range(HEADS):
                        pe.wait_ge(ss_done, h + 1)
                        for b in range(TB):
                            last = nc.tensor.matmul(bank[4][:, TB * h + b:TB * h + b + 1], ke[:, h, b * P:(b + 1) * P],
                                                    ones[:, 0:1], start=True, stop=True)
                    last.then_inc(rms_mm, 1)
                if j == 1:
                    for h in range(HEADS):
                        pe.wait_ge(rms_diag, h + 1)
                        nc.tensor.matmul(bank[4 + h][:, :], ones[:, :], ke[:, h, :], start=True, stop=True).then_inc(rms_bcast, 1)
            for q in range(2):
                for p in (2 * q, 2 * q + 1):
                    if q == 0:
                        pe.wait_ge(gla_evac, 27 + 2 * p)
                    out_a(LN_GLA_OUT, GLA_OUT_N, p, 0, mo_hi_g, mo_lo_g)
                for p in (2 * q, 2 * q + 1):
                    out_b(LN_GLA_OUT, GLA_OUT_N, p, y_hi, y_lo, None)
                    if p == 0:
                        shift_sum(LN_GLA_OUT)
            stats(LN_GLA_OUT, FFN_N[1])
            ffn(1)
            ffn(2)

            n0 = CONV_N

            def diag_chunk(g):
                pe.wait_ge(lo_ready, DIAG_N + g + 1)
                if g == 0:
                    pe.wait_ge(cin_done, 2)
                    pe.wait_ge(conv_evac, 20)
                for j in range(TAPS_K[g]):
                    tap = 8 * g + j
                    for t in range(2):
                        last = mm3(bank[2 + t][:, :], g % 2, j, t, cin_hi[:, t, tap:tap + SEQ], cin_lo[:, t, tap:tap + SEQ],
                                   tap == 0, tap == WIDTH - 1)
                last.then_inc(w_used, 1)

            def conv_chunk(j, read=None):
                if read is not None:
                    pe.wait_ge(conv_evac, read)
                chunk(n0 + j, j % 2, (2 * (j % 2), 2 * (j % 2) + 1), 8 * (LN_FFN[2] + 1) if j == 0 else None)

            for j in range(6):
                conv_chunk(j, 2 * (j - 1) if j >= 2 else None)
            pe.wait_ge(conv_evac, 9)
            scores(1, 0)
            pe.wait_ge(conv_evac, 10)
            conv_chunk(6)
            transposes(1, 0)
            pe.wait_ge(p_exp, 20)
            shift_sum(LN_CONV)
            pe.wait_ge(conv_evac, 12)
            conv_chunk(7)
            outputs(1, 0)
            pe.wait_ge(shift_ready, LN_CONV + 1)
            scores(1, 1)
            conv_chunk(8, 14)
            transposes(1, 1)
            conv_chunk(9, 16)
            outputs(1, 1)
            scores(1, 2)
            diag_chunk(0)
            transposes(1, 2)
            diag_chunk(1)
            outputs(1, 2)
            scores(1, 3)
            diag_chunk(2)
            transposes(1, 3)
            diag_chunk(3)
            outputs(1, 3)
            out_a(LN_CONV_OUT, CONV_OUT_N, 0, 1, mo_hi_c, mo_lo_c)
            pe.wait_ge(conv_evac, 22)
            out_a(LN_CONV_OUT, CONV_OUT_N, 1, 1, mo_hi_c, mo_lo_c)
            sums_u(LN_CONV)
            stats(LN_CONV, CONV_OUT_N + 2)
            for q in range(2):
                if q:
                    for p in (2, 3):
                        out_a(LN_CONV_OUT, CONV_OUT_N, p, 1, mo_hi_c, mo_lo_c)
                for p in (2 * q, 2 * q + 1):
                    out_b(LN_CONV_OUT, CONV_OUT_N, p, c_hi, c_lo, 8 * (LN_CONV + 1))
                    if p == 0:
                        shift_sum(LN_CONV_OUT)
            stats(LN_CONV_OUT, FFN_N[3])
            ffn(3)
            for k in range(DK):
                pe.wait_ge(affine_done, 8 * LN_FFN[3] + k + 1)
                if k >= 4:
                    pe.wait_ge(fin_evac, k - 3)
                for b in range(TB):
                    last = nc.tensor.transpose(bank[k % 4][:, b * P:(b + 1) * P], u[:, k, b * P:(b + 1) * P], ident[:, :])
                last.then_inc(fin_mm, 1)


_INS = ["x", "mem", "ln_g", "ln_b", "ffn1_w_gu", "ffn1_w_down", "ffn2_w_gu", "ffn2_w_down", "mem_w_kv",
        "gla_w_in", "gla_w_gate2", "gla_b_gate", "gla_g_onorm", "gla_w_out",
        "conv_w_in", "conv_w_dw", "conv_b_dw", "conv_ln_g", "conv_ln_b", "conv_w_out"]


def kernel(**inputs):
    import numpy as _np
    import concourse.bacc as _bacc
    from concourse import mybir as _mybir
    from concourse.bass_utils import run_bass_kernel_spmd as _run

    nc = _bacc.Bacc("TRN2", target_bir_lowering=False, num_devices=1)
    arrays, aps = {}, {}
    for name in _INS:
        x = _np.ascontiguousarray(inputs[name])
        arrays[f"in_{name}_dram"] = x
        aps[name] = nc.dram_tensor(f"in_{name}_dram", x.shape, _mybir.dt.from_np(x.dtype), kind="ExternalInput").ap()
    out = nc.dram_tensor("out_0_dram", (1, SEQ, D), _mybir.dt.float32, kind="ExternalOutput").ap()
    build(nc, aps, out)
    r = _run(nc, [arrays], core_ids=[0])
    return r.results[0]["out_0_dram"]
```
